# Optimizing a Trainium2 kernel written in Bass

```python
import jax, jax.numpy as jnp
from jax import lax
import numpy as np

D_MODEL = 1024
BATCH = 1
SEQ = 256
DEPTH = 2

CTX_LEN = 256
GRID_W = 64
HEAD_DIM = 64
N_Q_HEADS = 4
N_KV_HEADS = 2
Q_PER_KV = N_Q_HEADS // N_KV_HEADS
Q_W = N_Q_HEADS * HEAD_DIM
KV_W = N_KV_HEADS * HEAD_DIM
FOURIER_GROUPS = 4
FOURIER_GROUP_W = 64
F_W = FOURIER_GROUPS * FOURIER_GROUP_W
N_BRANCH = 4
BRANCH_W = 256
IN_W = 3 * (Q_W + 2 * KV_W) + F_W + N_BRANCH * D_MODEL
Q_BLOCK = 128
WINDOW = 128
NA_KH_MAX = 8
NA_KW = 16
ROPE_THETA = 10000.0
N_EXPERTS = 16
EXPERT_FF = 1024
EC_CAPACITY = 2
N_MOD = 6
DN_ALPHA = (2 * DEPTH) ** 0.25
DN_BETA = (8 * DEPTH) ** -0.25
LN_EPS = 1e-6
RMS_EPS = 1e-6
NEG_INF = -1e30


def layer_norm(h, g, b):
    hf = h.astype(jnp.float32)
    mu = jnp.mean(hf, -1, keepdims=True)
    var = jnp.mean(jnp.square(hf - mu), -1, keepdims=True)
    return ((hf - mu) * lax.rsqrt(var + LN_EPS)).astype(h.dtype) * g + b

def rms_norm(h, g):
    hf = h.astype(jnp.float32)
    return (hf * lax.rsqrt(jnp.mean(hf * hf, -1, keepdims=True) + RMS_EPS)).astype(h.dtype) * g

def heads(t, n):
    return t.reshape(t.shape[:-1] + (n, HEAD_DIM))

def group_q(q):
    return q.reshape(q.shape[:-2] + (N_KV_HEADS, Q_PER_KV, HEAD_DIM))

def flat_heads(o):
    return o.reshape(o.shape[:2] + (Q_W,))

def split_columns(p):
    widths = (Q_W, KV_W, KV_W, F_W, Q_W, KV_W, KV_W, Q_W, KV_W, KV_W)
    offs, o = [], 0
    for w in widths:
        o += w
        offs.append(o)
    return jnp.split(p, offs, axis=-1)

def axial_rope_tables(n_tokens, dtype):
    t = jnp.arange(n_tokens)
    axis_dim = HEAD_DIM // 2
    inv = ROPE_THETA ** (-jnp.arange(0, axis_dim, 2, dtype=jnp.float32) / axis_dim)
    out = []
    for pos in (t // GRID_W, t % GRID_W):
        ang = pos.astype(jnp.float32)[:, None, None] * inv
        out.append(jnp.cos(ang).astype(dtype))
        out.append(jnp.sin(ang).astype(dtype))
    return tuple(out)

def rotate(t, cos, sin):
    h = t.shape[-1] // 2
    t1, t2 = t[..., :h], t[..., h:]
    return jnp.concatenate([t1 * cos - t2 * sin, t1 * sin + t2 * cos], -1)

def axial_rope(t, rope):
    cos_r, sin_r, cos_c, sin_c = rope
    half = HEAD_DIM // 2
    return jnp.concatenate([rotate(t[..., :half], cos_r, sin_r),
                            rotate(t[..., half:], cos_c, sin_c)], -1)

def neighbourhood_tables(n_tokens):
    rows = n_tokens // GRID_W
    kh = min(NA_KH_MAX, rows)
    t = jnp.arange(n_tokens)
    r, col = t // GRID_W, t % GRID_W
    r0 = jnp.clip(r - kh // 2, 0, rows - kh)
    c0 = jnp.clip(col - NA_KW // 2, 0, GRID_W - NA_KW)
    kr = r0[:, None, None] + jnp.arange(kh)[None, :, None]
    kc = c0[:, None, None] + jnp.arange(NA_KW)[None, None, :]
    shape = (n_tokens, kh, NA_KW)
    idx = jnp.broadcast_to(kr * GRID_W + kc, shape).reshape(n_tokens, -1)
    off_r = jnp.broadcast_to(kr - r[:, None, None] + NA_KH_MAX - 1, shape).reshape(n_tokens, -1)
    off_c = jnp.broadcast_to(kc - col[:, None, None] + NA_KW - 1, shape).reshape(n_tokens, -1)
    return idx, off_r, off_c

def gqa_softmax(q, k, v, bias=None, sink=None):
    s = jnp.einsum("bqhgd,bkhd->bhgqk", q, k).astype(jnp.float32) * HEAD_DIM ** -0.5
    if bias is not None:
        s = s + bias
    if sink is not None:
        sk = jnp.broadcast_to(sink.astype(jnp.float32)[None, :, :, None, None], s.shape[:-1] + (1,))
        p = jax.nn.softmax(jnp.concatenate([s, sk], -1), axis=-1)[..., :-1]
    else:
        p = jax.nn.softmax(s, axis=-1)
    return jnp.einsum("bhgqk,bkhd->bqhgd", p.astype(v.dtype), v)

def to_blocks(q):
    B, S = q.shape[:2]
    return jnp.swapaxes(q.reshape((B, S // Q_BLOCK, Q_BLOCK) + q.shape[2:]), 0, 1)

def from_blocks(ob, like):
    return flat_heads(jnp.swapaxes(ob, 0, 1).reshape(like.shape))

def global_attention(q, k_all, v_all):
    ob = lax.map(lambda qq: gqa_softmax(qq, k_all, v_all), to_blocks(q))
    return from_blocks(ob, q)

def window_attention(q, k_lat, v_lat, k_ctx, v_ctx, sink):
    S = q.shape[1]
    nblk = S // Q_BLOCK
    span = Q_BLOCK + 2 * WINDOW
    pad = ((0, 0), (WINDOW, WINDOW), (0, 0), (0, 0))
    k_pad, v_pad = jnp.pad(k_lat, pad), jnp.pad(v_lat, pad)
    ctx_bias = jnp.zeros((Q_BLOCK, k_ctx.shape[1]), jnp.float32)

    def one_block(args):
        qq, blk = args
        start = blk * Q_BLOCK
        kk = lax.dynamic_slice_in_dim(k_pad, start, span, axis=1)
        vv = lax.dynamic_slice_in_dim(v_pad, start, span, axis=1)
        q_pos = start + jnp.arange(Q_BLOCK)
        k_pos = start - WINDOW + jnp.arange(span)
        ok = (jnp.abs(q_pos[:, None] - k_pos[None, :]) <= WINDOW) & (k_pos >= 0) & (k_pos < S)
        bias = jnp.concatenate([ctx_bias, jnp.where(ok, 0.0, NEG_INF)], -1)
        return gqa_softmax(qq, jnp.concatenate([k_ctx, kk], 1), jnp.concatenate([v_ctx, vv], 1), bias, sink)

    ob = lax.map(one_block, (to_blocks(q), jnp.arange(nblk)))
    return from_blocks(ob, q)

def neighbourhood_attention(q, k_lat, v_lat, k_ctx, v_ctx, rpb, na_tab):
    idx, off_r, off_c = na_tab
    S = q.shape[1]
    nblk = S // Q_BLOCK
    n_nb = idx.shape[1]
    n_ctx = k_ctx.shape[1]
    scale = HEAD_DIM ** -0.5
    rpb_g = rpb.reshape((N_KV_HEADS, Q_PER_KV) + rpb.shape[1:]).astype(jnp.float32)
    bias = rpb_g[:, :, off_r, off_c]
    bias_b = jnp.moveaxis(bias.reshape(N_KV_HEADS, Q_PER_KV, nblk, Q_BLOCK, n_nb), 2, 0)
    idx_b = idx.reshape(nblk, Q_BLOCK, n_nb)

    def one_block(args):
        qq, ib, bb = args
        kk, vv = k_lat[:, ib], v_lat[:, ib]
        s_ctx = jnp.einsum("bqhgd,bchd->bhgqc", qq, k_ctx).astype(jnp.float32) * scale
        s_nb = jnp.einsum("bqhgd,bqkhd->bhgqk", qq, kk).astype(jnp.float32) * scale + bb
        p = jax.nn.softmax(jnp.concatenate([s_ctx, s_nb], -1), axis=-1).astype(v_lat.dtype)
        return (jnp.einsum("bhgqc,bchd->bqhgd", p[..., :n_ctx], v_ctx)
                + jnp.einsum("bhgqk,bqkhd->bqhgd", p[..., n_ctx:], vv))

    ob = lax.map(one_block, (to_blocks(q), idx_b, bias_b))
    return from_blocks(ob, q)

def fourier_mix(u):
    g = u.reshape(u.shape[:-1] + (FOURIER_GROUPS, FOURIER_GROUP_W)).astype(jnp.float32)
    f = jnp.fft.fft2(g, axes=(-3, -1), norm="ortho").real
    return f.reshape(u.shape).astype(u.dtype)

def merge_branches(branches, gate_logits, w_branch, w_out):
    gates = jax.nn.sigmoid(gate_logits)
    merged = gates[..., :D_MODEL] * (branches[0] @ w_branch[0])
    for i in range(1, N_BRANCH):
        merged = merged + gates[..., i * D_MODEL:(i + 1) * D_MODEL] * (branches[i] @ w_branch[i])
    return merged @ w_out

def token_mixers(u_lat, u_ctx, w_in, qk_gain, sink_logit, na_rpb, w_branch, w_out, rope, na_tab, with_ctx):
    pl = split_columns(u_lat @ w_in)
    pc = split_columns(u_ctx @ w_in)
    sink = sink_logit.reshape(N_KV_HEADS, Q_PER_KV)
    qa = group_q(axial_rope(rms_norm(heads(pl[0], N_Q_HEADS), qk_gain[0]), rope))
    ka = axial_rope(rms_norm(heads(pl[1], N_KV_HEADS), qk_gain[1]), rope)
    va = heads(pl[2], N_KV_HEADS)
    ka_c = rms_norm(heads(pc[1], N_KV_HEADS), qk_gain[1])
    va_c = heads(pc[2], N_KV_HEADS)
    br_a = global_attention(qa, jnp.concatenate([ka_c, ka], 1), jnp.concatenate([va_c, va], 1))
    br_b = fourier_mix(pl[3])
    qc = group_q(axial_rope(heads(pl[4], N_Q_HEADS), rope))
    kc = axial_rope(heads(pl[5], N_KV_HEADS), rope)
    vc = heads(pl[6], N_KV_HEADS)
    kc_c, vc_c = heads(pc[5], N_KV_HEADS), heads(pc[6], N_KV_HEADS)
    br_c = window_attention(qc, kc, vc, kc_c, vc_c, sink)
    qd = group_q(heads(pl[7], N_Q_HEADS))
    kd, vd = heads(pl[8], N_KV_HEADS), heads(pl[9], N_KV_HEADS)
    kd_c, vd_c = heads(pc[8], N_KV_HEADS), heads(pc[9], N_KV_HEADS)
    br_d = neighbourhood_attention(qd, kd, vd, kd_c, vd_c, na_rpb, na_tab)
    y_lat = merge_branches([br_a, br_b, br_c, br_d], pl[10], w_branch, w_out)
    if not with_ctx:
        return y_lat, None
    qa_c = group_q(rms_norm(heads(pc[0], N_Q_HEADS), qk_gain[0]))
    qc_c = group_q(heads(pc[4], N_Q_HEADS))
    qd_c = group_q(heads(pc[7], N_Q_HEADS))
    br_ctx = [flat_heads(gqa_softmax(qa_c, ka_c, va_c)),
              fourier_mix(pc[3]),
              flat_heads(gqa_softmax(qc_c, kc_c, vc_c, sink=sink)),
              flat_heads(gqa_softmax(qd_c, kd_c, vd_c))]
    y_ctx = merge_branches(br_ctx, pc[10], w_branch, w_out)
    return y_lat, y_ctx

def expert_choice_ffn(h, w_router, w_gate, w_up, w_down):
    B, n, D = h.shape
    cap = max(1, EC_CAPACITY * n // N_EXPERTS)
    aff = jax.nn.softmax(jnp.einsum("bnd,de->bne", h, w_router).astype(jnp.float32), axis=-1)
    sel_w, sel_idx = lax.top_k(jnp.swapaxes(aff, 1, 2), cap)
    xs = jax.vmap(lambda hb, ib: hb[ib])(h, sel_idx)
    a = jnp.einsum("becd,edf->becf", xs, w_gate)
    u = jnp.einsum("becd,edf->becf", xs, w_up)
    y = jnp.einsum("becf,efd->becd", jax.nn.silu(a) * u, w_down) * sel_w[..., None].astype(h.dtype)
    scatter = lambda yb, ib: jnp.zeros((n, D), h.dtype).at[ib.reshape(-1)].add(yb.reshape(-1, D))
    return jax.vmap(scatter)(y, sel_idx)

def trunk_layer(h_lat, h_ctx, c, c_ctx, w_mod, b_mod, w_in, qk_gain, sink_logit, na_rpb, w_branch,
                w_out, ln1_g, ln1_b, w_router, w_gate, w_up, w_down, ln2_g, ln2_b, rope, na_tab, with_ctx):
    m_lat = (jax.nn.silu(c) @ w_mod + b_mod)[:, None, :]
    m_ctx = jax.nn.silu(c_ctx) @ w_mod + b_mod
    sh1, sc1, g1, sh2, sc2, g2 = jnp.split(m_lat, N_MOD, -1)
    csh1, csc1, cg1, csh2, csc2, cg2 = jnp.split(m_ctx, N_MOD, -1)
    u_lat = h_lat * (1.0 + sc1) + sh1
    u_ctx = h_ctx * (1.0 + csc1) + csh1
    y_lat, y_ctx = token_mixers(u_lat, u_ctx, w_in, qk_gain, sink_logit, na_rpb, w_branch, w_out,
                                rope, na_tab, with_ctx)
    h_lat = layer_norm(DN_ALPHA * h_lat + g1 * y_lat, ln1_g, ln1_b)
    u_lat = h_lat * (1.0 + sc2) + sh2
    h_lat = layer_norm(DN_ALPHA * h_lat + g2 * expert_choice_ffn(u_lat, w_router, w_gate, w_up, w_down),
                       ln2_g, ln2_b)
    if with_ctx:
        h_ctx = layer_norm(DN_ALPHA * h_ctx + cg1 * y_ctx, ln1_g, ln1_b)
        u_ctx = h_ctx * (1.0 + csc2) + csh2
        h_ctx = layer_norm(DN_ALPHA * h_ctx + cg2 * expert_choice_ffn(u_ctx, w_router, w_gate, w_up, w_down),
                           ln2_g, ln2_b)
    return h_lat, h_ctx

def first_inputs(seed: int = 0) -> dict:
    key = jax.random.key(seed)
    ks = jax.random.split(key, 22)
    L, D, E, F = DEPTH, D_MODEL, N_EXPERTS, EXPERT_FF

    def nrm(k, shape, s):
        return jax.random.normal(k, shape, jnp.float32) * s

    return {
        "x": nrm(ks[0], (BATCH, SEQ, D), 1.0),
        "c": nrm(ks[1], (BATCH, D), 1.0),
        "ctx": nrm(ks[2], (BATCH, CTX_LEN, D), 1.0),
        "c_ctx": nrm(ks[3], (D,), 1.0),
        "w_mod": nrm(ks[4], (L, D, N_MOD * D), 0.5 * D ** -0.5),
        "b_mod": nrm(ks[5], (L, N_MOD * D), 0.02),
        "w_in": nrm(ks[6], (L, D, IN_W), D ** -0.5),
        "qk_gain": 1.0 + nrm(ks[7], (L, 2, HEAD_DIM), 0.1),
        "sink_logit": nrm(ks[8], (L, N_Q_HEADS), 0.5),
        "na_rpb": nrm(ks[9], (L, N_Q_HEADS, 2 * NA_KH_MAX - 1, 2 * NA_KW - 1), 0.5),
        "w_branch": nrm(ks[10], (L, N_BRANCH, BRANCH_W, D), DN_BETA * BRANCH_W ** -0.5),
        "w_out": nrm(ks[11], (L, D, D), DN_BETA * D ** -0.5),
        "ln1_g": 1.0 + nrm(ks[12], (L, D), 0.1),
        "ln1_b": nrm(ks[13], (L, D), 0.02),
        "w_router": nrm(ks[14], (L, D, E), D ** -0.5),
        "w_gate": nrm(ks[15], (L, E, D, F), D ** -0.5),
        "w_up": nrm(ks[16], (L, E, D, F), D ** -0.5),
        "w_down": nrm(ks[17], (L, E, F, D), DN_BETA * F ** -0.5),
        "ln2_g": 1.0 + nrm(ks[18], (L, D), 0.1),
        "ln2_b": nrm(ks[19], (L, D), 0.02),
    }

def first_block(x, c, ctx, c_ctx, w_mod, b_mod, w_in, qk_gain, sink_logit, na_rpb, w_branch, w_out,
              ln1_g, ln1_b, w_router, w_gate, w_up, w_down, ln2_g, ln2_b):
    n_tokens = x.shape[1]
    rope = axial_rope_tables(n_tokens, x.dtype)
    na_tab = neighbourhood_tables(n_tokens)
    h_lat, h_ctx = x, ctx
    for l in range(DEPTH):
        h_lat, h_ctx = trunk_layer(
            h_lat, h_ctx, c, c_ctx, w_mod[l], b_mod[l], w_in[l], qk_gain[l], sink_logit[l], na_rpb[l],
            w_branch[l], w_out[l], ln1_g[l], ln1_b[l], w_router[l], w_gate[l], w_up[l], w_down[l],
            ln2_g[l], ln2_b[l], rope, na_tab, l < DEPTH - 1)
    return h_lat


DEEPNORM_ALPHA = (2 * DEPTH) ** 0.25
DEEPNORM_BETA = (8 * DEPTH) ** -0.25
LN_EPS_2 = 1e-5

CONV_CH = D_MODEL
CONV_WIDTH = 31
SSM_INNER = D_MODEL
SSM_HEAD_DIM = 64
SSM_HEADS = SSM_INNER // SSM_HEAD_DIM
SSM_GROUPS = 2
SSM_HPG = SSM_HEADS // SSM_GROUPS
SSM_STATE = 128
SSM_CONV = 4
SSM_CHUNK = 128
SSM_XBC = SSM_INNER + 2 * SSM_GROUPS * SSM_STATE
EVEN_IN = 2 * CONV_CH + SSM_INNER + SSM_XBC + SSM_HEADS
EVEN_MIX = CONV_CH + SSM_INNER

GLA_HEADS = 4
GLA_DK_TOTAL = D_MODEL // 2
GLA_DV_TOTAL = D_MODEL
GLA_DK = GLA_DK_TOTAL // GLA_HEADS
GLA_DV = GLA_DV_TOTAL // GLA_HEADS
GLA_RANK = 16
GLA_TAU = 16.0
GLA_CHUNK = 64
ODD_IN = 2 * GLA_DK_TOTAL + 2 * GLA_DV_TOTAL + GLA_RANK

MEM_LEN = 256
XA_HEADS = 4
XA_HEAD_DIM = D_MODEL // XA_HEADS
D_FF = 4 * D_MODEL

N_EVEN = (DEPTH + 1) // 2
N_ODD = DEPTH // 2


def layer_norm_2(x, g, b):
    xf = x.astype(jnp.float32)
    mu = jnp.mean(xf, -1, keepdims=True)
    var = jnp.mean(jnp.square(xf - mu), -1, keepdims=True)
    return ((xf - mu) * lax.rsqrt(var + LN_EPS_2) * g + b).astype(x.dtype)

def rms_norm_2(x, g):
    xf = x.astype(jnp.float32)
    return (xf * lax.rsqrt(jnp.mean(xf * xf, -1, keepdims=True) + LN_EPS_2) * g).astype(x.dtype)

def causal_depthwise_conv(x, w, b):
    width = w.shape[0]
    y = lax.conv_general_dilated(x, w[:, None, :].astype(x.dtype), window_strides=(1,),
                                 padding=[(width - 1, 0)],
                                 dimension_numbers=('NWC', 'WIO', 'NWC'),
                                 feature_group_count=x.shape[-1])
    return y + b

def ssd_chunked(x, a, b_mat, c_mat):
    bsz, seqlen = x.shape[:2]
    nc, q = seqlen // SSM_CHUNK, SSM_CHUNK
    xc = x.reshape(bsz, nc, q, SSM_GROUPS, SSM_HPG, SSM_HEAD_DIM)
    ac = jnp.moveaxis(a.astype(jnp.float32).reshape(bsz, nc, q, SSM_GROUPS, SSM_HPG), 2, -1)
    bm = b_mat.reshape(bsz, nc, q, SSM_GROUPS, SSM_STATE)
    cm = c_mat.reshape(bsz, nc, q, SSM_GROUPS, SSM_STATE)
    a_cs = jnp.cumsum(ac, axis=-1)
    causal = jnp.tril(jnp.ones((q, q), dtype=bool))
    seg = a_cs[..., :, None] - a_cs[..., None, :]
    decay = jnp.exp(jnp.where(causal, seg, -jnp.inf)).astype(x.dtype)
    cb = jnp.einsum('bclgn,bcsgn->bcgls', cm, bm)
    y_diag = jnp.einsum('bcgkls,bcsgkp->bclgkp', cb[:, :, :, None] * decay, xc)
    decay_to_end = jnp.exp(a_cs[..., -1:] - a_cs).astype(x.dtype)
    states = jnp.einsum('bcsgn,bcgks,bcsgkp->bcgkpn', bm, decay_to_end, xc)
    chunk_decay = jnp.exp(a_cs[..., -1])

    def step(h, inp):
        st, dec = inp
        return h * dec[..., None, None] + st, h

    h0 = jnp.zeros((bsz, SSM_GROUPS, SSM_HPG, SSM_HEAD_DIM, SSM_STATE), jnp.float32)
    _, prev = lax.scan(step, h0, (jnp.moveaxis(states, 1, 0), jnp.moveaxis(chunk_decay, 1, 0)))
    prev = jnp.moveaxis(prev, 0, 1)
    y_off = jnp.einsum('bclgn,bcgkpn,bcgkl->bclgkp', cm, prev, jnp.exp(a_cs))
    return (y_diag + y_off).astype(x.dtype).reshape(bsz, seqlen, SSM_HEADS, SSM_HEAD_DIM)

def even_mixer(x, w_in, conv_w, conv_b, conv_ln_g, conv_ln_b, ssm_conv_w, ssm_conv_b,
               dt_bias, a_log, d_skip, ssm_norm_g, w_out):
    bsz, seqlen, _ = x.shape
    proj = x @ w_in
    c0 = CONV_CH
    c1 = 2 * CONV_CH
    c2 = c1 + SSM_INNER
    c3 = c2 + SSM_XBC
    conv_val, conv_gate, z, xbc, dt = jnp.split(proj, [c0, c1, c2, c3], axis=-1)
    u = conv_val * jax.nn.sigmoid(conv_gate)
    u = causal_depthwise_conv(u, conv_w, conv_b)
    u = jax.nn.silu(layer_norm_2(u, conv_ln_g, conv_ln_b))
    xbc = jax.nn.silu(causal_depthwise_conv(xbc, ssm_conv_w, ssm_conv_b))
    xs, bm, cm = jnp.split(xbc, [SSM_INNER, SSM_INNER + SSM_GROUPS * SSM_STATE], axis=-1)
    dt = jax.nn.softplus((dt + dt_bias).astype(jnp.float32))
    a = -jnp.exp(a_log.astype(jnp.float32))
    xs_h = xs.reshape(bsz, seqlen, SSM_HEADS, SSM_HEAD_DIM)
    y = ssd_chunked((xs_h * dt[..., None]).astype(x.dtype), dt * a,
                    bm.reshape(bsz, seqlen, SSM_GROUPS, SSM_STATE),
                    cm.reshape(bsz, seqlen, SSM_GROUPS, SSM_STATE))
    y = (y + xs_h * d_skip[:, None]).reshape(bsz, seqlen, SSM_INNER) * jax.nn.silu(z)
    y = rms_norm_2(y.reshape(bsz, seqlen, SSM_GROUPS, SSM_INNER // SSM_GROUPS),
                 ssm_norm_g.reshape(SSM_GROUPS, SSM_INNER // SSM_GROUPS)).reshape(bsz, seqlen, SSM_INNER)
    return jnp.concatenate([u, y.astype(u.dtype)], axis=-1) @ w_out

def gla_chunked(q, k, v, log_g):
    bsz, seqlen = q.shape[:2]
    n, c = seqlen // GLA_CHUNK, GLA_CHUNK
    q = q.reshape(bsz, n, c, GLA_HEADS, GLA_DK)
    k = k.reshape(bsz, n, c, GLA_HEADS, GLA_DK)
    v = v.reshape(bsz, n, c, GLA_HEADS, GLA_DV)
    b_cs = jnp.cumsum(log_g.astype(jnp.float32).reshape(bsz, n, c, GLA_HEADS, GLA_DK), axis=2)
    q_t = q * jnp.exp(b_cs) * (GLA_DK ** -0.5)
    k_t = k * jnp.exp(-b_cs)
    k_end = k * jnp.exp(b_cs[:, :, -1:] - b_cs)
    causal = jnp.tril(jnp.ones((c, c), dtype=bool))
    att = jnp.where(causal, jnp.einsum('bnlhd,bnshd->bnhls', q_t, k_t), 0.0)
    o = jnp.einsum('bnhls,bnshv->bnlhv', att, v)
    kv = jnp.einsum('bnshd,bnshv->bnhdv', k_end, v)
    chunk_decay = jnp.exp(b_cs[:, :, -1])

    def step(s, inp):
        kv_c, dec = inp
        return s * dec[..., None] + kv_c, s

    s0 = jnp.zeros((bsz, GLA_HEADS, GLA_DK, GLA_DV), jnp.float32)
    _, prev = lax.scan(step, s0, (jnp.moveaxis(kv, 1, 0), jnp.moveaxis(chunk_decay, 1, 0)))
    prev = jnp.moveaxis(prev, 0, 1)
    o = o + jnp.einsum('bnlhd,bnhdv->bnlhv', q_t, prev)
    return o.astype(v.dtype).reshape(bsz, seqlen, GLA_HEADS, GLA_DV)

def odd_mixer(x, w_in, w_gate2, b_gate, head_norm_g, w_out):
    bsz, seqlen, _ = x.shape
    proj = x @ w_in
    s0 = GLA_DK_TOTAL
    s1 = 2 * GLA_DK_TOTAL
    s2 = s1 + GLA_DV_TOTAL
    s3 = s2 + GLA_DV_TOTAL
    q, k, v, g_out, g_low = jnp.split(proj, [s0, s1, s2, s3], axis=-1)
    log_g = jax.nn.log_sigmoid((g_low @ w_gate2 + b_gate).astype(jnp.float32)) / GLA_TAU
    o = gla_chunked(q.reshape(bsz, seqlen, GLA_HEADS, GLA_DK),
                    k.reshape(bsz, seqlen, GLA_HEADS, GLA_DK),
                    v.reshape(bsz, seqlen, GLA_HEADS, GLA_DV),
                    log_g.reshape(bsz, seqlen, GLA_HEADS, GLA_DK))
    o = rms_norm_2(o, head_norm_g).reshape(bsz, seqlen, GLA_DV_TOTAL) * jax.nn.silu(g_out)
    return o @ w_out

def memory_cross_attention(x, mem, w_q, w_k, w_v, w_o):
    bsz, seqlen, _ = x.shape
    q = (x @ w_q).reshape(bsz, seqlen, XA_HEADS, XA_HEAD_DIM)
    k = (mem @ w_k).reshape(bsz, mem.shape[1], XA_HEADS, XA_HEAD_DIM)
    v = (mem @ w_v).reshape(bsz, mem.shape[1], XA_HEADS, XA_HEAD_DIM)
    s = jnp.einsum('blhd,bmhd->bhlm', q, k).astype(jnp.float32) * (XA_HEAD_DIM ** -0.5)
    p = jax.nn.softmax(s, axis=-1).astype(v.dtype)
    o = jnp.einsum('bhlm,bmhd->blhd', p, v).reshape(bsz, seqlen, D_MODEL)
    return o @ w_o

def sq_relu_mlp(x, w1, w2):
    return jnp.square(jax.nn.relu(x @ w1)) @ w2

def second_inputs(seed: int = 0) -> dict:
    key = jax.random.key(seed)
    ks = iter(jax.random.split(key, 40))
    f32 = jnp.float32

    def nrm(shape, scale):
        return jax.random.normal(next(ks), shape, f32) * scale

    dt0 = jnp.exp(jax.random.uniform(next(ks), (N_EVEN, SSM_HEADS), f32,
                                     np.log(1e-3).astype(np.float32), np.log(1e-1).astype(np.float32)))
    return {
        "x": nrm((BATCH, SEQ, D_MODEL), 1.0),
        "mem": nrm((BATCH, MEM_LEN, D_MODEL), 1.0),
        "even_w_in": nrm((N_EVEN, D_MODEL, EVEN_IN), D_MODEL ** -0.5),
        "even_conv_w": nrm((N_EVEN, CONV_WIDTH, CONV_CH), CONV_WIDTH ** -0.5),
        "even_conv_b": nrm((N_EVEN, CONV_CH), 0.01),
        "even_conv_ln_g": 1.0 + nrm((N_EVEN, CONV_CH), 0.02),
        "even_conv_ln_b": nrm((N_EVEN, CONV_CH), 0.02),
        "even_ssm_conv_w": nrm((N_EVEN, SSM_CONV, SSM_XBC), SSM_CONV ** -0.5),
        "even_ssm_conv_b": nrm((N_EVEN, SSM_XBC), 0.01),
        "even_dt_bias": dt0 + jnp.log(-jnp.expm1(-dt0)),
        "even_a_log": jnp.log(jax.random.uniform(next(ks), (N_EVEN, SSM_HEADS), f32, 1.0, 16.0)),
        "even_d_skip": 1.0 + nrm((N_EVEN, SSM_HEADS), 0.02),
        "even_ssm_norm_g": 1.0 + nrm((N_EVEN, SSM_INNER), 0.02),
        "even_w_out": nrm((N_EVEN, EVEN_MIX, D_MODEL), EVEN_MIX ** -0.5 * DEEPNORM_BETA),
        "odd_w_in": nrm((N_ODD, D_MODEL, ODD_IN), D_MODEL ** -0.5),
        "odd_w_gate2": nrm((N_ODD, GLA_RANK, GLA_DK_TOTAL), GLA_RANK ** -0.5),
        "odd_b_gate": nrm((N_ODD, GLA_DK_TOTAL), 0.1),
        "odd_head_norm_g": 1.0 + nrm((N_ODD, GLA_DV), 0.02),
        "odd_w_out": nrm((N_ODD, GLA_DV_TOTAL, D_MODEL), GLA_DV_TOTAL ** -0.5 * DEEPNORM_BETA),
        "xa_w_q": nrm((DEPTH, D_MODEL, D_MODEL), D_MODEL ** -0.5),
        "xa_w_k": nrm((DEPTH, D_MODEL, D_MODEL), D_MODEL ** -0.5),
        "xa_w_v": nrm((DEPTH, D_MODEL, D_MODEL), D_MODEL ** -0.5),
        "xa_w_o": nrm((DEPTH, D_MODEL, D_MODEL), D_MODEL ** -0.5 * DEEPNORM_BETA),
        "mlp_w1": nrm((DEPTH, D_MODEL, D_FF), D_MODEL ** -0.5),
        "mlp_w2": nrm((DEPTH, D_FF, D_MODEL), D_FF ** -0.5 * DEEPNORM_BETA),
        "ln_g": 1.0 + nrm((DEPTH, 3, D_MODEL), 0.02),
        "ln_b": nrm((DEPTH, 3, D_MODEL), 0.02),
    }

def second_block(x, mem, even_w_in, even_conv_w, even_conv_b, even_conv_ln_g, even_conv_ln_b,
              even_ssm_conv_w, even_ssm_conv_b, even_dt_bias, even_a_log, even_d_skip,
              even_ssm_norm_g, even_w_out, odd_w_in, odd_w_gate2, odd_b_gate, odd_head_norm_g,
              odd_w_out, xa_w_q, xa_w_k, xa_w_v, xa_w_o, mlp_w1, mlp_w2, ln_g, ln_b):
    h = x
    for i in range(DEPTH):
        j = i // 2
        if i % 2 == 0:
            m = even_mixer(h, even_w_in[j], even_conv_w[j], even_conv_b[j], even_conv_ln_g[j],
                           even_conv_ln_b[j], even_ssm_conv_w[j], even_ssm_conv_b[j],
                           even_dt_bias[j], even_a_log[j], even_d_skip[j], even_ssm_norm_g[j],
                           even_w_out[j])
        else:
            m = odd_mixer(h, odd_w_in[j], odd_w_gate2[j], odd_b_gate[j], odd_head_norm_g[j],
                          odd_w_out[j])
        h = layer_norm_2(DEEPNORM_ALPHA * h + m, ln_g[i, 0], ln_b[i, 0])
        h = layer_norm_2(DEEPNORM_ALPHA * h + memory_cross_attention(h, mem, xa_w_q[i], xa_w_k[i],
                                                                   xa_w_v[i], xa_w_o[i]),
                       ln_g[i, 1], ln_b[i, 1])
        h = layer_norm_2(DEEPNORM_ALPHA * h + sq_relu_mlp(h, mlp_w1[i], mlp_w2[i]),
                       ln_g[i, 2], ln_b[i, 2])
    return h


def setup_inputs(seed=0):
    out = dict(first_inputs(seed))
    for name, value in second_inputs(seed + 1).items():
        if name != "x":
            out[name + "_2"] = value
    return out


def reference(
    x, c, ctx, c_ctx, w_mod, b_mod, w_in, qk_gain, sink_logit, na_rpb, w_branch, w_out, ln1_g,
    ln1_b, w_router, w_gate, w_up, w_down, ln2_g, ln2_b, mem_2, even_w_in_2, even_conv_w_2,
    even_conv_b_2, even_conv_ln_g_2, even_conv_ln_b_2, even_ssm_conv_w_2, even_ssm_conv_b_2,
    even_dt_bias_2, even_a_log_2, even_d_skip_2, even_ssm_norm_g_2, even_w_out_2, odd_w_in_2,
    odd_w_gate2_2, odd_b_gate_2, odd_head_norm_g_2, odd_w_out_2, xa_w_q_2, xa_w_k_2, xa_w_v_2,
    xa_w_o_2, mlp_w1_2, mlp_w2_2, ln_g_2, ln_b_2,
):
    x = first_block(
        x, c, ctx, c_ctx, w_mod, b_mod, w_in, qk_gain, sink_logit, na_rpb, w_branch, w_out,
        ln1_g, ln1_b, w_router, w_gate, w_up, w_down, ln2_g, ln2_b,
    )
    return second_block(
        x, mem_2, even_w_in_2, even_conv_w_2, even_conv_b_2, even_conv_ln_g_2, even_conv_ln_b_2,
        even_ssm_conv_w_2, even_ssm_conv_b_2, even_dt_bias_2, even_a_log_2, even_d_skip_2,
        even_ssm_norm_g_2, even_w_out_2, odd_w_in_2, odd_w_gate2_2, odd_b_gate_2,
        odd_head_norm_g_2, odd_w_out_2, xa_w_q_2, xa_w_k_2, xa_w_v_2, xa_w_o_2, mlp_w1_2,
        mlp_w2_2, ln_g_2, ln_b_2,
    )


_drawn_inputs = setup_inputs


def setup_inputs(seed=0):
    import zlib

    import numpy as np

    out = dict(_drawn_inputs(seed))
    spreads = {}
    factors = {'ctx': 8.0,
     'c_ctx': 3.891,
     'b_mod': 8.0,
     'qk_gain': 8.0,
     'sink_logit': 64.0,
     'na_rpb': 8.0,
     'even_conv_b_2': 8.0,
     'even_conv_ln_g_2': 8.0,
     'even_conv_ln_b_2': 8.0,
     'even_ssm_conv_b_2': 8.0,
     'even_d_skip_2': 8.0,
     'even_ssm_norm_g_2': 8.0,
     'odd_b_gate_2': 5.736,
     'odd_head_norm_g_2': 25.251}
    for name, (base, spread) in spreads.items():
        noise = np.random.default_rng([zlib.crc32(name.encode()), seed]).standard_normal(out[name].shape)
        drawn = base * np.exp(spread * noise) if base else spread * noise
        out[name] = __import__('jax').numpy.asarray(drawn.astype(out[name].dtype))
    for name, factor in factors.items():
        out[name] = (out[name] * factor).astype(out[name].dtype)
    return out
```

```python
from contextlib import ExitStack

import numpy as np
import concourse.bass as bass
from concourse import mybir

F32 = mybir.dt.float32
U32 = mybir.dt.uint32
ALU = mybir.AluOpType
ACT = mybir.ActivationFunctionType
AX = mybir.AxisListType

P = 128
D = 1024
KT = D // P
S = 256
TB = S // P
UNIT = 2048
UC = UNIT // KT
RING = 8
DEPTH = 2
HD = 64
E = 16
CAP = 32
NEG = -1e30
ALPHA = float((2 * DEPTH) ** 0.25)
EPS1, EPS2 = 1e-6, 1e-5
CONV_W, SSM_W = 31, 4
SSM_HEADS = 16
GLA_CHUNK, GLA_TAU = 64, 16.0
MOD_UNITS = 6 * D // UC
EXPERT_UNITS = 12
GROUP = 4
GROUP_UNITS = GROUP * EXPERT_UNITS


def columns(widths):
    at, out = 0, {}
    for name, width in widths:
        out[name] = (at, width)
        at += width
    return out, at


VEC, NVEC = columns([
    ("c", 2 * KT), ("b_mod", DEPTH * 48), ("ln1_g", DEPTH * KT), ("ln1_b", DEPTH * KT),
    ("ln2_g", DEPTH * KT), ("ln2_b", DEPTH * KT), ("ln_g", DEPTH * 3 * KT), ("ln_b", DEPTH * 3 * KT),
    ("conv_b", KT), ("conv_ln_g", KT), ("conv_ln_b", KT), ("ssm_conv_b", 12), ("ssm_norm_g", KT),
    ("b_gate", 4), ("head_norm_g", 2), ("conv_w", KT * CONV_W), ("ssm_conv_w", 12 * SSM_W),
    ("qk_gain", DEPTH * 2), ("sink", DEPTH * 4), ("d_skip", KT), ("dt_bias", 1), ("a_log", 1),
    ("w_router", DEPTH * KT * E), ("w_dt", KT * SSM_HEADS), ("w_low", KT * 16), ("w_gate2", 512)])

CON, NCON = columns([
    ("ident", P), ("ones", P), ("headones", P), ("rot", P), ("rev", P), ("cos", S), ("sin", S),
    ("dft", 2 * P), ("seqcos", 2 * S), ("seqsin", 2 * S), ("window", TB * S), ("near", 64),
    ("causal", P), ("iota", CAP), ("chunked", P), ("carry", S)])


def constants():
    out = np.zeros((P, NCON), np.float32)

    def put(name, value):
        at, width = CON[name]
        out[:, at:at + width] = np.asarray(value, np.float64).reshape(P, width)

    p = np.arange(P)
    put("ident", np.eye(P))
    put("ones", np.ones((P, P)))
    put("headones", p[:, None] // HD == p[None] // HD)
    half, quarter = HD // 2, HD // 4
    rot = np.zeros((P, P))
    for m in range(P):
        if m % half < quarter:
            rot[m + quarter, m] = -1.0
        else:
            rot[m - quarter, m] = 1.0
    put("rot", rot)
    put("rev", np.eye(P)[::-1])
    inv = (10000.0 ** (-np.arange(0, half, 2, dtype=np.float32) / half)).astype(np.float32)
    t = np.arange(S)
    pos = np.where((p % HD < half)[:, None], (t // 64)[None], (t % 64)[None]).astype(np.float32)
    angle = (pos * inv[p % quarter][:, None]).astype(np.float32)
    put("cos", np.cos(angle))
    put("sin", np.sin(angle))
    same = (p[:, None] // 64 == p[None] // 64)
    wa = 2 * np.pi * np.outer(p % 64, p % 64) / 64
    put("dft", np.concatenate([np.cos(wa) * same, np.sin(wa) * same], 1))
    sa = 2 * np.pi * np.outer(t, t) / S
    fold = lambda m: m.reshape(TB, P, S).transpose(1, 0, 2)
    put("seqcos", fold(np.cos(sa) / 128.0))
    put("seqsin", fold(-np.sin(sa) / 128.0))
    put("window", fold(np.where(np.abs(t[:, None] - t[None]) <= 128, 0.0, NEG)))
    col = 63 - p % 64
    first = np.clip(col - 8, 0, 48)[:, None]
    kc = np.arange(64)[None]
    put("near", np.where((kc >= first) & (kc < first + 16), 0.0, NEG))
    put("causal", np.where(p[None] >= p[:, None], 0.0, NEG))
    put("iota", np.broadcast_to(np.arange(CAP), (P, CAP)))
    put("chunked", (p[None] >= p[:, None]) & (p[:, None] // GLA_CHUNK == p[None] // GLA_CHUNK))
    put("carry", np.broadcast_to(t % GLA_CHUNK != 0, (P, S)))
    return out


def units_of(w):
    k, n = w.shape
    return w.reshape(k // D, KT, P, n // UC, UC).transpose(3, 0, 2, 1, 4).reshape(-1, P, UNIT)


def weight_stream(i):
    parts = [units_of(i["w_mod"][l]) for l in range(DEPTH)]
    for l in range(DEPTH):
        w_in = units_of(i["w_in"][l])
        parts.append(w_in[:7])
        for b in range(4):
            parts.append(w_in[7 + 4 * b:11 + 4 * b])
            parts.append(i["w_branch"][l, b].reshape(1, 2, P, D).transpose(0, 2, 1, 3).reshape(1, P, UNIT))
        parts.append(units_of(i["w_out"][l]))
        for e in range(E):
            gate, up = units_of(i["w_gate"][l, e]), units_of(i["w_up"][l, e])
            for c in range(4):
                parts += [gate[c:c + 1], up[c:c + 1]]
            parts.append(units_of(i["w_down"][l, e]))
    even = units_of(i["even_w_in_2"][0][:, :4608])
    for c in range(4):
        parts += [even[c:c + 1], even[4 + c:5 + c]]
    parts += [even[12:], even[8:12], units_of(i["even_w_out_2"][0])]
    for l in range(DEPTH):
        if l == 1:
            odd = units_of(i["odd_w_in_2"][0][:, :3072])
            parts += [odd, units_of(i["odd_w_out_2"][0])]
        parts += [units_of(i[f"xa_w_{n}_2"][l]) for n in "kvqo"]
        parts += [units_of(i["mlp_w1_2"][l]), units_of(i["mlp_w2_2"][l])]
    return np.concatenate(parts, 0)


def vectors(i):
    out = np.zeros((P, NVEC), np.float32)

    def put(name, value):
        at, width = VEC[name]
        value = np.asarray(value).reshape(-1, width)
        out[:value.shape[0], at:at + width] = value

    tiles = lambda v: v.reshape(-1, P).T
    put("c", np.stack([i["c"][0], i["c_ctx"]]).reshape(2, KT, P).transpose(2, 1, 0))
    for name, key in (("b_mod", "b_mod"), ("ln1_g", "ln1_g"), ("ln1_b", "ln1_b"), ("ln2_g", "ln2_g"),
                      ("ln2_b", "ln2_b"), ("ln_g", "ln_g_2"), ("ln_b", "ln_b_2"), ("conv_b", "even_conv_b_2"),
                      ("conv_ln_g", "even_conv_ln_g_2"), ("conv_ln_b", "even_conv_ln_b_2"),
                      ("ssm_conv_b", "even_ssm_conv_b_2"), ("ssm_norm_g", "even_ssm_norm_g_2"),
                      ("b_gate", "odd_b_gate_2"), ("head_norm_g", "odd_head_norm_g_2")):
        put(name, tiles(i[key]))
    put("conv_w", i["even_conv_w_2"][0].reshape(CONV_W, KT, P).transpose(2, 1, 0))
    put("ssm_conv_w", i["even_ssm_conv_w_2"][0].reshape(SSM_W, 12, P).transpose(2, 1, 0))
    put("qk_gain", np.tile(i["qk_gain"].reshape(DEPTH * 2, HD).T, (2, 1)))
    put("sink", np.broadcast_to(i["sink_logit"].reshape(1, -1), (P, DEPTH * 4)))
    put("d_skip", np.repeat(i["even_d_skip_2"][0].reshape(KT, 2), HD, 1).T)
    put("dt_bias", i["even_dt_bias_2"][0].reshape(-1, 1))
    put("a_log", i["even_a_log_2"][0].reshape(-1, 1))
    put("w_router", i["w_router"].reshape(DEPTH, KT, P, E).transpose(2, 0, 1, 3))
    put("w_dt", i["even_w_in_2"][0][:, 4608:].reshape(KT, P, SSM_HEADS).transpose(1, 0, 2))
    put("w_low", i["odd_w_in_2"][0][:, 3072:].reshape(KT, P, 16).transpose(1, 0, 2))
    put("w_gate2", i["odd_w_gate2_2"][0])
    return out


def neighbour_rows(rpb):
    out = np.zeros(rpb.shape[:2] + (7, P), np.float32)
    out[..., 48:79] = rpb[:, :, 4:11]
    return out


def feature_major(x):
    return x.reshape(-1, KT, P).transpose(2, 1, 0)


class Count:

    def __init__(self, engine):
        self.engine, self.n, self.turn, self.per = engine, {}, None, {}

    def at(self, sem, more=1, less=0):
        self.skip(sem, more)
        value = self.n[sem.name] - less
        assert value > 0, sem.name
        per = self.per.get(sem.name, 0)
        return value if self.turn is None or not per else self.turn * per + value

    def skip(self, sem, more):
        self.n[sem.name] = self.n.get(sem.name, 0) + more

    def loop(self, times, per):
        return _Loop(self, times, per)


class _Loop:
    def __init__(self, count, times, per):
        self.count, self.times, self.per = count, times, {s.name: k for s, k in per}

    def __enter__(self):
        c = self.count
        self.fori = c.engine.Fori(0, self.times)
        self.start = dict(c.n)
        c.turn, c.per = self.fori.__enter__(), self.per
        return c.turn

    def __exit__(self, *what):
        done = self.fori.__exit__(*what)
        c = self.count
        for name, value in c.n.items():
            rise = value - self.start.get(name, 0)
            assert rise == self.per.get(name, 0), (name, rise)
            c.n[name] = self.start.get(name, 0) + rise * self.times
        c.turn, c.per = None, {}
        return done


def build(nc, ap, out):
    units = ap["units"]
    n_units = units.shape[0]
    with ExitStack() as ctx:
        def sb(name, *shape):
            return ctx.enter_context(nc.sbuf_tensor(name, [P, *shape], F32))

        def sem(name):
            return ctx.enter_context(nc.semaphore(name))

        ring = sb("ring", RING, UNIT)
        vec = sb("vec", NVEC)
        con = sb("con", NCON)
        h = sb("h", KT, 2 * S)
        u = sb("u", KT, 2 * S)
        mod = sb("mod", DEPTH * 48, 2)
        cs = sb("cs", KT, 2)
        small = sb("small", 1216)
        arena = sb("arena", 21504)
        ps = ctx.enter_context(nc.psum_tensor("ps", [P, 8, 512], F32))

        def uflat(x):
            return x[:, :, :].rearrange("p k n -> p (k n)")

        def V(name):
            at, width = VEC[name]
            return vec[:, at:at + width]

        def C(name, rows=P):
            at, width = CON[name]
            return con[0:rows, at:at + width]

        def part(at, *shape, of=arena, rows=P):
            n = int(np.prod(shape))
            v = of[0:rows, at:at + n]
            if len(shape) == 2:
                v = v.rearrange("p (a b) -> p a b", b=shape[1])
            if len(shape) == 3:
                v = v.rearrange("p (a b c) -> p a b c", b=shape[1], c=shape[2])
            if len(shape) == 4:
                v = v.rearrange("p (a b c d) -> p a b c d", b=shape[1], c=shape[2], d=shape[3])
            return v

        ident, ones = C("ident"), C("ones")

        qk = part(0, 12, 512)
        val = part(6144, 4, 384)
        four = part(7680, 2, 512)
        prob = [part(8704, 4, 512), part(10752, 4, 512)]
        probT = part(12800, 4, 512)
        bias = part(14848, 8, S)
        branch = part(16896, 8, 512)
        fmid = part(12800, 2, 2 * S)
        nsq = part(8704, 4, 512)
        rtmp = part(10752, 8, S)
        merged = part(0, KT, 512)
        gate = part(4096, KT, 512)
        gated = [part(12800, 2, 512), part(13824, 2, 512)]
        sq1 = part(8704, KT, 512)
        xs = part(0, KT, E, 64)
        wsel = part(8192, 4, 512)
        acc = part(10240, KT, 512)
        y4 = part(14336, 2, D)
        htok = part(14336, 4, D)
        hid = part(18432, KT, 64)
        xcur = part(18944, KT, 64)
        eneg = part(19456, 2, 128)
        pick = part(10240, 4, 512)
        wpick = part(12288, 4, 512)
        logit = part(19712, 4, E)
        aff = part(19776, TB, 2, E)
        rowa, rowb, rowc = part(19840, S), part(20096, S), part(20352, S)
        rank = part(20608, TB, 2, E)
        top8 = part(20672, 4, 8)
        onesrow = part(20704, S)
        sq2 = part(0, KT, 512)

        cpad = part(0, KT, CONV_W - 1 + S)
        conv = part(2288, KT, S)
        zed = part(4336, KT, S)
        xpad = part(6384, 12, SSM_W - 1 + S)
        xneg = part(6384, 12, S)
        egate = part(19476, 2, S)
        xbc = part(9492, 12, S)
        mixin = part(12564, 2 * KT, S)
        xdt = part(16660, TB, D)
        cb = part(18708, 2, 384)
        decay = [part(19476, 384), part(19860, 384)]
        mask = [part(20244, 384), part(20628, 384)]
        sel = part(0, SSM_HEADS, P, rows=16)
        dtv, acs = small[0:16, 768:1024], small[0:16, 256:512]
        dts, dtc = small[0:16, 512:768], small[0:16, 0:256]
        dtT, acsT = small[:, 1056:1088], small[:, 1088:1120]
        nega = small[0:16, 1120:1121]
        t1, t2 = part(0, KT, S, of=uflat(u)), part(KT * S, KT, S, of=uflat(u))
        mem = h[:, :, S:]
        xk, xq = part(0, KT, S), part(2048, KT, S)
        xv = part(4096, TB, D)
        xp = part(6144, 4, S)
        xpT = part(7168, 8, P)
        xo = part(8192, KT, S)
        relu2 = part(0, 4 * KT, S)
        gq, gk = part(0, 4, S), part(1024, 4, S)
        gv = part(2048, TB, D)
        gout = part(4096, KT, S)
        logg, eb, en = part(6144, 4, S), part(7168, 4, S), part(8192, 4, S)
        qt, ktl, kend = part(9216, 4, S), part(10240, 4, S), part(11264, 4, S)
        kendT = part(12288, TB * 4, P)
        att = part(13312, TB * 4, P)
        hist = part(14336, 4, 3 * S)
        go = part(17408, KT, S)
        low = part(19456, S, rows=16)
        gmid = part(19712, 4, S)
        gend = part(20736, 4, 4)

        stat = small[:, 0:512]
        stat2 = small[:, 512:1024]
        tick = small[:, 1160:1161]
        es, nsink = small[:, 1140:1148], small[:, 1148:1156]
        mx, sums, rec = small[:, 1024:1032], small[:, 1032:1040], small[:, 1040:1048]

        inputs_loaded = sem("inputs_loaded")
        bias_loaded = sem("bias_loaded")
        memory_loaded = sem("memory_loaded")
        loaded = [sem(f"unit_loaded_{s}") for s in range(RING)]
        units_used = sem("units_used")
        products_taken = sem("products_taken")
        dve_step, act_step = sem("dve_step"), sem("act_step")
        pe_step = sem("pe_step")
        dve_to_pe = sem("operands_ready")
        dve_to_act = sem("arguments_ready")
        act_to_dve = sem("functions_ready")
        act_to_pe = sem("act_operands_ready")
        pe_to_dve = sem("sums_ready")
        pe_to_act = sem("blocks_ready")
        normed = sem("normed")
        variances_ready = sem("variances_ready")
        inverses_ready = sem("inverses_ready")
        decay_ready = sem("decay_ready")
        head_done = sem("head_done")
        y_tile_kept = sem("y_tile_kept")
        squares_kept = sem("squares_kept")
        scores_ready = sem("scores_ready")
        exps_ready = sem("exps_ready")
        probs_ready = sem("probs_ready")
        turned = sem("probs_turned")
        turned_kept = sem("turned_kept")
        mixed = sem("values_mixed")
        mixed_kept = sem("mixed_kept")
        hidden_ready = sem("hidden_ready")
        y_kept = sem("outputs_kept")
        scattered = sem("scattered")
        added = sem("scattered_added")
        xcur_ready = sem("expert_input_ready")
        stored = sem("stored")

        block = ctx.enter_context(nc.Block())

        @block.sync
        def _(sp):
            sp.dma_start(vec[:, :], ap["vectors"]).then_inc(inputs_loaded, 16)
            sp.dma_start(con[:, :], ap["constants"]).then_inc(inputs_loaded, 16)
            for s in range(RING):
                sp.dma_start(ring[:, s, :], units[s]).then_inc(loaded[s], 16)
                if s == 3:
                    sp.dma_start(h[:, :, :], ap["tokens"]).then_inc(inputs_loaded, 16)
            turns = n_units // RING - 1
            assert n_units % RING == 0
            with sp.Fori(0, turns) as i:
                for s in range(RING):
                    sp.wait_ge(units_used, i * RING + s + 1)
                    sp.dma_start(ring[:, s, :], units[bass.ds(i * RING + RING + s, 1)]
                                 .rearrange("a p n -> (a p) n")).then_inc(loaded[s], 16)
            sp.wait_ge(normed, 2 * DEPTH + 3 * DEPTH)
            sp.dma_start(out, h[:, :, 0:S]).then_inc(stored, 16)
            sp.wait_ge(stored, 16)

        @block.gpsimd
        def _(pool):
            for l in range(DEPTH):
                if l:
                    pool.wait_ge(normed, 2)
                for hd in range(4):
                    for b in range(TB):
                        for r in range(2):
                            at = ap["neighbours"][l, hd, 2 - 2 * b + r, 0:1]
                            src = bass.AP(at.tensor, at.offset, [[1, 64], [P, 4], [1, 64]])
                            pool.dma_start(bias[64 * r:64 * (r + 1), hd * TB + b, :]
                                           .rearrange("p (r c) -> p r c", c=64), src).then_inc(bias_loaded, 16)
            pool.wait_ge(normed, 4)
            pool.dma_start(h[:, :, S:], ap["memory"]).then_inc(memory_loaded, 16)

        @block.tensor
        def _(pe):
            count = Count(pe)
            at = count.at
            state = {"unit": 0, "product": 0}

            def unit():
                n = state["unit"]
                pe_wait_unit(n)
                state["unit"] += 1
                return ring[:, n % RING, :].rearrange("p (k c) -> p k c", c=UC)

            def pe_wait_unit(n):
                value = 16 * (n // RING + 1)
                if count.turn is None:
                    pe.wait_ge(loaded[n % RING], value)
                else:
                    pe.wait_ge(loaded[n % RING], count.turn * (16 * state["body"] // RING) + value)

            def loop(times, body, per):
                assert body % RING == 0
                state["body"] = body
                return count.loop(times, per)

            def after_loop(times, body, products=0):
                state["unit"] += (times - 1) * body
                state["product"] += (times - 1) * products

            def claim():
                n = state["product"]
                state["product"] += 1
                if n >= 4:
                    pe.wait_ge(products_taken, at(products_taken))
                return 2 * (n % 4)

            def drained():
                n = state["product"]
                pe.wait_ge(products_taken, n)

            def project(rhs, n, tiles=2, groups=1, used=True):
                g = claim()
                for q in range(groups):
                    w = unit()
                    for j in range(tiles):
                        for kt in range(KT):
                            last = nc.tensor.matmul(ps[:, g + j, 0:n], w[:, kt, j * P:(j + 1) * P],
                                                    rhs[:, q * KT + kt, 0:n], start=(q == 0 and kt == 0),
                                                    stop=(q == groups - 1 and kt == KT - 1))
                    last.then_inc(units_used, 1)

            def normalize(x, sq, n, taken=False):
                for src, ready, bank in ((x, dve_to_pe, 7), (sq, act_to_pe, 6)):
                    if taken and bank == 7:
                        drained()
                    else:
                        pe.wait_ge(ready, at(ready))
                    for kt in range(KT):
                        last = nc.tensor.matmul(ps[:, bank, 0:n], ones, src[:, kt, 0:n],
                                                start=(kt == 0), stop=(kt == KT - 1))
                    last.then_inc(pe_to_dve, 1)
                pe.wait_ge(dve_to_pe, at(dve_to_pe))

            pe.wait_ge(dve_to_pe, at(dve_to_pe))
            with loop(DEPTH * MOD_UNITS // 8, 8, [(dve_to_pe, 1)]):
                pe.wait_ge(dve_to_pe, at(dve_to_pe))
                for q in range(8):
                    w = unit()
                    for j in range(2):
                        for kt in range(KT):
                            last = nc.tensor.matmul(ps[:, q // 4, (q % 4 * 2 + j) * 2:(q % 4 * 2 + j) * 2 + 2],
                                                    w[:, kt, j * P:(j + 1) * P], cs[:, kt, :],
                                                    start=(kt == 0), stop=(kt == KT - 1))
                    last.then_inc(units_used, 1)
            after_loop(DEPTH * MOD_UNITS // 8, 8)
            pe.wait_ge(dve_to_pe, at(dve_to_pe))

            def attend(l, T):
                batches = [(k, b) for k in range(3) for b in range(T // P)]

                def scores(n):
                    k, b = batches[n]
                    lat = b < TB
                    lo = 0 if lat else S
                    if n >= 1:
                        pe.wait_ge(exps_ready, at(exps_ready))
                    for hd in range(4):
                        t, s = hd // 2, hd % 2 * HD
                        extra = lat and k > 0
                        last = nc.tensor.matmul(ps[:, hd, lo:512], qk[s:s + HD, 4 * k + t, b * P:(b + 1) * P],
                                                qk[s:s + HD, 4 * k + 2 + t, lo:512], start=True, stop=not extra)
                        if lat and k == 1:
                            last = nc.tensor.matmul(ps[:, hd, 0:S], ident, C("window")[:, b * S:(b + 1) * S],
                                                    start=False, stop=True)
                        if lat and k == 2:
                            last = nc.tensor.matmul(ps[:, hd, 0:S], C("rev"), bias[:, hd * TB + b, :],
                                                    start=False, stop=True)
                    last.then_inc(scores_ready, 1)

                pe.wait_ge(dve_to_pe, at(dve_to_pe))
                scores(0)
                for n, (k, b) in enumerate(batches):
                    if n + 1 < len(batches):
                        scores(n + 1)
                    else:
                        pe.wait_ge(exps_ready, at(exps_ready))
                    first = 0 if b < TB else TB
                    pe.wait_ge(probs_ready, at(probs_ready))
                    for hd in range(4):
                        if state["turned"] >= 2:
                            pe.wait_ge(turned_kept, at(turned_kept))
                        for kb in range(first, 4):
                            last = nc.tensor.transpose(ps[:, 4 + hd % 2, kb * P:(kb + 1) * P],
                                                       prob[n % 2][:, hd, kb * P:(kb + 1) * P], ident)
                        last.then_inc(turned, 1)
                        state["turned"] += 1
                    if state["mixed"] >= 2:
                        pe.wait_ge(mixed_kept, at(mixed_kept))
                    m = 6 + state["mixed"] % 2
                    for hd in range(4):
                        t, s = hd // 2, hd % 2 * HD
                        pe.wait_ge(turned_kept, state["turned"] - 3 + hd)
                        for kb in range(first, 4):
                            last = nc.tensor.matmul(ps[s:s + HD, m, t * P:(t + 1) * P],
                                                    val[:, kb, k * P + t * HD:k * P + (t + 1) * HD],
                                                    probT[:, hd, kb * P:(kb + 1) * P],
                                                    start=(kb == first), stop=(kb == 3))
                    last.then_inc(mixed, 1)
                    state["mixed"] += 1

            state["turned"] = state["mixed"] = 0

            def layer(l):
                T = 512 if l == 0 else S
                nb = T // P
                pe.wait_ge(dve_to_pe, at(dve_to_pe))
                for kind in range(3):
                    project(u, T)
                    w = unit()
                    g = claim()
                    for kt in range(KT):
                        nc.tensor.matmul(ps[:, g, :], w[:, kt, 0:P], u[:, kt, :],
                                         start=(kt == 0), stop=(kt == KT - 1))
                    for b in range(4):
                        for kt in range(KT):
                            last = nc.tensor.matmul(ps[:, g + 1, b * P:(b + 1) * P], u[:, kt, b * P:(b + 1) * P],
                                                    w[:, kt, P:2 * P], start=(kt == 0), stop=(kt == KT - 1))
                    last.then_inc(units_used, 1)
                    if kind == 0:
                        project(u, T)
                drained()
                pe.wait_ge(act_to_pe, at(act_to_pe))
                for t in range(4):
                    n = T if t < 2 else 512
                    last = nc.tensor.matmul(ps[:, t, 0:n], C("headones"), nsq[:, t, 0:n], start=True, stop=True)
                last.then_inc(pe_to_dve, 1)
                pe.wait_ge(dve_to_pe, at(dve_to_pe))
                for t in range(8):
                    last = nc.tensor.matmul(ps[:, 4 + t // 2, t % 2 * S:(t % 2 + 1) * S], C("rot"),
                                            qk[:, t, 0:S], start=True, stop=True)
                last.then_inc(pe_to_dve, 1)
                for st in range(T // S):
                    for b in range(TB):
                        for t in range(2):
                            last = nc.tensor.matmul(ps[:, b, t * S:(t + 1) * S],
                                                    four[:, t, st * S + b * P:st * S + (b + 1) * P], C("dft"),
                                                    start=True, stop=True)
                    last.then_inc(pe_to_dve, 1)
                    pe.wait_ge(dve_to_pe, at(dve_to_pe))
                    for t in range(2):
                        for j in range(2):
                            for b in range(TB):
                                last = nc.tensor.matmul(ps[:, 2 + t, 0:S], fmid[:, b, t * S + j * P:t * S + (j + 1) * P],
                                                        C("seqsin" if j else "seqcos")[:, b * S:(b + 1) * S],
                                                        start=(j == 0 and b == 0), stop=(j == 1 and b == TB - 1))
                    last.then_inc(pe_to_dve, 1)
                attend(l, T)
                pe.wait_ge(dve_to_pe, at(dve_to_pe))
                for br in range(4):
                    for c in range(4):
                        project(u, T)
                    wb = unit().rearrange("p k c -> p (k c)").rearrange("p (k c) -> p k c", c=D)
                    for c in range(4):
                        g = claim()
                        for j in range(2):
                            for kt in range(2):
                                last = nc.tensor.matmul(ps[:, g + j, 0:T], wb[:, kt, (2 * c + j) * P:(2 * c + j + 1) * P],
                                                        branch[:, 2 * br + kt, 0:T], start=(kt == 0), stop=(kt == 1))
                    last.then_inc(units_used, 1)
                pe.wait_ge(dve_to_pe, at(dve_to_pe))
                for c in range(4):
                    project(merged, T)
                normalize(u, sq1, T)
                pe.wait_ge(dve_to_pe, at(dve_to_pe))
                for b in range(nb):
                    for kt in range(KT):
                        last = nc.tensor.matmul(ps[:, 0, b * E:(b + 1) * E], u[:, kt, b * P:(b + 1) * P],
                                                V("w_router")[:, (l * KT + kt) * E:(l * KT + kt + 1) * E],
                                                start=(kt == 0), stop=(kt == KT - 1))
                last.then_inc(pe_to_dve, 1)
                for b in range(nb):
                    for half in range(2):
                        n = 2 * b + half
                        if n >= 4:
                            pe.wait_ge(act_to_pe, at(act_to_pe))
                        for j in range(4):
                            last = nc.tensor.transpose(ps[:, 4 + n % 4, j * P:(j + 1) * P],
                                                       h[:, 4 * half + j, b * P:(b + 1) * P], ident)
                        last.then_inc(pe_to_act, 1)
                rows = nb // TB * E
                pe.wait_ge(dve_to_pe, at(dve_to_pe))
                for b in range(TB):
                    last = nc.tensor.transpose(ps[0:rows, 1, b * P:(b + 1) * P],
                                               aff[:, b, 0:nb // TB, :].rearrange("p s e -> p (s e)"), ident)
                last.then_inc(pe_to_dve, 1)
                pe.wait_ge(dve_to_pe, at(dve_to_pe))
                for b in range(TB):
                    last = nc.tensor.transpose(ps[:, 2, b * 2 * E:b * 2 * E + rows], rowc[0:rows, b * P:(b + 1) * P],
                                               ident[0:rows, 0:rows])
                last.then_inc(pe_to_dve, 1)
                pe.wait_ge(dve_to_pe, at(dve_to_pe))
                pe.wait_ge(act_to_pe, at(act_to_pe, 4))
                for kt in range(KT):
                    for st in range(nb // TB):
                        n = kt * (nb // TB) + st
                        if n >= 4:
                            pe.wait_ge(dve_to_pe, at(dve_to_pe))
                        for b in range(TB):
                            last = nc.tensor.matmul(ps[:, n % 4, :], htok[:, st * TB + b, kt * P:(kt + 1) * P],
                                                    pick[:, st * TB + b, :], start=(b == 0), stop=(b == TB - 1))
                        last.then_inc(pe_to_dve, 1)
                for q in range(4):
                    for b in range(nb):
                        last = nc.tensor.transpose(ps[:, 4 + q, b * P:(b + 1) * P], wpick[:, b, q * P:(q + 1) * P], ident)
                    last.then_inc(pe_to_act, 1)
                pe.wait_ge(dve_to_pe, at(dve_to_pe, 4))
                pe.wait_ge(act_to_pe, at(act_to_pe, 4))
                slots = CAP * nb // TB
                if l == 0:
                    pe.wait_ge(hidden_ready, at(hidden_ready, 2))
                    pe.wait_ge(y_kept, at(y_kept))
                    count.skip(added, 2)
                with loop(E // GROUP, GROUP_UNITS, [(hidden_ready, 4 * GROUP), (y_kept, GROUP), (added, KT),
                                                    (xcur_ready, GROUP)]) as turn:
                    for e4 in range(GROUP):
                        pe.wait_ge(xcur_ready, at(xcur_ready))
                        for c in range(4):
                            pe.wait_ge(hidden_ready, at(hidden_ready, 0 if c == 0 else 1, less=1))
                            for up in range(2):
                                w = unit()
                                for j in range(2):
                                    for kt in range(KT):
                                        last = nc.tensor.matmul(ps[:, 2 * (c % 2) + up, j * slots:(j + 1) * slots],
                                                                w[:, kt, j * P:(j + 1) * P], xcur[:, kt, 0:slots],
                                                                start=(kt == 0), stop=(kt == KT - 1))
                                last.then_inc(units_used, 1)
                        pe.wait_ge(hidden_ready, at(hidden_ready))
                        pe.wait_ge(y_kept, at(y_kept, 0))
                        for c in range(4):
                            w = unit()
                            for kt in range(KT):
                                last = nc.tensor.matmul(ps[0:slots, 4 + c // 2, c % 2 * UC:(c % 2 + 1) * UC],
                                                        hid[:, kt, 0:slots], w[:, kt, :],
                                                        start=(kt == 0), stop=(kt == KT - 1))
                            last.then_inc(units_used, 1)
                        count.skip(y_kept, 1)
                    pe.wait_ge(y_kept, at(y_kept, 0))
                    for kt in range(KT):
                        pe.wait_ge(added, at(added, 0 if kt == 0 else 1, less=1))
                        for st in range(nb // TB):
                            last = nc.tensor.matmul(ps[:, 6 + kt % 2, st * S:(st + 1) * S],
                                                    y4[:, st, kt * P:(kt + 1) * P],
                                                    wsel[:, bass.ds(turn, 1), st * S:(st + 1) * S]
                                                    .rearrange("p a n -> p (a n)"), start=True, stop=True)
                        last.then_inc(scattered, 1)
                    count.skip(added, 1)
                after_loop(E // GROUP, GROUP_UNITS)
                normalize(u, sq2, T)

            for l in range(DEPTH):
                layer(l)

            def memory_attention():
                for c in range(4):
                    project(mem, S)
                for c in range(4):
                    w = unit()
                    g = claim()
                    for b in range(TB):
                        for kt in range(KT):
                            last = nc.tensor.matmul(ps[:, g + b, 0:S], mem[:, kt, b * P:(b + 1) * P], w[:, kt, :],
                                                    start=(kt == 0), stop=(kt == KT - 1))
                    last.then_inc(units_used, 1)
                pe.wait_ge(normed, at(normed))
                for c in range(4):
                    project(h, S)
                drained()
                for b in range(TB):
                    for hd in range(4):
                        for j in range(2):
                            last = nc.tensor.matmul(ps[:, hd // 2, hd % 2 * S:(hd % 2 + 1) * S],
                                                    xq[:, 2 * hd + j, b * P:(b + 1) * P], xk[:, 2 * hd + j, :],
                                                    start=(j == 0), stop=(j == 1))
                    last.then_inc(pe_to_dve, 1)
                    pe.wait_ge(dve_to_pe, at(dve_to_pe))
                    for hd in range(4):
                        for kb in range(TB):
                            n = 2 * hd + kb
                            last = nc.tensor.transpose(ps[:, 2 + n // 4, n % 4 * P:(n % 4 + 1) * P],
                                                       xp[:, hd, kb * P:(kb + 1) * P], ident)
                    last.then_inc(pe_to_act, 1)
                    pe.wait_ge(act_to_pe, at(act_to_pe))
                    for t in range(KT):
                        for kb in range(TB):
                            last = nc.tensor.matmul(ps[:, 4 + t // 4, t % 4 * P:(t % 4 + 1) * P],
                                                    xv[:, kb, t * P:(t + 1) * P], xpT[:, t // 2 * 2 + kb, :],
                                                    start=(kb == 0), stop=(kb == TB - 1))
                    last.then_inc(pe_to_dve, 1)
                pe.wait_ge(dve_to_pe, at(dve_to_pe))
                for c in range(4):
                    project(xo, S)
                normalize(t1, t2, S, taken=True)

            def mlp():
                pe.wait_ge(normed, at(normed))
                with loop(2, 8, [(products_taken, 8)]):
                    for c in range(8):
                        project(h, S)
                after_loop(2, 8, 8)
                pe.wait_ge(squares_kept, at(squares_kept, 16))
                for c in range(4):
                    project(relu2, S, groups=4)
                normalize(t1, t2, S, taken=True)

            def even_mixer():
                pe.wait_ge(normed, at(normed, 4))
                for kt in range(KT):
                    last = nc.tensor.matmul(ps[0:16, 7, 0:S], V("w_dt")[:, kt * 16:(kt + 1) * 16], h[:, kt, 0:S],
                                            start=(kt == 0), stop=(kt == KT - 1))
                last.then_inc(pe_to_dve, 1)
                pe.wait_ge(dve_to_pe, at(dve_to_pe))
                for c in range(18):
                    project(h, S)
                drained()
                normalize(conv, t2, S)
                for n, rows in enumerate((dtv, acs)):
                    for b in range(TB):
                        last = nc.tensor.transpose(ps[:, 5, (2 * n + b) * 16:(2 * n + b + 1) * 16],
                                                   rows[:, b * P:(b + 1) * P], ident[0:16, 0:16])
                last.then_inc(pe_to_dve, 1)
                pe.wait_ge(dve_to_pe, at(dve_to_pe))
                for b in range(TB):
                    for n in range(2):
                        for j in range(4):
                            last = nc.tensor.transpose(ps[:, 2 * b + n, j * P:(j + 1) * P],
                                                       xbc[:, 4 * n + j, b * P:(b + 1) * P], ident)
                last.then_inc(pe_to_dve, 1)
                for g in range(2):
                    nc.tensor.matmul(ps[:, 4 + g, 0:S], xbc[:, 8 + g, 0:P], xbc[:, 10 + g, :], start=True, stop=True)
                    last = nc.tensor.matmul(ps[:, 4 + g, S:S + P], xbc[:, 8 + g, P:S], xbc[:, 10 + g, P:S],
                                            start=True, stop=True)
                last.then_inc(pe_to_dve, 1)
                pe.wait_ge(dve_to_pe, at(dve_to_pe))

                def spread(n):
                    if n >= 2:
                        pe.wait_ge(decay_ready, at(decay_ready))
                    bank = ps[:, n % 2, :]
                    nc.tensor.matmul(bank[:, 0:S], sel[:, n, :], acs, start=True, stop=False)
                    nc.tensor.matmul(bank[:, 0:P], ident, C("causal"), start=False, stop=True)
                    nc.tensor.matmul(bank[:, S:S + P], sel[:, n, :], acs[:, P:S], start=True, stop=False)
                    nc.tensor.matmul(bank[:, S:S + P], ident, C("causal"), start=False, stop=True)\
                        .then_inc(pe_to_act, 1)

                spread(0)
                for n in range(SSM_HEADS):
                    if n + 1 < SSM_HEADS:
                        spread(n + 1)
                    pe.wait_ge(dve_to_pe, at(dve_to_pe))
                    t, s = n // 2, n % 2 * HD
                    if n % 2 == 0 and t >= 2:
                        pe.wait_ge(y_tile_kept, at(y_tile_kept))
                    y = ps[s:s + HD, 2 + t % 2, :]
                    nc.tensor.matmul(y[:, 0:S], xdt[:, 0, n * HD:(n + 1) * HD], mask[n % 2][:, 0:S],
                                     start=True, stop=False)
                    last = nc.tensor.matmul(y[:, P:S], xdt[:, 1, n * HD:(n + 1) * HD], mask[n % 2][:, S:384],
                                            start=False, stop=True)
                    last.then_inc(head_done, 1)
                pe.wait_ge(y_tile_kept, at(y_tile_kept, 2))
                pe.wait_ge(act_to_pe, at(act_to_pe))
                for g in range(2):
                    for j in range(4):
                        last = nc.tensor.matmul(ps[:, 6 + g, 0:S], ones, t2[:, 4 * g + j, :], start=(j == 0), stop=(j == 3))
                last.then_inc(pe_to_dve, 1)
                pe.wait_ge(dve_to_pe, at(dve_to_pe))
                for c in range(4):
                    project(mixin, S, groups=2)
                normalize(t1, t2, S, taken=True)

            def odd_mixer():
                pe.wait_ge(normed, at(normed))
                for c in range(4):
                    project(h, S)
                for c in range(4):
                    w = unit()
                    g = claim()
                    for b in range(TB):
                        for kt in range(KT):
                            last = nc.tensor.matmul(ps[:, g + b, 0:S], h[:, kt, b * P:(b + 1) * P], w[:, kt, :],
                                                    start=(kt == 0), stop=(kt == KT - 1))
                    last.then_inc(units_used, 1)
                for c in range(4):
                    project(h, S)
                drained()
                for kt in range(KT):
                    last = nc.tensor.matmul(ps[0:16, 0, 0:S], V("w_low")[:, kt * 16:(kt + 1) * 16], h[:, kt, 0:S],
                                            start=(kt == 0), stop=(kt == KT - 1))
                last.then_inc(pe_to_dve, 1)
                pe.wait_ge(dve_to_pe, at(dve_to_pe))
                for hd in range(4):
                    last = nc.tensor.matmul(ps[:, 2 + hd // 2, hd % 2 * S:(hd % 2 + 1) * S],
                                            V("w_gate2")[0:16, hd * P:(hd + 1) * P], low, start=True, stop=True)
                last.then_inc(pe_to_dve, 1)
                pe.wait_ge(dve_to_pe, at(dve_to_pe))
                for b in range(TB):
                    for hd in range(4):
                        last = nc.tensor.transpose(ps[:, b, hd * P:(hd + 1) * P], kend[:, hd, b * P:(b + 1) * P], ident)
                last.then_inc(pe_to_act, 1)
                for b in range(TB):
                    for hd in range(4):
                        last = nc.tensor.matmul(ps[:, 4 + b, hd * P:(hd + 1) * P], ktl[:, hd, b * P:(b + 1) * P],
                                                qt[:, hd, b * P:(b + 1) * P], start=True, stop=True)
                last.then_inc(pe_to_dve, 1)
                pe.wait_ge(act_to_pe, at(act_to_pe))
                pe.wait_ge(dve_to_pe, at(dve_to_pe))
                for c in range(3):
                    for hd in range(4):
                        n = c * 4 + hd
                        if n >= 2:
                            pe.wait_ge(dve_to_pe, at(dve_to_pe))
                        lo = c % 2 * GLA_CHUNK
                        nc.tensor.matmul(ps[:, 6 + n % 2, 0:S], kendT[lo:lo + GLA_CHUNK, c // 2 * 4 + hd, :],
                                         gv[lo:lo + GLA_CHUNK, c // 2, hd * S:(hd + 1) * S], start=True, stop=True)\
                            .then_inc(pe_to_dve, 1)
                pe.wait_ge(dve_to_pe, at(dve_to_pe, 2))
                for hd in range(4):
                    for j in range(2):
                        v0 = hd * S + j * P
                        for b in range(TB):
                            nc.tensor.matmul(ps[:, hd, j * S + b * P:j * S + (b + 1) * P], gv[:, b, v0:v0 + P],
                                             att[:, b * 4 + hd, :], start=True, stop=False)
                            for c in range(2 * b, 2 * b + 2):
                                if c:
                                    last = nc.tensor.matmul(
                                        ps[:, hd, j * S + c * GLA_CHUNK:j * S + (c + 1) * GLA_CHUNK],
                                        hist[:, hd, (c - 1) * S + j * P:(c - 1) * S + (j + 1) * P],
                                        qt[:, hd, c * GLA_CHUNK:(c + 1) * GLA_CHUNK], start=False, stop=(c % 2 == 1))
                last.then_inc(pe_to_dve, 1)
                pe.wait_ge(act_to_pe, at(act_to_pe))
                for hd in range(4):
                    for j in range(2):
                        last = nc.tensor.matmul(ps[:, 4 + hd // 2, hd % 2 * S:(hd % 2 + 1) * S], ones,
                                                t2[:, 2 * hd + j, :], start=(j == 0), stop=(j == 1))
                last.then_inc(pe_to_dve, 1)
                pe.wait_ge(dve_to_pe, at(dve_to_pe))
                for c in range(4):
                    project(go, S)
                normalize(t1, t2, S, taken=True)

            even_mixer()
            pe.wait_ge(memory_loaded, 16)
            memory_attention()
            mlp()
            odd_mixer()
            memory_attention()
            mlp()
            assert state["unit"] == n_units

        @block.scalar
        def _(act):
            count = Count(act)
            at = count.at

            def link(instruction):
                instruction.then_inc(act_step, 1)
                act.wait_ge(act_step, at(act_step))
            A = nc.scalar.activation

            def inverse_roots(*tiles):
                act.wait_ge(variances_ready, at(variances_ready))
                for x in tiles:
                    last = A(x, x, ACT.Ln)
                link(last)
                for x in tiles:
                    last = A(x, x, ACT.Exp, scale=-0.5)
                last.then_inc(inverses_ready, 1)

            def normalize(x, sq, n, tiles, gain, shift, signal=True):
                act.wait_ge(dve_to_act, at(dve_to_act))
                A(sq[:, :, 0:n], x[:, :, 0:n], ACT.Square).then_inc(act_to_pe, 1)
                inverse_roots(stat2[:, 0:n])
                act.wait_ge(dve_to_act, at(dve_to_act))
                for kt in range(KT):
                    last = A(tiles[:, kt, 0:n], x[:, kt, 0:n], ACT.Identity, bias=shift[:, kt:kt + 1],
                             scale=gain[:, kt:kt + 1])
                if signal:
                    last.then_inc(normed, 1)
                else:
                    link(last)

            act.wait_ge(inputs_loaded, 48)
            A(cs[:, :, :], V("c").rearrange("p (k s) -> p k s", s=2), ACT.Exp, scale=-1.0).then_inc(act_to_dve, 1)
            count.skip(units_used, DEPTH * MOD_UNITS)
            state = {"turned": 0, "product": 0, "mixed": 0}

            def attend(l, T):
                batches = [(k, b) for k in range(3) for b in range(T // P)]

                def exps(n):
                    k, b = batches[n]
                    lo = 0 if b < TB else S
                    m = mx[:, n % 2 * 4:n % 2 * 4 + 4]
                    act.wait_ge(dve_to_act, at(dve_to_act))
                    for hd in range(4):
                        last = A(prob[n % 2][:, hd, lo:512], ps[:, hd, lo:512], ACT.Exp, scale=HD ** -0.5,
                                 bias=m[:, hd:hd + 1], accum_out=sums[:, n % 2 * 4 + hd:n % 2 * 4 + hd + 1])
                    if k == 1:
                        last = A(es[:, n % 2 * 4:n % 2 * 4 + 4], es[:, n % 2 * 4:n % 2 * 4 + 4], ACT.Exp)
                    last.then_inc(exps_ready, 1)

                exps(0)
                for n, (k, b) in enumerate(batches):
                    if n + 1 < len(batches):
                        exps(n + 1)
                    lo = 0 if b < TB else S
                    if l or n:
                        act.wait_ge(mixed, at(mixed, 0))
                    for hd in range(4):
                        act.wait_ge(turned, at(turned))
                        A(probT[:, hd, lo:512], ps[:, 4 + hd % 2, lo:512], ACT.Copy).then_inc(turned_kept, 1)
                    count.skip(mixed, 1)

            def layer(l):
                T = 512 if l == 0 else S
                nb = T // P
                count.skip(units_used, 7)
                act.wait_ge(dve_to_act, at(dve_to_act))
                A(nsq[:, 0:2, 0:T], qk[:, 0:2, 0:T], ACT.Square)
                A(nsq[:, 2:4, :], qk[:, 2:4, :], ACT.Square).then_inc(act_to_pe, 1)
                state["product"] += 7
                inverse_roots(nsq[:, 0:2, 0:T], nsq[:, 2:4, :])
                attend(l, T)
                for br in range(4):
                    if br:
                        act.wait_ge(dve_to_act, at(dve_to_act))
                    for c in range(4):
                        g = 2 * (state["product"] % 4)
                        state["product"] += 1
                        act.wait_ge(units_used, at(units_used))
                        A(gate[:, 2 * c:2 * c + 2, 0:T], ps[:, g:g + 2, 0:T], ACT.Exp, scale=-1.0)\
                            .then_inc(act_to_dve, 1)
                    count.skip(units_used, 1)
                    state["product"] += 4
                count.skip(units_used, 4)
                state["product"] += 4
                normalize(u, sq1, T, h, V("ln1_g")[:, l * KT:], V("ln1_b")[:, l * KT:])
                act.wait_ge(dve_to_act, at(dve_to_act))
                A(logit[:, 0:nb, :], logit[:, 0:nb, :], ACT.Exp).then_inc(act_to_dve, 1)
                for b in range(nb):
                    for half in range(2):
                        act.wait_ge(pe_to_act, at(pe_to_act))
                        A(htok[:, b, half * 512:(half + 1) * 512], ps[:, 4 + (2 * b + half) % 4, :], ACT.Copy)\
                            .then_inc(act_to_pe, 1)
                for q in range(4):
                    act.wait_ge(pe_to_act, at(pe_to_act))
                    A(wsel[:, q, 0:T], ps[:, 4 + q, 0:T], ACT.Copy).then_inc(act_to_pe, 1)
                slots = CAP * nb // TB
                act.wait_ge(dve_to_act, at(dve_to_act))
                with count.loop(E // GROUP, [(units_used, GROUP_UNITS)]) as turn:
                    for e4 in range(GROUP):
                        act.wait_ge(units_used, at(units_used, 0, less=4))
                        A(xcur[:, :, 0:slots], xs[:, :, bass.ds(turn * GROUP + e4, 1), 0:slots]
                          .rearrange("p k a s -> p k (a s)"), ACT.Copy).then_inc(xcur_ready, 1)
                        for c in range(4):
                            act.wait_ge(units_used, at(units_used))
                            A(eneg[:, c % 2, 0:2 * slots], ps[:, 2 * (c % 2), 0:2 * slots], ACT.Exp, scale=-1.0)\
                                .then_inc(act_to_dve, 1)
                            count.skip(units_used, 1)
                        count.skip(units_used, 4)
                normalize(u, sq2, T, h, V("ln2_g")[:, l * KT:], V("ln2_b")[:, l * KT:])

            for l in range(DEPTH):
                layer(l)

            def latent_norm(n):
                normalize(t1, t2, S, h, V("ln_g")[:, n * KT:], V("ln_b")[:, n * KT:])

            def memory_attention():
                count.skip(units_used, 12)
                state["product"] += 12
                for b in range(TB):
                    act.wait_ge(dve_to_act, at(dve_to_act))
                    for hd in range(4):
                        last = A(xp[:, hd, :], ps[:, hd // 2, hd % 2 * S:(hd % 2 + 1) * S], ACT.Exp, scale=1.0 / 16,
                                 bias=mx[:, hd:hd + 1], accum_out=sums[:, hd:hd + 1])
                    last.then_inc(act_to_dve, 1)
                    act.wait_ge(pe_to_act, at(pe_to_act))
                    A(xpT[:, :, :], ps[:, 2:4, :].rearrange("p a (b n) -> p (a b) n", n=P), ACT.Copy)\
                        .then_inc(act_to_pe, 1)
                count.skip(units_used, 4)
                state["product"] += 4

            def even_mixer():
                A(nega, V("a_log")[0:16, :], ACT.Exp)
                act.wait_ge(dve_to_act, at(dve_to_act))
                A(dtc, dts, ACT.Exp, scale=-1.0).then_inc(act_to_dve, 1)
                act.wait_ge(dve_to_act, at(dve_to_act))
                A(dts, acs, ACT.Ln).then_inc(act_to_dve, 1)
                for c in range(4):
                    act.wait_ge(units_used, at(units_used, 2))
                    g = 2 * ((state["product"] + 1) % 4)
                    state["product"] += 2
                    if c:
                        act.wait_ge(dve_to_act, at(dve_to_act))
                    A(egate, ps[:, g:g + 2, 0:S], ACT.Exp, scale=-1.0).then_inc(act_to_dve, 1)
                count.skip(units_used, 6)
                state["product"] += 6
                for c in range(4):
                    act.wait_ge(units_used, at(units_used))
                    g = 2 * (state["product"] % 4)
                    state["product"] += 1
                    act.wait_ge(dve_to_act, at(dve_to_act))
                    A(egate, ps[:, g:g + 2, 0:S], ACT.Exp, scale=-1.0).then_inc(act_to_dve, 1)
                act.wait_ge(dve_to_act, at(dve_to_act))
                A(xneg, xbc[:, :, :], ACT.Exp, scale=-1.0).then_inc(act_to_dve, 1)
                normalize(conv, t2, S, mixin, V("conv_ln_g"), V("conv_ln_b"), signal=False)
                A(conv, mixin[:, 0:KT, :], ACT.Exp, scale=-1.0).then_inc(act_to_dve, 1)
                for n in range(SSM_HEADS):
                    act.wait_ge(pe_to_act, at(pe_to_act))
                    A(decay[n % 2][:, 0:S], ps[:, n % 2, 0:S], ACT.Exp, bias=acsT[:, n:n + 1])
                    A(decay[n % 2][:, S:384], ps[:, n % 2, S:384], ACT.Exp, bias=acsT[:, 16 + n:17 + n])\
                        .then_inc(decay_ready, 1)
                act.wait_ge(dve_to_act, at(dve_to_act))
                A(t2, mixin[:, KT:, :], ACT.Square).then_inc(act_to_pe, 1)
                inverse_roots(small[:, 0:512])
                count.skip(units_used, 8)
                state["product"] += 4

            def odd_mixer():
                count.skip(units_used, 8)
                state["product"] += 8
                for c in range(4):
                    act.wait_ge(units_used, at(units_used))
                    g = 2 * (state["product"] % 4)
                    state["product"] += 1
                    if c:
                        act.wait_ge(dve_to_act, at(dve_to_act))
                    A(gmid[:, 0:2, :], ps[:, g:g + 2, 0:S], ACT.Exp, scale=-1.0).then_inc(act_to_dve, 1)
                act.wait_ge(dve_to_act, at(dve_to_act))
                link(A(en, en, ACT.Exp, scale=-1.0))
                A(en, en, ACT.Ln, bias=1.0).then_inc(act_to_dve, 1)
                act.wait_ge(dve_to_act, at(dve_to_act))
                A(qt, eb, ACT.Exp)
                A(ktl, eb, ACT.Exp, scale=-1.0)
                A(kend, gmid, ACT.Exp)
                A(gend, eb.rearrange("p h (c n) -> p h c n", n=GLA_CHUNK)[:, :, :, GLA_CHUNK - 1], ACT.Exp)\
                    .then_inc(act_to_dve, 1)
                act.wait_ge(pe_to_act, at(pe_to_act))
                A(kendT, ps[:, 0:2, :].rearrange("p b (h n) -> p (b h) n", n=P), ACT.Copy).then_inc(act_to_pe, 1)
                act.wait_ge(dve_to_act, at(dve_to_act))
                A(t2, go, ACT.Square).then_inc(act_to_pe, 1)
                inverse_roots(small[:, 0:1024])
                count.skip(units_used, 4)
                state["product"] += 4

            even_mixer()
            latent_norm(0)
            for l in range(DEPTH):
                if l:
                    odd_mixer()
                    latent_norm(3)
                memory_attention()
                latent_norm(3 * l + 1)
                count.skip(units_used, 32)
                state["product"] += 20
                latent_norm(3 * l + 2)

        @block.vector
        def _(dve):
            count = Count(dve)
            at = count.at

            def link(instruction):
                instruction.then_inc(dve_step, 1)
                dve.wait_ge(dve_step, at(dve_step))
            v = nc.vector
            state = {"product": 0}

            def product(more=1):
                dve.wait_ge(units_used, at(units_used, more))
                g = 2 * (state["product"] % 4)
                state["product"] += 1
                return g

            def taken(instruction, n=1):
                instruction.then_inc(products_taken, n)

            def wide(x, shape, axis=1):
                return x.unsqueeze(axis).broadcast_to(shape)

            def normalize(x, n, eps):
                dve.wait_ge(pe_to_dve, at(pe_to_dve))
                link(v.tensor_scalar(stat[:, 0:n], ps[:, 7, 0:n], 1.0 / D, None, ALU.mult))
                v.tensor_tensor(x[:, :, 0:n], x[:, :, 0:n], wide(stat[:, 0:n], [P, KT, n]), ALU.subtract).then_inc(dve_to_act, 1)
                dve.wait_ge(pe_to_dve, at(pe_to_dve))
                v.tensor_scalar(stat2[:, 0:n], ps[:, 6, 0:n], 1.0 / D, eps, ALU.mult, ALU.add)\
                    .then_inc(variances_ready, 1)
                mark().then_inc(dve_to_pe, 1)
                dve.wait_ge(inverses_ready, at(inverses_ready))
                v.tensor_tensor(x[:, :, 0:n], x[:, :, 0:n], wide(stat2[:, 0:n], [P, KT, n]), ALU.mult).then_inc(dve_to_act, 1)

            def modulate(l, chunk, streams):
                for kt in range(KT):
                    for st in range(streams):
                        last = v.tensor_scalar(u[:, kt, st * S:(st + 1) * S], h[:, kt, st * S:(st + 1) * S],
                                               mod[:, l * 48 + (chunk + 1) * 8 + kt, st:st + 1],
                                               mod[:, l * 48 + chunk * 8 + kt, st:st + 1], ALU.mult, ALU.add)
                last.then_inc(dve_to_pe, 1)

            def mark():
                return v.tensor_copy(tick, ident[:, 0:1])

            def settle():
                link(mark())

            def sigmoid(e):
                link(v.tensor_scalar(e, e, 1.0, None, ALU.add))
                link(v.reciprocal(e, e))

            dve.wait_ge(inputs_loaded, 48)
            dve.wait_ge(act_to_dve, at(act_to_dve))
            sigmoid(cs[:, :, :])
            v.tensor_tensor(cs[:, :, :], cs[:, :, :], V("c").rearrange("p (k s) -> p k s", s=2), ALU.mult).then_inc(dve_to_pe, 2)
            with count.loop(DEPTH * MOD_UNITS // 8, [(units_used, 8)]) as turn:
                dve.wait_ge(units_used, at(units_used, 8))
                v.tensor_tensor(
                    mod[:, bass.ds(turn * 16, 16), :].rearrange("p (h t) s -> p h t s", h=2),
                    ps[:, 0:2, 0:16].rearrange("p h (t s) -> p h t s", s=2),
                    wide(V("b_mod")[:, bass.ds(turn * 16, 16)].rearrange("p (h t) -> p h t", h=2), [P, 2, 8, 2], 3),
                    ALU.add).then_inc(dve_to_pe, 1)
            dve.wait_ge(dve_to_pe, 2 + DEPTH * MOD_UNITS // 8)
            for l in range(DEPTH):
                for chunk in (1, 4):
                    m = mod[:, l * 48 + chunk * 8:l * 48 + chunk * 8 + 8, :]
                    last = v.tensor_scalar(m, m, 1.0, None, ALU.add)
            link(last)
            v.tensor_scalar(nsink, V("sink"), -1.0, None, ALU.mult)
            v.memset(mx[:, 0:1], 0.0).then_inc(hidden_ready, 2)
            v.memset(mx[:, 1:2], 0.0).then_inc(y_kept, 1)

            def attend(l, T):
                batches = [(k, b) for k in range(3) for b in range(T // P)]

                def maxima(n):
                    k, b = batches[n]
                    lo = 0 if b < TB else S
                    m = mx[:, n % 2 * 4:n % 2 * 4 + 4]
                    dve.wait_ge(scores_ready, at(scores_ready))
                    link(v.tensor_reduce(m, ps[:, 0:4, lo:512], AX.X, ALU.max))
                    last = v.tensor_scalar(m, m, -(HD ** -0.5), None, ALU.mult)
                    if k == 1:
                        link(last)
                        link(v.tensor_tensor(m, m, nsink[:, 4 * l:4 * l + 4], ALU.min))
                        last = v.tensor_tensor(es[:, n % 2 * 4:n % 2 * 4 + 4], m, nsink[:, 4 * l:4 * l + 4], ALU.subtract)
                    last.then_inc(dve_to_act, 1)

                def keep(n):
                    k, b = batches[n]
                    dve.wait_ge(mixed, at(mixed))
                    o = 0 if k == 0 else 2 * k + 2
                    v.tensor_copy(branch[:, o:o + 2, b * P:(b + 1) * P],
                                            ps[:, 6 + state["mixed"] % 2, 0:2 * P].rearrange("p (t n) -> p t n", n=P)).then_inc(mixed_kept, 1)
                    state["mixed"] += 1

                maxima(0)
                for n, (k, b) in enumerate(batches):
                    lo = 0 if b < TB else S
                    q = n % 2 * 4
                    dve.wait_ge(exps_ready, at(exps_ready))
                    if k == 1:
                        link(v.tensor_tensor(sums[:, q:q + 4], sums[:, q:q + 4], es[:, q:q + 4], ALU.add))
                    link(v.reciprocal(rec[:, 0:4], sums[:, q:q + 4]))
                    pr = prob[n % 2][:, :, lo:512]
                    v.tensor_tensor(pr, pr, wide(rec[:, 0:4], [P, 4, 512 - lo], 2), ALU.mult).then_inc(probs_ready, 1)
                    if n + 1 < len(batches):
                        maxima(n + 1)
                    if n:
                        keep(n - 1)
                keep(len(batches) - 1)

            state["mixed"] = 0

            def layer(l):
                T = 512 if l == 0 else S
                nb, ns = T // P, T // S
                if l:
                    dve.wait_ge(normed, at(normed))
                modulate(l, 0, 2)
                for kind in range(3):
                    g = product()
                    taken(v.tensor_copy(qk[:, 4 * kind:4 * kind + 2, 0:T], ps[:, g:g + 2, 0:T]))
                    g = product()
                    for t in range(2):
                        for half in range(2):
                            v.tensor_copy(qk[half * HD:(half + 1) * HD, 4 * kind + 2 + t, :],
                                          ps[t * HD:(t + 1) * HD, g, :])
                    last = v.tensor_copy(val[:, :, kind * P:(kind + 1) * P],
                                         ps[:, g + 1, :].rearrange("p (b n) -> p b n", n=P))
                    taken(last)
                    if kind == 0:
                        g = product()
                        mark().then_inc(dve_to_act, 1)
                        taken(v.tensor_copy(four[:, :, 0:T], ps[:, g:g + 2, 0:T]))
                dve.wait_ge(pe_to_dve, at(pe_to_dve))
                for t, n in ((0, T), (2, 512)):
                    v.tensor_scalar(nsq[:, t:t + 2, 0:n], ps[:, t:t + 2, 0:n], 1.0 / HD, EPS1, ALU.mult, ALU.add)
                mark().then_inc(variances_ready, 1)
                dve.wait_ge(inverses_ready, at(inverses_ready))
                for t, n in ((0, T), (2, 512)):
                    last = v.scalar_tensor_tensor(qk[:, t:t + 2, 0:n], qk[:, t:t + 2, 0:n],
                                                  V("qk_gain")[:, 2 * l + t // 2:2 * l + t // 2 + 1],
                                                  nsq[:, t:t + 2, 0:n], ALU.mult, ALU.mult)
                last.then_inc(dve_to_pe, 1)
                dve.wait_ge(pe_to_dve, at(pe_to_dve))
                link(v.tensor_tensor(rtmp, ps[:, 4:8, :].rearrange("p a (b n) -> p (a b) n", n=S),
                                          wide(C("sin"), [P, 8, S]), ALU.mult))
                link(v.tensor_tensor(qk[:, 0:8, 0:S], qk[:, 0:8, 0:S], wide(C("cos"), [P, 8, S]), ALU.mult))
                link(v.tensor_tensor(qk[:, 0:8, 0:S], qk[:, 0:8, 0:S], rtmp, ALU.add))
                for st in range(ns):
                    dve.wait_ge(pe_to_dve, at(pe_to_dve))
                    v.tensor_copy(fmid, ps[:, 0:2, :]).then_inc(dve_to_pe, 1)
                    dve.wait_ge(pe_to_dve, at(pe_to_dve))
                    v.tensor_copy(branch[:, 2:4, st * S:(st + 1) * S], ps[:, 2:4, 0:S])
                dve.wait_ge(bias_loaded, 16 * 16 * (l + 1))
                rows = bias.rearrange("p a (r c) -> p (a r) c", c=64)
                v.scalar_tensor_tensor(rows, rows, HD ** 0.5, wide(C("near"), [P, 32, 64]), ALU.mult, ALU.add)\
                    .then_inc(dve_to_pe, 1)
                attend(l, T)
                mark().then_inc(dve_to_pe, 1)
                for br in range(4):
                    for c in range(4):
                        state["product"] += 1
                        dve.wait_ge(units_used, at(units_used))
                        dve.wait_ge(act_to_dve, at(act_to_dve))
                        e = gate[:, 2 * c:2 * c + 2, 0:T]
                        a = v.tensor_scalar(e, e, 1.0, None, ALU.add)
                        a.then_inc(products_taken, 1)
                        settle()
                        v.reciprocal(e, e)
                    settle()
                    for c in range(4):
                        g = product(1 if c == 0 else 0)
                        e, m = gate[:, 2 * c:2 * c + 2, 0:T], merged[:, 2 * c:2 * c + 2, 0:T]
                        if br == 0:
                            last = v.tensor_tensor(m, e, ps[:, g:g + 2, 0:T], ALU.mult)
                            taken(last)
                        else:
                            t = gated[c % 2][:, :, 0:T]
                            taken(v.tensor_tensor(t, e, ps[:, g:g + 2, 0:T], ALU.mult))
                            settle()
                            last = v.tensor_tensor(m, m, t, ALU.add)
                    if br < 3:
                        settle()
                        mark().then_inc(dve_to_act, 1)
                    else:
                        last.then_inc(dve_to_pe, 1)
                for c in range(4):
                    g = product()
                    for j in range(2):
                        for st in range(ns):
                            last = v.tensor_scalar(u[:, 2 * c + j, st * S:(st + 1) * S],
                                                   ps[:, g + j, st * S:(st + 1) * S],
                                                   mod[:, l * 48 + 16 + 2 * c + j, st:st + 1], None, ALU.mult)
                    taken(last)
                settle()
                v.scalar_tensor_tensor(u[:, :, 0:T], h[:, :, 0:T], ALPHA, u[:, :, 0:T], ALU.mult, ALU.add)\
                    .then_inc(dve_to_pe, 1)
                normalize(u, T, EPS1)
                dve.wait_ge(normed, at(normed))
                modulate(l, 3, ns)
                dve.wait_ge(pe_to_dve, at(pe_to_dve))
                lg, lp = logit[:, 0:nb, :], ps[:, 0, 0:nb * E].rearrange("p (b e) -> p b e", e=E)
                link(v.tensor_reduce(mx[:, 0:nb], lp, AX.X, ALU.max))
                v.tensor_tensor(lg, lp, wide(mx[:, 0:nb], [P, nb, E], 2), ALU.subtract).then_inc(dve_to_act, 1)
                dve.wait_ge(act_to_dve, at(act_to_dve))
                link(v.tensor_reduce(sums[:, 0:nb], lg, AX.X, ALU.add))
                link(v.reciprocal(rec[:, 0:nb], sums[:, 0:nb]))
                for st in range(ns):
                    last = v.tensor_tensor(aff[:, :, st, :], logit[:, st * TB:(st + 1) * TB, :],
                                           wide(rec[:, st * TB:(st + 1) * TB], [P, TB, E], 2), ALU.mult)
                last.then_inc(dve_to_pe, 1)
                R = ns * E
                ra, rb, rc = rowa[0:R, :], rowb[0:R, :], rowc[0:R, :]
                dve.wait_ge(pe_to_dve, at(pe_to_dve))
                link(v.tensor_copy(ra, ps[0:R, 1, 0:S]))
                src = ra
                for r, dst in enumerate((rb, rc, rb, rc)):
                    link(v.max(top8[0:R, r, :], src))
                    link(v.match_replace(dst, top8[0:R, r, :], src, -1.0))
                    src = dst
                v.memset(onesrow[0:R, :], 1.0)
                link(v.tensor_scalar(rb, rc, 0.0, None, ALU.is_lt))
                link(v.tensor_tensor_scan(ra, onesrow[0:R, :], rb, 0.0, ALU.mult, ALU.add))
                link(v.tensor_tensor(rc, ra, rb, ALU.mult))
                v.tensor_scalar(rc, rc, -1.0, None, ALU.add).then_inc(dve_to_pe, 1)
                dve.wait_ge(pe_to_dve, at(pe_to_dve))
                link(v.tensor_copy(rank[:, :, 0:ns, :], ps[:, 2, 0:TB * 2 * E]
                                        .rearrange("p (b s e) -> p b s e", b=TB, s=2)[:, :, 0:ns, :]))
                for st in range(ns):
                    for b in range(TB):
                        sel4 = pick[:, st * TB + b, :].rearrange("p (e n) -> p e n", n=CAP)
                        v.tensor_tensor(sel4, wide(rank[:, b, st, :], [P, E, CAP], 2), wide(C("iota"), [P, E, CAP]),
                                        ALU.is_equal)
                settle()
                for st in range(ns):
                    for b in range(TB):
                        sel4 = pick[:, st * TB + b, :].rearrange("p (e n) -> p e n", n=CAP)
                        last = v.tensor_tensor(wpick[:, st * TB + b, :].rearrange("p (e n) -> p e n", n=CAP), sel4,
                                               wide(aff[:, b, st, :], [P, E, CAP], 2), ALU.mult)
                last.then_inc(dve_to_pe, 1)
                for kt in range(KT):
                    for st in range(ns):
                        dve.wait_ge(pe_to_dve, at(pe_to_dve))
                        v.tensor_scalar(xs[:, kt, :, st * CAP:(st + 1) * CAP],
                                        ps[:, (kt * ns + st) % 4, :].rearrange("p (e n) -> p e n", n=CAP),
                                        mod[:, l * 48 + 32 + kt, st:st + 1], mod[:, l * 48 + 24 + kt, st:st + 1],
                                        ALU.mult, ALU.add).then_inc(dve_to_pe, 1)
                slots = CAP * ns
                mark().then_inc(dve_to_act, 1)
                dve.wait_ge(units_used, at(units_used, 0, less=-1))
                last = v.memset(acc[:, :, 0:T], 0.0)
                if l == 0:
                    last.then_inc(added, 2)
                else:
                    link(last)
                with count.loop(E // GROUP, [(units_used, GROUP_UNITS), (act_to_dve, 4 * GROUP), (scattered, KT),
                                            (dve_step, 3 * 4 * GROUP)]):
                    for e4 in range(GROUP):
                        for c in range(4):
                            e = eneg[:, c % 2, 0:2 * slots]
                            dve.wait_ge(act_to_dve, at(act_to_dve))
                            link(v.tensor_scalar(e, e, 1.0, None, ALU.add))
                            link(v.reciprocal(e, e))
                            link(v.tensor_tensor(e, e, ps[:, 2 * (c % 2), 0:2 * slots], ALU.mult))
                            dve.wait_ge(units_used, at(units_used, 2))
                            v.tensor_tensor(hid[:, 2 * c:2 * c + 2, 0:slots], e.rearrange("p (j n) -> p j n", j=2),
                                            ps[:, 2 * (c % 2) + 1, 0:2 * slots].rearrange("p (j n) -> p j n", j=2),
                                            ALU.mult).then_inc(hidden_ready, 1)
                        dve.wait_ge(units_used, at(units_used, 4))
                        for st in range(ns):
                            last = v.tensor_copy(y4[CAP * e4:CAP * (e4 + 1), st, :].rearrange("p (a n) -> p a n", a=2),
                                                 ps[CAP * st:CAP * (st + 1), 4:6, :])
                        last.then_inc(y_kept, 1)
                    for kt in range(KT):
                        dve.wait_ge(scattered, at(scattered))
                        v.tensor_tensor(acc[:, kt, 0:T], acc[:, kt, 0:T], ps[:, 6 + kt % 2, 0:T], ALU.add)\
                            .then_inc(added, 1)
                dve.wait_ge(added, 2 + (l + 1) * KT * E // GROUP)
                for kt in range(KT):
                    for st in range(ns):
                        last = v.tensor_scalar(u[:, kt, st * S:(st + 1) * S], acc[:, kt, st * S:(st + 1) * S],
                                               mod[:, l * 48 + 40 + kt, st:st + 1], None, ALU.mult)
                link(last)
                v.scalar_tensor_tensor(u[:, :, 0:T], h[:, :, 0:T], ALPHA, u[:, :, 0:T], ALU.mult, ALU.add)\
                    .then_inc(dve_to_pe, 1)
                normalize(u, T, EPS1)

            for l in range(DEPTH):
                layer(l)

            def residual(units_each=1):
                for c in range(4):
                    g = product(units_each)
                    taken(v.scalar_tensor_tensor(t1[:, 2 * c:2 * c + 2, :], h[:, 2 * c:2 * c + 2, 0:S], ALPHA,
                                                 ps[:, g:g + 2, 0:S], ALU.mult, ALU.add))

            def memory_attention():
                for c in range(4):
                    g = product()
                    taken(v.tensor_copy(xk[:, 2 * c:2 * c + 2, :], ps[:, g:g + 2, 0:S]))
                for c in range(4):
                    g = product()
                    taken(v.tensor_copy(xv[:, :, c * UC:(c + 1) * UC], ps[:, g:g + 2, 0:S]))
                dve.wait_ge(normed, at(normed))
                for c in range(4):
                    g = product()
                    taken(v.tensor_copy(xq[:, 2 * c:2 * c + 2, :], ps[:, g:g + 2, 0:S]))
                for b in range(TB):
                    dve.wait_ge(pe_to_dve, at(pe_to_dve))
                    link(v.tensor_reduce(mx[:, 0:4], ps[:, 0:2, :].rearrange("p a (b n) -> p (a b) n", n=S),
                                              AX.X, ALU.max))
                    v.tensor_scalar(mx[:, 0:4], mx[:, 0:4], -1.0 / 16, None, ALU.mult).then_inc(dve_to_act, 1)
                    dve.wait_ge(act_to_dve, at(act_to_dve))
                    link(v.reciprocal(rec[:, 0:4], sums[:, 0:4]))
                    v.tensor_tensor(xp, xp, wide(rec[:, 0:4], [P, 4, S], 2), ALU.mult).then_inc(dve_to_pe, 1)
                    dve.wait_ge(pe_to_dve, at(pe_to_dve))
                    last = v.tensor_copy(xo[:, :, b * P:(b + 1) * P],
                                         ps[:, 4:6, :].rearrange("p a (b n) -> p (a b) n", n=P))
                last.then_inc(dve_to_pe, 1)
                residual()
                normalize(t1, S, EPS2)

            def mlp():
                dve.wait_ge(normed, at(normed))
                with count.loop(2, [(units_used, 8), (dve_step, 8)]) as turn:
                    for c in range(8):
                        g = product()
                        r = relu2[:, bass.ds(turn * 16 + 2 * c, 2), :]
                        taken(v.tensor_scalar(r, ps[:, g:g + 2, 0:S], 0.0, None, ALU.max))
                        settle()
                        v.tensor_tensor(r, r, r, ALU.mult).then_inc(squares_kept, 1)
                state["product"] += 8
                residual(4)
                normalize(t1, S, EPS2)

            def even_mixer():
                v.memset(cpad[:, :, 0:CONV_W - 1], 0.0)
                v.memset(xpad[:, :, 0:SSM_W - 1], 0.0)
                dve.wait_ge(pe_to_dve, at(pe_to_dve))
                v.tensor_scalar(dtv, ps[0:16, 7, 0:S], V("dt_bias")[0:16, :], None, ALU.add).then_inc(dve_to_pe, 1)
                settle()
                link(v.tensor_scalar(dts, dtv, -1.0, None, ALU.mult))
                v.tensor_tensor(dts, dtv, dts, ALU.max).then_inc(dve_to_act, 1)
                dve.wait_ge(act_to_dve, at(act_to_dve))
                v.tensor_scalar(acs, dtc, 1.0, None, ALU.add).then_inc(dve_to_act, 1)
                dve.wait_ge(act_to_dve, at(act_to_dve))
                link(v.tensor_scalar(acs, acs, -1.0, None, ALU.add))
                egate16 = part(20244, S, rows=16)
                link(v.tensor_scalar(egate16, acs, 0.0, None, ALU.is_equal))
                link(v.tensor_tensor(acs, acs, egate16, ALU.add))
                link(v.tensor_tensor(dts, dts, egate16, ALU.add))
                link(v.reciprocal(acs, acs))
                link(v.tensor_tensor(dts, dts, acs, ALU.mult))
                link(v.tensor_tensor(dts, dts, dtc, ALU.mult))
                link(v.scalar_tensor_tensor(dtv, dtv, 0.0, dts, ALU.max, ALU.add))
                link(v.tensor_scalar(dtc, dtv, nega, -1.0, ALU.mult, ALU.mult))
                link(v.memset(dts, 1.0))
                link(v.tensor_tensor_scan(acs, dts, dtc, 0.0, ALU.mult, ALU.add))

                conv_b, conv_w = V("conv_b"), V("conv_w")
                steps = []
                for c in range(4):
                    for w in range(CONV_W):
                        steps.append((c, w))

                def convolve(n):
                    for _ in range(n):
                        c, w = steps.pop(0)
                        for j in range(2):
                            t = 2 * c + j
                            src, k = cpad[:, t, w:w + S], conv_w[:, t * CONV_W + w:t * CONV_W + w + 1]
                            if w == 0:
                                ins = v.tensor_scalar(conv[:, t, :], src, k, conv_b[:, t:t + 1], ALU.mult, ALU.add)
                            else:
                                dve.wait_ge(dve_step, at(dve_step, 0, less=1))
                                ins = v.scalar_tensor_tensor(conv[:, t, :], src, k, conv[:, t, :], ALU.mult, ALU.add)
                            ins.then_inc(dve_step, 1)
                            count.skip(dve_step, 1)

                for c in range(4):
                    g = product(2)
                    gg = product(0)
                    dve.wait_ge(act_to_dve, at(act_to_dve))
                    sigmoid(egate)
                    v.tensor_tensor(cpad[:, 2 * c:2 * c + 2, CONV_W - 1:], egate, ps[:, g:g + 2, 0:S], ALU.mult)\
                        .then_inc(products_taken, 2)
                    settle()
                    mark().then_inc(dve_to_act, 1)
                    if c:
                        convolve(14)
                for c in range(6):
                    g = product()
                    taken(v.tensor_copy(xpad[:, 2 * c:2 * c + 2, SSM_W - 1:], ps[:, g:g + 2, 0:S]))
                    convolve(8)
                for c in range(4):
                    g = product()
                    dve.wait_ge(act_to_dve, at(act_to_dve))
                    sigmoid(egate)
                    taken(v.tensor_tensor(zed[:, 2 * c:2 * c + 2, :], egate, ps[:, g:g + 2, 0:S], ALU.mult))
                    settle()
                    if c < 3:
                        mark().then_inc(dve_to_act, 1)
                    convolve(8)
                sb_, sw = V("ssm_conv_b"), V("ssm_conv_w")
                for w in range(SSM_W):
                    for t in range(12):
                        src, k = xpad[:, t, w:w + S], sw[:, t * SSM_W + w:t * SSM_W + w + 1]
                        if w == 0:
                            ins = v.tensor_scalar(xbc[:, t, :], src, k, sb_[:, t:t + 1], ALU.mult, ALU.add)
                        else:
                            dve.wait_ge(dve_step, at(dve_step, 0, less=11))
                            ins = v.scalar_tensor_tensor(xbc[:, t, :], src, k, xbc[:, t, :], ALU.mult, ALU.add)
                        ins.then_inc(dve_step, 1)
                        count.skip(dve_step, 1)
                dve.wait_ge(dve_step, at(dve_step, 0))
                mark().then_inc(dve_to_act, 1)
                convolve(len(steps))
                dve.wait_ge(dve_step, at(dve_step, 0))
                mark().then_inc(dve_to_pe, 1)
                dve.wait_ge(act_to_dve, at(act_to_dve))
                sigmoid(xneg)
                link(v.tensor_tensor(xbc[:, :, :], xbc[:, :, :], xneg, ALU.mult))
                normalize(conv, S, EPS2)
                dve.wait_ge(act_to_dve, at(act_to_dve))
                sigmoid(conv)
                v.tensor_tensor(mixin[:, 0:KT, :], mixin[:, 0:KT, :], conv, ALU.mult)
                v.tensor_copy(sel, wide(ident[0:16, 0:16], [16, 16, P], 2))
                dve.wait_ge(pe_to_dve, at(pe_to_dve))
                v.tensor_copy(dtT, ps[:, 5, 0:32])
                link(v.tensor_scalar(acsT, ps[:, 5, 32:64], -1.0, None, ALU.mult))
                mark().then_inc(dve_to_pe, 1)
                dve.wait_ge(pe_to_dve, at(pe_to_dve))
                for b in range(TB):
                    v.tensor_tensor(xdt[:, b, :].rearrange("p (h n) -> p h n", n=HD),
                                    ps[:, 2 * b:2 * b + 2, :].rearrange("p a (h n) -> p (a h) n", n=HD),
                                    wide(dtT[:, b * 16:(b + 1) * 16], [P, 16, HD], 2), ALU.mult)
                dve.wait_ge(pe_to_dve, at(pe_to_dve))
                v.tensor_copy(cb[:, :, :], ps[:, 4:6, 0:384]).then_inc(dve_to_pe, 1)

                def gate_pair(t):
                    dve.wait_ge(head_done, at(head_done, 2))
                    y = mixin[:, KT + t, :]
                    v.scalar_tensor_tensor(y, xbc[:, t, :], V("d_skip")[:, t:t + 1], ps[:, 2 + t % 2, 0:S],
                                           ALU.mult, ALU.add).then_inc(y_tile_kept, 1)
                    settle()
                    return v.tensor_tensor(y, y, zed[:, t, :], ALU.mult)

                settle()
                for n in range(SSM_HEADS):
                    dve.wait_ge(decay_ready, at(decay_ready))
                    if n >= 2:
                        dve.wait_ge(head_done, n - 1)
                    v.tensor_tensor(mask[n % 2], decay[n % 2], cb[:, n // 8, :], ALU.mult).then_inc(dve_to_pe, 1)
                    if n >= 2 and n % 2 == 0:
                        gate_pair(n // 2 - 1)
                gate_pair(KT - 1).then_inc(dve_to_act, 1)
                dve.wait_ge(pe_to_dve, at(pe_to_dve))
                r2 = small[:, 0:512].rearrange("p (g n) -> p g n", g=2)
                v.tensor_scalar(r2, ps[:, 6:8, 0:S], 1.0 / 512, EPS2, ALU.mult, ALU.add).then_inc(variances_ready, 1)
                dve.wait_ge(inverses_ready, at(inverses_ready))
                for t in range(KT):
                    last = v.scalar_tensor_tensor(mixin[:, KT + t, :], mixin[:, KT + t, :],
                                                  V("ssm_norm_g")[:, t:t + 1], r2[:, t // 4, :], ALU.mult, ALU.mult)
                last.then_inc(dve_to_pe, 1)
                residual(2)
                normalize(t1, S, EPS2)

            def odd_mixer():
                dve.wait_ge(normed, at(normed))
                for q in (gq, gk):
                    for c in range(2):
                        g = product()
                        taken(v.tensor_copy(q[:, 2 * c:2 * c + 2, :], ps[:, g:g + 2, 0:S]))
                for c in range(4):
                    g = product()
                    taken(v.tensor_copy(gv[:, :, c * UC:(c + 1) * UC], ps[:, g:g + 2, 0:S]))
                for c in range(4):
                    g = product()
                    dve.wait_ge(act_to_dve, at(act_to_dve))
                    sigmoid(gmid[:, 0:2, :])
                    taken(v.tensor_tensor(gout[:, 2 * c:2 * c + 2, :], gmid[:, 0:2, :], ps[:, g:g + 2, 0:S], ALU.mult))
                    settle()
                    if c < 3:
                        mark().then_inc(dve_to_act, 1)
                dve.wait_ge(pe_to_dve, at(pe_to_dve))
                v.tensor_copy(low, ps[0:16, 0, 0:S]).then_inc(dve_to_pe, 1)
                dve.wait_ge(pe_to_dve, at(pe_to_dve))
                link(v.tensor_tensor(logg, ps[:, 2:4, :].rearrange("p a (b n) -> p (a b) n", n=S),
                                          wide(V("b_gate"), [P, 4, S], 2), ALU.add))
                link(v.tensor_scalar(en, logg, -1.0, None, ALU.mult))
                v.tensor_tensor(en, logg, en, ALU.max).then_inc(dve_to_act, 1)
                dve.wait_ge(act_to_dve, at(act_to_dve))
                link(v.scalar_tensor_tensor(logg, logg, 0.0, en, ALU.min, ALU.subtract))
                link(v.tensor_scalar(logg, logg, 1.0 / GLA_TAU, None, ALU.mult))
                for hd in range(4):
                    last = v.tensor_tensor_scan(eb[:, hd, :], C("carry"), logg[:, hd, :], 0.0, ALU.mult, ALU.add)
                link(last)
                for hd in range(4):
                    x = eb[:, hd, :].rearrange("p (c n) -> p c n", n=GLA_CHUNK)
                    last = v.tensor_tensor(gmid[:, hd, :].rearrange("p (c n) -> p c n", n=GLA_CHUNK),
                                           x[:, :, GLA_CHUNK - 1:].broadcast_to([P, 4, GLA_CHUNK]), x, ALU.subtract)
                last.then_inc(dve_to_act, 1)
                dve.wait_ge(act_to_dve, at(act_to_dve))
                v.scalar_tensor_tensor(qt, qt, float(P) ** -0.5, gq, ALU.mult, ALU.mult)
                v.tensor_tensor(ktl, ktl, gk, ALU.mult)
                v.tensor_tensor(kend, kend, gk, ALU.mult).then_inc(dve_to_pe, 1)
                link(v.memset(att, 0.0))
                dve.wait_ge(pe_to_dve, at(pe_to_dve))
                keep = wide(C("chunked").bitcast(U32), [P, 4, P])
                v.copy_predicated(att[:, 0:4, :], keep, ps[:, 4, :].rearrange("p (h n) -> p h n", n=P))
                v.copy_predicated(att[:, 4:8, :], keep, ps[:, 5, :].rearrange("p (h n) -> p h n", n=P))\
                    .then_inc(dve_to_pe, 1)
                for c in range(3):
                    for hd in range(4):
                        n = c * 4 + hd
                        dve.wait_ge(pe_to_dve, at(pe_to_dve))
                        kv, new = ps[:, 6 + n % 2, 0:S], hist[:, hd, c * S:(c + 1) * S]
                        if c == 0:
                            ins = v.tensor_copy(new, kv)
                        else:
                            ins = v.scalar_tensor_tensor(new, hist[:, hd, (c - 1) * S:c * S], gend[:, hd, c:c + 1], kv,
                                                         ALU.mult, ALU.add)
                        ins.then_inc(dve_to_pe, 1)
                        if hd == 3:
                            settle()
                dve.wait_ge(pe_to_dve, at(pe_to_dve))
                v.tensor_copy(go[:, :, :], ps[:, 0:4, :].rearrange("p a (b n) -> p (a b) n", n=S)).then_inc(dve_to_act, 1)
                dve.wait_ge(pe_to_dve, at(pe_to_dve))
                r4 = small[:, 0:1024].rearrange("p (h n) -> p h n", h=4)
                v.tensor_scalar(r4, ps[:, 4:6, :].rearrange("p a (b n) -> p (a b) n", n=S), 1.0 / S, EPS2,
                                ALU.mult, ALU.add).then_inc(variances_ready, 1)
                dve.wait_ge(inverses_ready, at(inverses_ready))
                for t in range(KT):
                    last = v.scalar_tensor_tensor(go[:, t, :], go[:, t, :], V("head_norm_g")[:, t % 2:t % 2 + 1],
                                                  r4[:, t // 2, :], ALU.mult, ALU.mult)
                link(last)
                v.tensor_tensor(go, go, gout, ALU.mult).then_inc(dve_to_pe, 1)
                residual()
                normalize(t1, S, EPS2)

            dve.wait_ge(normed, at(normed))
            even_mixer()
            for l in range(DEPTH):
                if l:
                    odd_mixer()
                memory_attention()
                mlp()


def kernel(**inputs):
    import concourse.bacc as bacc
    from concourse.bass_utils import run_bass_kernel_spmd

    i = {k: np.asarray(v) for k, v in inputs.items()}
    arrays = {
        "tokens": feature_major(np.concatenate([i["x"][0], i["ctx"][0]], 0)),
        "memory": feature_major(i["mem_2"][0]),
        "vectors": vectors(i),
        "constants": constants(),
        "neighbours": neighbour_rows(i["na_rpb"]),
        "units": weight_stream(i),
    }
    arrays = {k: np.ascontiguousarray(v) for k, v in arrays.items()}
    nc = bacc.Bacc("TRN2", target_bir_lowering=False, num_devices=1)
    ap = {k: nc.dram_tensor(k, v.shape, F32, kind="ExternalInput").ap() for k, v in arrays.items()}
    out = nc.dram_tensor("out", (P, KT, S), F32, kind="ExternalOutput").ap()
    build(nc, ap, out)
    got = run_bass_kernel_spmd(nc, [arrays], core_ids=[0]).results[0]["out"]
    return np.ascontiguousarray(np.asarray(got).transpose(2, 1, 0).reshape(1, S, D))
```

```python
from contextlib import ExitStack

import numpy as np
import concourse.bass as bass
from concourse import mybir

F32 = mybir.dt.float32
U32 = mybir.dt.uint32
ALU = mybir.AluOpType
ACT = mybir.ActivationFunctionType
AX = mybir.AxisListType

P = 128
D = 1024
KT = D // P
S = 256
TB = S // P
UNIT = 2048
UC = UNIT // KT
RING = 8
DEPTH = 2
HD = 64
E = 16
CAP = 32
NEG = -1e30
ALPHA = float((2 * DEPTH) ** 0.25)
EPS1, EPS2 = 1e-6, 1e-5
CONV_W, SSM_W = 31, 4
POOL_PAIRS = 1
SSM_HEADS = 16
GLA_CHUNK, GLA_TAU = 64, 16.0
EXPERT_UNITS = 12
GROUP = 4
GROUP_UNITS = GROUP * EXPERT_UNITS


def columns(widths):
    at, out = 0, {}
    for name, width in widths:
        out[name] = (at, width)
        at += width
    return out, at


VEC, NVEC = columns([
    ("c", 2 * KT), ("b_mod", DEPTH * 48), ("ln1_g", DEPTH * KT), ("ln1_b", DEPTH * KT),
    ("ln2_g", DEPTH * KT), ("ln2_b", DEPTH * KT), ("ln_g", DEPTH * 3 * KT), ("ln_b", DEPTH * 3 * KT),
    ("conv_b", KT), ("conv_ln_g", KT), ("conv_ln_b", KT), ("ssm_conv_b", 12), ("ssm_norm_g", KT),
    ("b_gate", 4), ("head_norm_g", 2), ("conv_w", KT * CONV_W), ("ssm_conv_w", 12 * SSM_W),
    ("qk_gain", DEPTH * 2), ("sink", DEPTH * 4), ("d_skip", KT), ("dt_bias", 1), ("a_log", 1),
    ("w_router", DEPTH * KT * E), ("w_dt", KT * SSM_HEADS), ("w_low", KT * 16), ("w_gate2", 512)])

CON, NCON = columns([
    ("ident", P), ("ones", P), ("headones", P), ("rot", P), ("rev", P), ("cos", S), ("sin", S),
    ("dft", 2 * P), ("seqcos", 2 * S), ("seqsin", 2 * S), ("window", TB * S), ("near", 64),
    ("causal", P), ("iota", CAP), ("chunked", P), ("carry", S)])


def constants():
    out = np.zeros((P, NCON), np.float32)

    def put(name, value):
        at, width = CON[name]
        out[:, at:at + width] = np.asarray(value, np.float64).reshape(P, width)

    p = np.arange(P)
    put("ident", np.eye(P))
    put("ones", np.ones((P, P)))
    put("headones", p[:, None] // HD == p[None] // HD)
    half, quarter = HD // 2, HD // 4
    rot = np.zeros((P, P))
    for m in range(P):
        if m % half < quarter:
            rot[m + quarter, m] = -1.0
        else:
            rot[m - quarter, m] = 1.0
    put("rot", rot)
    put("rev", np.eye(P)[::-1])
    inv = (10000.0 ** (-np.arange(0, half, 2, dtype=np.float32) / half)).astype(np.float32)
    t = np.arange(S)
    pos = np.where((p % HD < half)[:, None], (t // 64)[None], (t % 64)[None]).astype(np.float32)
    angle = (pos * inv[p % quarter][:, None]).astype(np.float32)
    put("cos", np.cos(angle))
    put("sin", np.sin(angle))
    same = (p[:, None] // 64 == p[None] // 64)
    wa = 2 * np.pi * np.outer(p % 64, p % 64) / 64
    put("dft", np.concatenate([np.cos(wa) * same, np.sin(wa) * same], 1))
    sa = 2 * np.pi * np.outer(t, t) / S
    fold = lambda m: m.reshape(TB, P, S).transpose(1, 0, 2)
    put("seqcos", fold(np.cos(sa) / 128.0))
    put("seqsin", fold(-np.sin(sa) / 128.0))
    put("window", fold(np.where(np.abs(t[:, None] - t[None]) <= 128, 0.0, NEG)))
    col = 63 - p % 64
    first = np.clip(col - 8, 0, 48)[:, None]
    kc = np.arange(64)[None]
    put("near", np.where((kc >= first) & (kc < first + 16), 0.0, NEG))
    put("causal", np.where(p[None] >= p[:, None], 0.0, NEG))
    put("iota", np.broadcast_to(np.arange(CAP), (P, CAP)))
    put("chunked", (p[None] >= p[:, None]) & (p[:, None] // GLA_CHUNK == p[None] // GLA_CHUNK))
    put("carry", np.broadcast_to(t % GLA_CHUNK != 0, (P, S)))
    return out


def units_of(w):
    k, n = w.shape
    return w.reshape(k // D, KT, P, n // UC, UC).transpose(3, 0, 2, 1, 4).reshape(-1, P, UNIT)


def weight_stream(i):
    w_mod = np.concatenate([units_of(i["w_mod"][l]) for l in range(DEPTH)], 0).reshape(-1, 8, P, UNIT)
    parts = [w_mod[0]]
    for l in range(DEPTH):
        w_in = units_of(i["w_in"][l])
        parts += [w_in[:3], w_mod[1], w_in[3:7]] if l == 0 else [w_in[:7]]
        for b in range(4):
            if l == 0:
                parts.append(w_mod[2 + b])
            parts.append(w_in[7 + 4 * b:11 + 4 * b])
            parts.append(i["w_branch"][l, b].reshape(1, 2, P, D).transpose(0, 2, 1, 3).reshape(1, P, UNIT))
        parts.append(units_of(i["w_out"][l]))
        for e in range(E):
            parts += [units_of(i["w_gate"][l, e]), units_of(i["w_up"][l, e])]
            parts.append(units_of(i["w_down"][l, e]))
    even = units_of(i["even_w_in_2"][0][:, :4608])
    for c in range(4):
        parts += [even[c:c + 1], even[4 + c:5 + c]]
    parts += [even[12:], even[8:12], units_of(i["even_w_out_2"][0])]
    for l in range(DEPTH):
        if l == 1:
            odd = units_of(i["odd_w_in_2"][0][:, :3072])
            parts += [odd, units_of(i["odd_w_out_2"][0])]
        parts += [units_of(i[f"xa_w_{n}_2"][l]) for n in "kvqo"]
        parts += [units_of(i["mlp_w1_2"][l]), units_of(i["mlp_w2_2"][l])]
    return np.concatenate(parts, 0)


def vectors(i):
    out = np.zeros((P, NVEC), np.float32)

    def put(name, value):
        at, width = VEC[name]
        value = np.asarray(value).reshape(-1, width)
        out[:value.shape[0], at:at + width] = value

    tiles = lambda v: v.reshape(-1, P).T
    put("c", np.stack([i["c"][0], i["c_ctx"]]).reshape(2, KT, P).transpose(2, 1, 0))
    for name, key in (("b_mod", "b_mod"), ("ln1_g", "ln1_g"), ("ln1_b", "ln1_b"), ("ln2_g", "ln2_g"),
                      ("ln2_b", "ln2_b"), ("ln_g", "ln_g_2"), ("ln_b", "ln_b_2"), ("conv_b", "even_conv_b_2"),
                      ("conv_ln_g", "even_conv_ln_g_2"), ("conv_ln_b", "even_conv_ln_b_2"),
                      ("ssm_conv_b", "even_ssm_conv_b_2"), ("ssm_norm_g", "even_ssm_norm_g_2"),
                      ("b_gate", "odd_b_gate_2"), ("head_norm_g", "odd_head_norm_g_2")):
        put(name, tiles(i[key]))
    put("conv_w", i["even_conv_w_2"][0].reshape(CONV_W, KT, P).transpose(2, 1, 0))
    put("ssm_conv_w", i["even_ssm_conv_w_2"][0].reshape(SSM_W, 12, P).transpose(2, 1, 0))
    put("qk_gain", np.tile(i["qk_gain"].reshape(DEPTH * 2, HD).T, (2, 1)))
    put("sink", np.broadcast_to(i["sink_logit"].reshape(1, -1), (P, DEPTH * 4)))
    put("d_skip", np.repeat(i["even_d_skip_2"][0].reshape(KT, 2), HD, 1).T)
    put("dt_bias", i["even_dt_bias_2"][0].reshape(-1, 1))
    put("a_log", i["even_a_log_2"][0].reshape(-1, 1))
    put("w_router", i["w_router"].reshape(DEPTH, KT, P, E).transpose(2, 0, 1, 3))
    put("w_dt", i["even_w_in_2"][0][:, 4608:].reshape(KT, P, SSM_HEADS).transpose(1, 0, 2))
    put("w_low", i["odd_w_in_2"][0][:, 3072:].reshape(KT, P, 16).transpose(1, 0, 2))
    put("w_gate2", i["odd_w_gate2_2"][0])
    return out


def neighbour_rows(rpb):
    out = np.zeros(rpb.shape[:2] + (7, P), np.float32)
    out[..., 48:79] = rpb[:, :, 4:11]
    return out


def feature_major(x):
    return x.reshape(-1, KT, P).transpose(2, 1, 0)


class Count:

    def __init__(self, engine):
        self.engine, self.n, self.turn, self.per = engine, {}, None, {}

    def at(self, sem, more=1, less=0):
        self.skip(sem, more)
        value = self.n[sem.name] - less
        assert value > 0, sem.name
        per = self.per.get(sem.name, 0)
        return value if self.turn is None or not per else self.turn * per + value

    def skip(self, sem, more):
        self.n[sem.name] = self.n.get(sem.name, 0) + more

    def loop(self, times, per):
        return _Loop(self, times, per)


class _Loop:
    def __init__(self, count, times, per):
        self.count, self.times, self.per = count, times, {s.name: k for s, k in per}

    def __enter__(self):
        c = self.count
        self.fori = c.engine.Fori(0, self.times)
        self.start = dict(c.n)
        c.turn, c.per = self.fori.__enter__(), self.per
        return c.turn

    def __exit__(self, *what):
        done = self.fori.__exit__(*what)
        c = self.count
        for name, value in c.n.items():
            rise = value - self.start.get(name, 0)
            assert rise == self.per.get(name, 0), (name, rise)
            c.n[name] = self.start.get(name, 0) + rise * self.times
        c.turn, c.per = None, {}
        return done


def build(nc, ap, out):
    units = ap["units"]
    n_units = units.shape[0]
    with ExitStack() as ctx:
        def sb(name, *shape):
            return ctx.enter_context(nc.sbuf_tensor(name, [P, *shape], F32))

        def sem(name):
            return ctx.enter_context(nc.semaphore(name))

        ring = sb("ring", RING, UNIT)
        vec = sb("vec", NVEC)
        con = sb("con", NCON)
        h = sb("h", KT, 2 * S)
        u = sb("u", KT, 2 * S)
        mod = sb("mod", DEPTH * 48, 2)
        small = sb("small", 1216)
        arena = sb("arena", 21504)
        cond = sb("cond", KT * 32)
        ps = ctx.enter_context(nc.psum_tensor("ps", [P, 8, 512], F32))

        def uflat(x):
            return x[:, :, :].rearrange("p k n -> p (k n)")

        def V(name):
            at, width = VEC[name]
            return vec[:, at:at + width]

        def C(name, rows=P):
            at, width = CON[name]
            return con[0:rows, at:at + width]

        def part(at, *shape, of=arena, rows=P):
            n = int(np.prod(shape))
            v = of[0:rows, at:at + n]
            if len(shape) == 2:
                v = v.rearrange("p (a b) -> p a b", b=shape[1])
            if len(shape) == 3:
                v = v.rearrange("p (a b c) -> p a b c", b=shape[1], c=shape[2])
            if len(shape) == 4:
                v = v.rearrange("p (a b c d) -> p a b c d", b=shape[1], c=shape[2], d=shape[3])
            return v

        ident, ones = C("ident"), C("ones")

        cs = cond[:, :].rearrange("p (k s) -> p k s", s=32)
        mrow = [part(20992, UC), part(20992 + UC, UC)]
        qk = part(0, 12, 512)
        val = part(6144, 4, 384)
        four = part(7680, 2, 512)
        prob = [part(8704, 4, 512), part(10752, 4, 512)]
        probT = part(12800, 4, 512)
        bias = part(14848, 8, S)
        branch = part(16896, 8, 512)
        fmid = part(12800, 2, 2 * S)
        nsq = part(8704, 4, 512)
        rtmp = part(10752, 8, S)
        merged = part(0, KT, 512)
        gate = part(4096, KT, 512)
        gated = [part(12800, 2, 512), part(13824, 2, 512)]
        sq1 = part(8704, KT, 512)
        xs = part(0, KT, E, 64)
        wsel = part(8192, 4, 512)
        acc = part(10240, KT, 512)
        y4 = part(14336, 2, D)
        htok = part(14336, 4, D)
        hid = part(18432, KT, 64)
        xcur = part(18944, KT, 64)
        sg = part(19456, 2, UC)
        hv = part(19968, 2, UC)
        pick = part(10240, 4, 512)
        wpick = part(12288, 4, 512)
        logit = part(19712, 4, E)
        aff = part(19776, TB, 2, E)
        rowa, rowb, rowc = part(19840, S), part(20096, S), part(20352, S)
        rank = part(20608, TB, 2, E)
        top8 = part(20672, 4, 8)
        onesrow = part(20704, S)
        sq2 = part(0, KT, 512)

        cpad = part(0, KT, CONV_W - 1 + S)
        conv = part(2288, KT, S)
        zed = part(4336, KT, S)
        tap = part(20480, 4, S)
        xpad = part(6384, 12, SSM_W - 1 + S)
        xsig = part(6384, 12, S)
        sig = part(19476, 2, S)
        xbc = part(9492, 12, S)
        mixin = part(12564, 2 * KT, S)
        xdt = part(16660, TB, D)
        cb = part(18708, 2, 384)
        decay = [part(19476, 384), part(19860, 384)]
        mask = [part(20244, 384), part(20628, 384)]
        sel = part(0, SSM_HEADS, P, rows=16)
        dtv, acs = small[0:16, 768:1024], small[0:16, 256:512]
        dts, dtc = small[0:16, 512:768], small[0:16, 0:256]
        dtT, acsT = small[:, 1056:1088], small[:, 1088:1120]
        nega = small[0:16, 1120:1121]
        t1, t2 = part(0, KT, S, of=uflat(u)), part(KT * S, KT, S, of=uflat(u))
        mem = h[:, :, S:]
        xk, xq = part(0, KT, S), part(2048, KT, S)
        xv = part(4096, TB, D)
        xp = part(6144, 4, S)
        xpT = part(7168, 8, P)
        xo = part(8192, KT, S)
        relu2 = part(0, 4 * KT, S)
        gq, gk = part(0, 4, S), part(1024, 4, S)
        gv = part(2048, TB, D)
        gout = part(4096, KT, S)
        logg, eb, en = part(6144, 4, S), part(7168, 4, S), part(8192, 4, S)
        qt, ktl, kend = part(9216, 4, S), part(10240, 4, S), part(11264, 4, S)
        kendT = part(12288, TB * 4, P)
        att = part(13312, TB * 4, P)
        hist = part(14336, 4, 3 * S)
        go = part(17408, KT, S)
        low = part(19456, S, rows=16)
        gmid = part(19712, 4, S)
        gend = part(20736, 4, 4)

        stat = small[:, 0:512]
        stat2 = small[:, 512:1024]
        tick = small[:, 1160:1192]
        es, nsink = small[:, 1140:1148], small[:, 1148:1156]
        mx, sums, rec = small[:, 1024:1032], small[:, 1032:1040], small[:, 1040:1048]

        vectors_loaded = sem("vectors_loaded")
        inputs_loaded = sem("inputs_loaded")
        bias_loaded = sem("bias_loaded")
        memory_loaded = sem("memory_loaded")
        loaded = [sem(f"unit_loaded_{s}") for s in range(RING)]
        units_used = sem("units_used")
        products_taken = sem("products_taken")
        dve_step, act_step = sem("dve_step"), sem("act_step")
        pool_step = sem("pool_step")
        pair_gated = sem("pair_gated")
        dve_to_pe = sem("operands_ready")
        dve_to_act = sem("arguments_ready")
        act_to_dve = sem("functions_ready")
        act_to_pe = sem("act_operands_ready")
        pe_to_dve = sem("sums_ready")
        pe_to_act = sem("blocks_ready")
        residual_ready = sem("residual_ready")
        centred = sem("centred")
        squares_ready = sem("squares_ready")
        scaled = sem("scaled")
        normed = sem("normed")
        variances_ready = sem("variances_ready")
        inverses_ready = sem("inverses_ready")
        decay_ready = sem("decay_ready")
        head_done = sem("head_done")
        y_tile_kept = sem("y_tile_kept")
        squares_kept = sem("squares_kept")
        scores_ready = sem("scores_ready")
        exps_ready = sem("exps_ready")
        probs_ready = sem("probs_ready")
        turned = sem("probs_turned")
        turned_kept = sem("turned_kept")
        mixed = sem("values_mixed")
        mixed_kept = sem("mixed_kept")
        hidden_ready = sem("hidden_ready")
        y_kept = sem("outputs_kept")
        scattered = sem("scattered")
        added = sem("scattered_added")
        xcur_ready = sem("expert_input_ready")
        stored = sem("stored")

        block = ctx.enter_context(nc.Block())

        @block.sync
        def _(sp):
            sp.dma_start(vec[:, :], ap["vectors"]).then_inc(vectors_loaded, 16)
            sp.dma_start(con[:, 0:P], ap["constants"][:, 0:P]).then_inc(vectors_loaded, 16)
            for s in range(RING):
                sp.dma_start(ring[:, s, :], units[s]).then_inc(loaded[s], 16)
            sp.dma_start(h[:, :, :], ap["tokens"]).then_inc(inputs_loaded, 16)
            sp.dma_start(con[:, P:], ap["constants"][:, P:]).then_inc(inputs_loaded, 16)
            turns = n_units // RING - 1
            assert n_units % RING == 0
            with sp.Fori(0, turns) as i:
                for s in range(RING):
                    sp.wait_ge(units_used, i * RING + s + 1)
                    sp.dma_start(ring[:, s, :], units[bass.ds(i * RING + RING + s, 1)]
                                 .rearrange("a p n -> (a p) n")).then_inc(loaded[s], 16)
            sp.wait_ge(normed, 2 * DEPTH + 3 * DEPTH)
            sp.dma_start(out, h[:, :, 0:S]).then_inc(stored, 16)
            sp.wait_ge(stored, 16)

        @block.gpsimd
        def _(pool):
            for l in range(DEPTH):
                if l:
                    pool.wait_ge(normed, 2)
                for hd in range(4):
                    for b in range(TB):
                        for r in range(2):
                            at = ap["neighbours"][l, hd, 2 - 2 * b + r, 0:1]
                            src = bass.AP(at.tensor, at.offset, [[1, 64], [P, 4], [1, 64]])
                            pool.dma_start(bias[64 * r:64 * (r + 1), hd * TB + b, :]
                                           .rearrange("p (r c) -> p r c", c=64), src).then_inc(bias_loaded, 16)
            pool.wait_ge(normed, 4)
            pool.dma_start(h[:, :, S:], ap["memory"]).then_inc(memory_loaded, 16)
            conv_b, conv_w = V("conv_b"), V("conv_w")
            done = 0
            for c in range(POOL_PAIRS):
                pool.wait_ge(pair_gated, c + 1)
                for w in range(CONV_W):
                    for add in ((False, True) if w else (False,)):
                        for t in (2 * c, 2 * c + 1):
                            src, k = cpad[:, t, w:w + S], conv_w[:, t * CONV_W + w:t * CONV_W + w + 1]
                            if done >= 2:
                                pool.wait_ge(pool_step, done - 1)
                            if w == 0:
                                ins = nc.gpsimd.tensor_scalar(conv[:, t, :], src, k, conv_b[:, t:t + 1], ALU.mult, ALU.add)
                            elif add:
                                ins = nc.gpsimd.tensor_tensor(conv[:, t, :], conv[:, t, :], tap[:, w % 2 * 2 + t % 2, :],
                                                              ALU.add)
                            else:
                                ins = nc.gpsimd.tensor_scalar(tap[:, w % 2 * 2 + t % 2, :], src, k, None, ALU.mult)
                            ins.then_inc(pool_step, 1)
                            done += 1

        @block.tensor
        def _(pe):
            count = Count(pe)
            at = count.at
            state = {"unit": 0, "product": 0}

            def unit():
                n = state["unit"]
                pe_wait_unit(n)
                state["unit"] += 1
                return ring[:, n % RING, :].rearrange("p (k c) -> p k c", c=UC)

            def pe_wait_unit(n):
                value = 16 * (n // RING + 1)
                if count.turn is None:
                    pe.wait_ge(loaded[n % RING], value)
                else:
                    pe.wait_ge(loaded[n % RING], count.turn * (16 * state["body"] // RING) + value)

            def loop(times, body, per):
                assert body % RING == 0
                state["body"] = body
                return count.loop(times, per)

            def after_loop(times, body, products=0):
                state["unit"] += (times - 1) * body
                state["product"] += (times - 1) * products

            def claim():
                n = state["product"]
                state["product"] += 1
                if n >= 4:
                    pe.wait_ge(products_taken, at(products_taken))
                return 2 * (n % 4)

            def drained():
                n = state["product"]
                pe.wait_ge(products_taken, n)

            def project(rhs, n, tiles=2, groups=1, used=True):
                g = claim()
                for q in range(groups):
                    w = unit()
                    for j in range(tiles):
                        for kt in range(KT):
                            last = nc.tensor.matmul(ps[:, g + j, 0:n], w[:, kt, j * P:(j + 1) * P],
                                                    rhs[:, q * KT + kt, 0:n], start=(q == 0 and kt == 0),
                                                    stop=(q == groups - 1 and kt == KT - 1))
                    last.then_inc(units_used, 1)

            def sums(x, n, c, g, ready, value):
                pe.wait_ge(ready, value)
                for kt in (2 * c, 2 * c + 1):
                    last = nc.tensor.matmul(ps[:, g, 0:n], ones, x[:, kt, 0:n], start=(kt == 0), stop=(kt == KT - 1))
                if c == KT // 2 - 1:
                    last.then_inc(pe_to_dve, 1)

            def squares(sq, n, g):
                for kt in range(KT):
                    if kt % 2 == 0:
                        pe.wait_ge(squares_ready, at(squares_ready))
                    last = nc.tensor.matmul(ps[:, g + 1, 0:n], ones, sq[:, kt, 0:n],
                                            start=(kt == 0), stop=(kt == KT - 1))
                last.then_inc(pe_to_dve, 1)

            def normalize(x, sq, n):
                g = claim()
                for c in range(KT // 2):
                    sums(x, n, c, g, residual_ready, at(residual_ready))
                squares(sq, n, g)

            def project_and_normalize(rhs, x, sq, n, groups=1, taken=True, between=None):
                first = state["product"]
                g = 2 * (first % 4)
                for c in range(KT // 2):
                    project(rhs, n, groups=groups)
                    if c:
                        sums(x, n, c - 1, g, *((products_taken, first + c) if taken
                                               else (residual_ready, at(residual_ready))))
                sums(x, n, KT // 2 - 1, g, *((products_taken, first + KT // 2) if taken
                                             else (residual_ready, at(residual_ready))))
                state["product"] += 1
                count.skip(products_taken, 1)
                if between:
                    between()
                squares(sq, n, g)

            def modulation():
                g = claim()
                for n in range(2):
                    w = [unit() for _ in range(4)]
                    for kt in range(KT):
                        for q in range(4):
                            last = nc.tensor.matmul(ps[32 * q:32 * (q + 1), g + n, 0:UC], cs[:, kt, :], w[q][:, kt, :],
                                                    start=(kt == 0), stop=(kt == KT - 1))
                    last.then_inc(units_used, 4)
                g = claim()
                pe.wait_ge(dve_to_pe, at(dve_to_pe))
                for t in range(2):
                    for n in range(2):
                        last = nc.tensor.transpose(ps[:, g, t * UC + n * P:t * UC + (n + 1) * P],
                                                   mrow[n][:, t * P:(t + 1) * P], ident)
                last.then_inc(pe_to_dve, 1)

            pe.wait_ge(dve_to_pe, at(dve_to_pe))
            modulation()

            def attend(l, T):
                batches = [(k, b) for k in range(3) for b in range(T // P)]

                def scores(n):
                    k, b = batches[n]
                    lat = b < TB
                    lo = 0 if lat else S
                    if n >= 1:
                        pe.wait_ge(exps_ready, at(exps_ready))
                    for hd in range(4):
                        t, s = hd // 2, hd % 2 * HD
                        extra = lat and k > 0
                        last = nc.tensor.matmul(ps[:, hd, lo:512], qk[s:s + HD, 4 * k + t, b * P:(b + 1) * P],
                                                qk[s:s + HD, 4 * k + 2 + t, lo:512], start=True, stop=not extra)
                        if lat and k == 1:
                            last = nc.tensor.matmul(ps[:, hd, 0:S], ident, C("window")[:, b * S:(b + 1) * S],
                                                    start=False, stop=True)
                        if lat and k == 2:
                            last = nc.tensor.matmul(ps[:, hd, 0:S], C("rev"), bias[:, hd * TB + b, :],
                                                    start=False, stop=True)
                    last.then_inc(scores_ready, 1)

                pe.wait_ge(dve_to_pe, at(dve_to_pe))
                scores(0)
                for n, (k, b) in enumerate(batches):
                    if n + 1 < len(batches):
                        scores(n + 1)
                    else:
                        pe.wait_ge(exps_ready, at(exps_ready))
                    first = 0 if b < TB else TB
                    pe.wait_ge(probs_ready, at(probs_ready))
                    for hd in range(4):
                        if state["turned"] >= 2:
                            pe.wait_ge(turned_kept, at(turned_kept))
                        for kb in range(first, 4):
                            last = nc.tensor.transpose(ps[:, 4 + hd % 2, kb * P:(kb + 1) * P],
                                                       prob[n % 2][:, hd, kb * P:(kb + 1) * P], ident)
                        last.then_inc(turned, 1)
                        state["turned"] += 1
                    if state["mixed"] >= 2:
                        pe.wait_ge(mixed_kept, at(mixed_kept))
                    m = 6 + state["mixed"] % 2
                    for hd in range(4):
                        t, s = hd // 2, hd % 2 * HD
                        pe.wait_ge(turned_kept, state["turned"] - 3 + hd)
                        for kb in range(first, 4):
                            last = nc.tensor.matmul(ps[s:s + HD, m, t * P:(t + 1) * P],
                                                    val[:, kb, k * P + t * HD:k * P + (t + 1) * HD],
                                                    probT[:, hd, kb * P:(kb + 1) * P],
                                                    start=(kb == first), stop=(kb == 3))
                    last.then_inc(mixed, 1)
                    state["mixed"] += 1

            state["turned"] = state["mixed"] = 0

            def layer(l):
                T = 512 if l == 0 else S
                nb = T // P
                pe.wait_ge(dve_to_pe, at(dve_to_pe))
                for kind in range(3):
                    if l == 0 and kind == 1:
                        modulation()
                    project(u, T)
                    w = unit()
                    g = claim()
                    for kt in range(KT):
                        nc.tensor.matmul(ps[:, g, :], w[:, kt, 0:P], u[:, kt, :],
                                         start=(kt == 0), stop=(kt == KT - 1))
                    for b in range(4):
                        for kt in range(KT):
                            last = nc.tensor.matmul(ps[:, g + 1, b * P:(b + 1) * P], u[:, kt, b * P:(b + 1) * P],
                                                    w[:, kt, P:2 * P], start=(kt == 0), stop=(kt == KT - 1))
                    last.then_inc(units_used, 1)
                    if kind == 0:
                        project(u, T)
                drained()
                pe.wait_ge(act_to_pe, at(act_to_pe))
                for t in range(4):
                    n = T if t < 2 else 512
                    last = nc.tensor.matmul(ps[:, t, 0:n], C("headones"), nsq[:, t, 0:n], start=True, stop=True)
                last.then_inc(pe_to_dve, 1)
                pe.wait_ge(dve_to_pe, at(dve_to_pe))
                for t in range(8):
                    last = nc.tensor.matmul(ps[:, 4 + t // 2, t % 2 * S:(t % 2 + 1) * S], C("rot"),
                                            qk[:, t, 0:S], start=True, stop=True)
                last.then_inc(pe_to_dve, 1)
                for st in range(T // S):
                    for b in range(TB):
                        for t in range(2):
                            last = nc.tensor.matmul(ps[:, b, t * S:(t + 1) * S],
                                                    four[:, t, st * S + b * P:st * S + (b + 1) * P], C("dft"),
                                                    start=True, stop=True)
                    last.then_inc(pe_to_dve, 1)
                    pe.wait_ge(dve_to_pe, at(dve_to_pe))
                    for t in range(2):
                        for j in range(2):
                            for b in range(TB):
                                last = nc.tensor.matmul(ps[:, 2 + t, 0:S], fmid[:, b, t * S + j * P:t * S + (j + 1) * P],
                                                        C("seqsin" if j else "seqcos")[:, b * S:(b + 1) * S],
                                                        start=(j == 0 and b == 0), stop=(j == 1 and b == TB - 1))
                    last.then_inc(pe_to_dve, 1)
                attend(l, T)
                pe.wait_ge(dve_to_pe, at(dve_to_pe))
                for br in range(4):
                    if l == 0:
                        modulation()
                    for c in range(4):
                        project(u, T)
                    wb = unit().rearrange("p k c -> p (k c)").rearrange("p (k c) -> p k c", c=D)
                    for c in range(4):
                        g = claim()
                        for j in range(2):
                            for kt in range(2):
                                last = nc.tensor.matmul(ps[:, g + j, 0:T], wb[:, kt, (2 * c + j) * P:(2 * c + j + 1) * P],
                                                        branch[:, 2 * br + kt, 0:T], start=(kt == 0), stop=(kt == 1))
                    last.then_inc(units_used, 1)
                pe.wait_ge(dve_to_pe, at(dve_to_pe))
                project_and_normalize(merged, u, sq1, T, taken=False)
                pe.wait_ge(dve_to_pe, at(dve_to_pe))
                for b in range(nb):
                    for kt in range(KT):
                        last = nc.tensor.matmul(ps[:, 0, b * E:(b + 1) * E], u[:, kt, b * P:(b + 1) * P],
                                                V("w_router")[:, (l * KT + kt) * E:(l * KT + kt + 1) * E],
                                                start=(kt == 0), stop=(kt == KT - 1))
                last.then_inc(pe_to_dve, 1)
                for b in range(nb):
                    for half in range(2):
                        n = 2 * b + half
                        if n >= 4:
                            pe.wait_ge(act_to_pe, at(act_to_pe))
                        for j in range(4):
                            last = nc.tensor.transpose(ps[:, 4 + n % 4, j * P:(j + 1) * P],
                                                       h[:, 4 * half + j, b * P:(b + 1) * P], ident)
                        last.then_inc(pe_to_act, 1)
                rows = nb // TB * E
                pe.wait_ge(dve_to_pe, at(dve_to_pe))
                for b in range(TB):
                    last = nc.tensor.transpose(ps[0:rows, 1, b * P:(b + 1) * P],
                                               aff[:, b, 0:nb // TB, :].rearrange("p s e -> p (s e)"), ident)
                last.then_inc(pe_to_dve, 1)
                pe.wait_ge(dve_to_pe, at(dve_to_pe))
                for b in range(TB):
                    last = nc.tensor.transpose(ps[:, 2, b * 2 * E:b * 2 * E + rows], rowc[0:rows, b * P:(b + 1) * P],
                                               ident[0:rows, 0:rows])
                last.then_inc(pe_to_dve, 1)
                pe.wait_ge(dve_to_pe, at(dve_to_pe))
                pe.wait_ge(act_to_pe, at(act_to_pe, 4))
                for kt in range(KT):
                    for st in range(nb // TB):
                        n = kt * (nb // TB) + st
                        if n >= 4:
                            pe.wait_ge(dve_to_pe, at(dve_to_pe))
                        for b in range(TB):
                            last = nc.tensor.matmul(ps[:, n % 4, :], htok[:, st * TB + b, kt * P:(kt + 1) * P],
                                                    pick[:, st * TB + b, :], start=(b == 0), stop=(b == TB - 1))
                        last.then_inc(pe_to_dve, 1)
                for q in range(4):
                    for b in range(nb):
                        last = nc.tensor.transpose(ps[:, 4 + q, b * P:(b + 1) * P], wpick[:, b, q * P:(q + 1) * P], ident)
                    last.then_inc(pe_to_act, 1)
                pe.wait_ge(dve_to_pe, at(dve_to_pe, 4))
                pe.wait_ge(act_to_pe, at(act_to_pe, 4))
                slots = CAP * nb // TB
                if l == 0:
                    pe.wait_ge(y_kept, at(y_kept))
                    count.skip(added, 2)
                beside = P // slots
                pairs = 4 // beside
                with loop(E // GROUP, GROUP_UNITS, [(hidden_ready, pairs * GROUP), (y_kept, GROUP), (added, KT),
                                                    (xcur_ready, GROUP), (act_to_pe, pairs * GROUP)]) as turn:
                    def chunks(bank, lo, lhsT):
                        w = [unit() for _ in range(beside)]
                        for kt in range(KT):
                            for j in range(beside):
                                last = nc.tensor.matmul(ps[j * slots:(j + 1) * slots, bank, lo:lo + UC],
                                                        lhsT[:, kt, 0:slots], w[j][:, kt, :],
                                                        start=(kt == 0), stop=(kt == KT - 1))
                        last.then_inc(units_used, beside)

                    for e4 in range(GROUP):
                        pe.wait_ge(xcur_ready, at(xcur_ready))
                        for up in range(2):
                            for p in range(pairs):
                                chunks(2 * up + (p if pairs > 1 else e4 % 2), 0, xcur)
                        for p in range(pairs):
                            pe.wait_ge(hidden_ready, at(hidden_ready))
                            for t in range(2):
                                last = nc.tensor.transpose(ps[:, 0 if p else 4, t * P:(t + 1) * P],
                                                           hv[:, p, t * P:(t + 1) * P], ident)
                            last.then_inc(pe_to_act, 1)
                        pe.wait_ge(act_to_pe, at(act_to_pe, pairs))
                        pe.wait_ge(y_kept, at(y_kept, 0))
                        for p in range(pairs):
                            chunks(5, p * UC, hid)
                        count.skip(y_kept, 1)
                    pe.wait_ge(y_kept, at(y_kept, 0))
                    for kt in range(KT):
                        pe.wait_ge(added, at(added, 0 if kt == 0 else 1, less=1))
                        for st in range(nb // TB):
                            last = nc.tensor.matmul(ps[:, 6 + kt % 2, st * S:(st + 1) * S],
                                                    y4[:, st, kt * P:(kt + 1) * P],
                                                    wsel[:, bass.ds(turn, 1), st * S:(st + 1) * S]
                                                    .rearrange("p a n -> p (a n)"), start=True, stop=True)
                        last.then_inc(scattered, 1)
                    count.skip(added, 1)
                after_loop(E // GROUP, GROUP_UNITS)
                normalize(u, sq2, T)

            for l in range(DEPTH):
                layer(l)

            def first_keys():
                project(mem, S)

            def memory_attention():
                for c in range(3):
                    project(mem, S)
                for c in range(4):
                    w = unit()
                    g = claim()
                    for b in range(TB):
                        for kt in range(KT):
                            last = nc.tensor.matmul(ps[:, g + b, 0:S], mem[:, kt, b * P:(b + 1) * P], w[:, kt, :],
                                                    start=(kt == 0), stop=(kt == KT - 1))
                    last.then_inc(units_used, 1)
                pe.wait_ge(normed, at(normed))
                for c in range(4):
                    project(h, S)
                drained()
                for b in range(TB):
                    for hd in range(4):
                        for j in range(2):
                            last = nc.tensor.matmul(ps[:, hd // 2, hd % 2 * S:(hd % 2 + 1) * S],
                                                    xq[:, 2 * hd + j, b * P:(b + 1) * P], xk[:, 2 * hd + j, :],
                                                    start=(j == 0), stop=(j == 1))
                    last.then_inc(pe_to_dve, 1)
                    pe.wait_ge(dve_to_pe, at(dve_to_pe))
                    for hd in range(4):
                        for kb in range(TB):
                            n = 2 * hd + kb
                            last = nc.tensor.transpose(ps[:, 2 + n // 4, n % 4 * P:(n % 4 + 1) * P],
                                                       xp[:, hd, kb * P:(kb + 1) * P], ident)
                    last.then_inc(pe_to_act, 1)
                    pe.wait_ge(act_to_pe, at(act_to_pe))
                    for t in range(KT):
                        for kb in range(TB):
                            last = nc.tensor.matmul(ps[:, 4 + t // 4, t % 4 * P:(t % 4 + 1) * P],
                                                    xv[:, kb, t * P:(t + 1) * P], xpT[:, t // 2 * 2 + kb, :],
                                                    start=(kb == 0), stop=(kb == TB - 1))
                    last.then_inc(pe_to_dve, 1)
                pe.wait_ge(dve_to_pe, at(dve_to_pe))
                project_and_normalize(xo, t1, t2, S)

            def mlp():
                pe.wait_ge(normed, at(normed))
                with loop(2, 8, [(products_taken, 8)]):
                    for c in range(8):
                        project(h, S)
                after_loop(2, 8, 8)
                pe.wait_ge(squares_kept, at(squares_kept, 16))
                project_and_normalize(relu2, t1, t2, S, groups=4)

            def even_mixer():
                pe.wait_ge(normed, at(normed, 4))
                for kt in range(KT):
                    last = nc.tensor.matmul(ps[0:16, 7, 0:S], V("w_dt")[:, kt * 16:(kt + 1) * 16], h[:, kt, 0:S],
                                            start=(kt == 0), stop=(kt == KT - 1))
                last.then_inc(pe_to_dve, 1)
                pe.wait_ge(dve_to_pe, at(dve_to_pe))
                for c in range(18):
                    project(h, S)
                drained()
                normalize(conv, t2, S)
                drained()
                for n, rows in enumerate((dtv, acs)):
                    for b in range(TB):
                        last = nc.tensor.transpose(ps[:, 5, (2 * n + b) * 16:(2 * n + b + 1) * 16],
                                                   rows[:, b * P:(b + 1) * P], ident[0:16, 0:16])
                last.then_inc(pe_to_dve, 1)
                pe.wait_ge(dve_to_pe, at(dve_to_pe))
                for b in range(TB):
                    for n in range(2):
                        for j in range(4):
                            last = nc.tensor.transpose(ps[:, 2 * b + n, j * P:(j + 1) * P],
                                                       xbc[:, 4 * n + j, b * P:(b + 1) * P], ident)
                last.then_inc(pe_to_dve, 1)
                for g in range(2):
                    nc.tensor.matmul(ps[:, 4 + g, 0:S], xbc[:, 8 + g, 0:P], xbc[:, 10 + g, :], start=True, stop=True)
                    last = nc.tensor.matmul(ps[:, 4 + g, S:S + P], xbc[:, 8 + g, P:S], xbc[:, 10 + g, P:S],
                                            start=True, stop=True)
                last.then_inc(pe_to_dve, 1)
                pe.wait_ge(dve_to_pe, at(dve_to_pe))

                def spread(n):
                    if n >= 2:
                        pe.wait_ge(decay_ready, at(decay_ready))
                    bank = ps[:, n % 2, :]
                    nc.tensor.matmul(bank[:, 0:S], sel[:, n, :], acs, start=True, stop=False)
                    nc.tensor.matmul(bank[:, 0:P], ident, C("causal"), start=False, stop=True)
                    nc.tensor.matmul(bank[:, S:S + P], sel[:, n, :], acs[:, P:S], start=True, stop=False)
                    nc.tensor.matmul(bank[:, S:S + P], ident, C("causal"), start=False, stop=True)\
                        .then_inc(pe_to_act, 1)

                spread(0)
                for n in range(SSM_HEADS):
                    if n + 1 < SSM_HEADS:
                        spread(n + 1)
                    pe.wait_ge(dve_to_pe, at(dve_to_pe))
                    t, s = n // 2, n % 2 * HD
                    if n % 2 == 0 and t >= 2:
                        pe.wait_ge(y_tile_kept, at(y_tile_kept))
                    y = ps[s:s + HD, 2 + t % 2, :]
                    nc.tensor.matmul(y[:, 0:S], xdt[:, 0, n * HD:(n + 1) * HD], mask[n % 2][:, 0:S],
                                     start=True, stop=False)
                    last = nc.tensor.matmul(y[:, P:S], xdt[:, 1, n * HD:(n + 1) * HD], mask[n % 2][:, S:384],
                                            start=False, stop=True)
                    last.then_inc(head_done, 1)
                pe.wait_ge(y_tile_kept, at(y_tile_kept, 2))
                pe.wait_ge(act_to_pe, at(act_to_pe))
                for g in range(2):
                    for j in range(4):
                        last = nc.tensor.matmul(ps[:, 6 + g, 0:S], ones, t2[:, 4 * g + j, :], start=(j == 0), stop=(j == 3))
                last.then_inc(pe_to_dve, 1)
                pe.wait_ge(dve_to_pe, at(dve_to_pe))
                pe.wait_ge(memory_loaded, 16)
                project_and_normalize(mixin, t1, t2, S, groups=2, between=first_keys)

            def odd_mixer():
                pe.wait_ge(normed, at(normed))
                for c in range(4):
                    project(h, S)
                for c in range(4):
                    w = unit()
                    g = claim()
                    for b in range(TB):
                        for kt in range(KT):
                            last = nc.tensor.matmul(ps[:, g + b, 0:S], h[:, kt, b * P:(b + 1) * P], w[:, kt, :],
                                                    start=(kt == 0), stop=(kt == KT - 1))
                    last.then_inc(units_used, 1)
                for c in range(4):
                    project(h, S)
                drained()
                for kt in range(KT):
                    last = nc.tensor.matmul(ps[0:16, 0, 0:S], V("w_low")[:, kt * 16:(kt + 1) * 16], h[:, kt, 0:S],
                                            start=(kt == 0), stop=(kt == KT - 1))
                last.then_inc(pe_to_dve, 1)
                pe.wait_ge(dve_to_pe, at(dve_to_pe))
                for hd in range(4):
                    last = nc.tensor.matmul(ps[:, 2 + hd // 2, hd % 2 * S:(hd % 2 + 1) * S],
                                            V("w_gate2")[0:16, hd * P:(hd + 1) * P], low, start=True, stop=True)
                last.then_inc(pe_to_dve, 1)
                pe.wait_ge(dve_to_pe, at(dve_to_pe))
                for b in range(TB):
                    for hd in range(4):
                        last = nc.tensor.transpose(ps[:, b, hd * P:(hd + 1) * P], kend[:, hd, b * P:(b + 1) * P], ident)
                last.then_inc(pe_to_act, 1)
                for b in range(TB):
                    for hd in range(4):
                        last = nc.tensor.matmul(ps[:, 4 + b, hd * P:(hd + 1) * P], ktl[:, hd, b * P:(b + 1) * P],
                                                qt[:, hd, b * P:(b + 1) * P], start=True, stop=True)
                last.then_inc(pe_to_dve, 1)
                pe.wait_ge(act_to_pe, at(act_to_pe))
                pe.wait_ge(dve_to_pe, at(dve_to_pe))
                for c in range(3):
                    for hd in range(4):
                        n = c * 4 + hd
                        if n >= 2:
                            pe.wait_ge(dve_to_pe, at(dve_to_pe))
                        lo = c % 2 * GLA_CHUNK
                        nc.tensor.matmul(ps[:, 6 + n % 2, 0:S], kendT[lo:lo + GLA_CHUNK, c // 2 * 4 + hd, :],
                                         gv[lo:lo + GLA_CHUNK, c // 2, hd * S:(hd + 1) * S], start=True, stop=True)\
                            .then_inc(pe_to_dve, 1)
                pe.wait_ge(dve_to_pe, at(dve_to_pe, 2))
                for hd in range(4):
                    for j in range(2):
                        v0 = hd * S + j * P
                        for b in range(TB):
                            nc.tensor.matmul(ps[:, hd, j * S + b * P:j * S + (b + 1) * P], gv[:, b, v0:v0 + P],
                                             att[:, b * 4 + hd, :], start=True, stop=False)
                            for c in range(2 * b, 2 * b + 2):
                                if c:
                                    last = nc.tensor.matmul(
                                        ps[:, hd, j * S + c * GLA_CHUNK:j * S + (c + 1) * GLA_CHUNK],
                                        hist[:, hd, (c - 1) * S + j * P:(c - 1) * S + (j + 1) * P],
                                        qt[:, hd, c * GLA_CHUNK:(c + 1) * GLA_CHUNK], start=False, stop=(c % 2 == 1))
                last.then_inc(pe_to_dve, 1)
                pe.wait_ge(act_to_pe, at(act_to_pe))
                for hd in range(4):
                    for j in range(2):
                        last = nc.tensor.matmul(ps[:, 4 + hd // 2, hd % 2 * S:(hd % 2 + 1) * S], ones,
                                                t2[:, 2 * hd + j, :], start=(j == 0), stop=(j == 1))
                last.then_inc(pe_to_dve, 1)
                pe.wait_ge(dve_to_pe, at(dve_to_pe))
                project_and_normalize(go, t1, t2, S, between=first_keys)

            even_mixer()
            memory_attention()
            mlp()
            odd_mixer()
            memory_attention()
            mlp()
            assert state["unit"] == n_units

        @block.scalar
        def _(act):
            count = Count(act)
            at = count.at

            def link(instruction):
                instruction.then_inc(act_step, 1)
                act.wait_ge(act_step, at(act_step))
            A = nc.scalar.activation

            def inverse_roots(*tiles):
                act.wait_ge(variances_ready, at(variances_ready))
                for x in tiles:
                    last = A(x, x, ACT.Ln)
                link(last)
                for x in tiles:
                    last = A(x, x, ACT.Exp, scale=-0.5)
                last.then_inc(inverses_ready, 1)

            def normalize(x, sq, n, tiles, gain, shift, signal=True):
                for kt in range(0, KT, 2):
                    act.wait_ge(centred, at(centred))
                    A(sq[:, kt:kt + 2, 0:n], x[:, kt:kt + 2, 0:n], ACT.Square).then_inc(squares_ready, 1)
                inverse_roots(stat2[:, 0:n])
                for kt in range(KT):
                    if kt % 2 == 0:
                        act.wait_ge(scaled, at(scaled))
                    last = A(tiles[:, kt, 0:n], x[:, kt, 0:n], ACT.Identity, bias=shift[:, kt:kt + 1],
                             scale=gain[:, kt:kt + 1])
                state["product"] += 1
                if signal:
                    last.then_inc(normed, 1)
                else:
                    link(last)

            act.wait_ge(vectors_loaded, 32)
            act.wait_ge(dve_to_act, at(dve_to_act))
            A(cs[:, :, 0:2], V("c").rearrange("p (k s) -> p k s", s=2), ACT.Sigmoid).then_inc(act_to_dve, 1)
            state = {"turned": 0, "product": 0, "mixed": 0}

            def modulation():
                count.skip(units_used, 8)
                state["product"] += 2

            modulation()

            def attend(l, T):
                batches = [(k, b) for k in range(3) for b in range(T // P)]

                def exps(n):
                    k, b = batches[n]
                    lo = 0 if b < TB else S
                    m = mx[:, n % 2 * 4:n % 2 * 4 + 4]
                    act.wait_ge(dve_to_act, at(dve_to_act))
                    for hd in range(4):
                        last = A(prob[n % 2][:, hd, lo:512], ps[:, hd, lo:512], ACT.Exp, scale=HD ** -0.5,
                                 bias=m[:, hd:hd + 1], accum_out=sums[:, n % 2 * 4 + hd:n % 2 * 4 + hd + 1])
                    if k == 1:
                        last = A(es[:, n % 2 * 4:n % 2 * 4 + 4], es[:, n % 2 * 4:n % 2 * 4 + 4], ACT.Exp)
                    last.then_inc(exps_ready, 1)

                exps(0)
                for n, (k, b) in enumerate(batches):
                    lo = 0 if b < TB else S
                    if l or n:
                        act.wait_ge(mixed, at(mixed, 0))
                    for hd in range(4):
                        act.wait_ge(turned, at(turned))
                        A(probT[:, hd, lo:512], ps[:, 4 + hd % 2, lo:512], ACT.Copy).then_inc(turned_kept, 1)
                    count.skip(mixed, 1)
                    if n + 1 < len(batches):
                        exps(n + 1)

            def layer(l):
                T = 512 if l == 0 else S
                nb = T // P
                count.skip(units_used, 7)
                if l == 0:
                    modulation()
                act.wait_ge(dve_to_act, at(dve_to_act))
                A(nsq[:, 0:2, 0:T], qk[:, 0:2, 0:T], ACT.Square)
                A(nsq[:, 2:4, :], qk[:, 2:4, :], ACT.Square).then_inc(act_to_pe, 1)
                state["product"] += 7
                inverse_roots(nsq[:, 0:2, 0:T], nsq[:, 2:4, :])
                attend(l, T)
                for br in range(4):
                    if l == 0:
                        modulation()
                    if br:
                        act.wait_ge(dve_to_act, at(dve_to_act))
                    for c in range(4):
                        g = 2 * (state["product"] % 4)
                        state["product"] += 1
                        act.wait_ge(units_used, at(units_used))
                        A(gate[:, 2 * c:2 * c + 2, 0:T], ps[:, g:g + 2, 0:T], ACT.Sigmoid)\
                            .then_inc(act_to_dve, 1)
                    count.skip(units_used, 1)
                    state["product"] += 4
                count.skip(units_used, 4)
                state["product"] += 4
                normalize(u, sq1, T, h, V("ln1_g")[:, l * KT:], V("ln1_b")[:, l * KT:])
                act.wait_ge(dve_to_act, at(dve_to_act))
                A(logit[:, 0:nb, :], logit[:, 0:nb, :], ACT.Exp).then_inc(act_to_dve, 1)
                for b in range(nb):
                    for half in range(2):
                        act.wait_ge(pe_to_act, at(pe_to_act))
                        A(htok[:, b, half * 512:(half + 1) * 512], ps[:, 4 + (2 * b + half) % 4, :], ACT.Copy)\
                            .then_inc(act_to_pe, 1)
                for q in range(4):
                    act.wait_ge(pe_to_act, at(pe_to_act))
                    A(wsel[:, q, 0:T], ps[:, 4 + q, 0:T], ACT.Copy).then_inc(act_to_pe, 1)
                slots = CAP * nb // TB
                act.wait_ge(dve_to_act, at(dve_to_act))
                beside = P // slots
                pairs = 4 // beside
                with count.loop(E // GROUP, [(units_used, GROUP_UNITS), (pe_to_act, pairs * GROUP)]) as turn:
                    for e4 in range(GROUP):
                        act.wait_ge(units_used, at(units_used, 0, less=4))
                        A(xcur[:, :, 0:slots], xs[:, :, bass.ds(turn * GROUP + e4, 1), 0:slots]
                          .rearrange("p k a s -> p k (a s)"), ACT.Copy).then_inc(xcur_ready, 1)
                        for p in range(pairs):
                            act.wait_ge(units_used, at(units_used, beside))
                            A(sg[:, p, :], ps[:, p if pairs > 1 else e4 % 2, 0:UC], ACT.Sigmoid).then_inc(act_to_dve, 1)
                        count.skip(units_used, 4)
                        for p in range(pairs):
                            act.wait_ge(pe_to_act, at(pe_to_act))
                            A(hid[:, 2 * beside * p:2 * beside * (p + 1), 0:slots].rearrange("p (j t) s -> p t j s", t=2),
                              ps[:, 0 if p else 4, 0:UC].rearrange("p (t j s) -> p t j s", t=2, s=slots), ACT.Copy)\
                                .then_inc(act_to_pe, 1)
                        count.skip(units_used, 4)
                normalize(u, sq2, T, h, V("ln2_g")[:, l * KT:], V("ln2_b")[:, l * KT:])

            for l in range(DEPTH):
                layer(l)

            def latent_norm(n):
                normalize(t1, t2, S, h, V("ln_g")[:, n * KT:], V("ln_b")[:, n * KT:])

            def memory_attention():
                count.skip(units_used, 12)
                state["product"] += 12
                for b in range(TB):
                    act.wait_ge(dve_to_act, at(dve_to_act))
                    for hd in range(4):
                        last = A(xp[:, hd, :], ps[:, hd // 2, hd % 2 * S:(hd % 2 + 1) * S], ACT.Exp, scale=1.0 / 16,
                                 bias=mx[:, hd:hd + 1], accum_out=sums[:, hd:hd + 1])
                    last.then_inc(act_to_dve, 1)
                    act.wait_ge(pe_to_act, at(pe_to_act))
                    A(xpT[:, :, :], ps[:, 2:4, :].rearrange("p a (b n) -> p (a b) n", n=P), ACT.Copy)\
                        .then_inc(act_to_pe, 1)
                count.skip(units_used, 4)
                state["product"] += 4

            def even_mixer():
                A(nega, V("a_log")[0:16, :], ACT.Exp)
                act.wait_ge(dve_to_act, at(dve_to_act))
                A(dtc, dts, ACT.Exp, scale=-1.0).then_inc(act_to_dve, 1)
                act.wait_ge(dve_to_act, at(dve_to_act))
                A(dts, acs, ACT.Ln).then_inc(act_to_dve, 1)
                for c in range(4):
                    act.wait_ge(units_used, at(units_used, 2))
                    g = 2 * ((state["product"] + 1) % 4)
                    state["product"] += 2
                    if c:
                        act.wait_ge(dve_to_act, at(dve_to_act))
                    A(sig, ps[:, g:g + 2, 0:S], ACT.Sigmoid).then_inc(act_to_dve, 1)
                count.skip(units_used, 6)
                state["product"] += 6
                for c in range(4):
                    act.wait_ge(units_used, at(units_used))
                    g = 2 * (state["product"] % 4)
                    state["product"] += 1
                    act.wait_ge(dve_to_act, at(dve_to_act))
                    A(sig, ps[:, g:g + 2, 0:S], ACT.Sigmoid).then_inc(act_to_dve, 1)
                act.wait_ge(dve_to_act, at(dve_to_act))
                A(xsig, xbc[:, :, :], ACT.Sigmoid).then_inc(act_to_dve, 1)
                normalize(conv, t2, S, mixin, V("conv_ln_g"), V("conv_ln_b"), signal=False)
                A(conv, mixin[:, 0:KT, :], ACT.Sigmoid).then_inc(act_to_dve, 1)
                for n in range(SSM_HEADS):
                    act.wait_ge(pe_to_act, at(pe_to_act))
                    A(decay[n % 2][:, 0:S], ps[:, n % 2, 0:S], ACT.Exp, bias=acsT[:, n:n + 1])
                    A(decay[n % 2][:, S:384], ps[:, n % 2, S:384], ACT.Exp, bias=acsT[:, 16 + n:17 + n])\
                        .then_inc(decay_ready, 1)
                act.wait_ge(dve_to_act, at(dve_to_act))
                A(t2, mixin[:, KT:, :], ACT.Square).then_inc(act_to_pe, 1)
                inverse_roots(small[:, 0:512])
                count.skip(units_used, 8)
                state["product"] += 4

            def odd_mixer():
                count.skip(units_used, 8)
                state["product"] += 8
                for c in range(4):
                    act.wait_ge(units_used, at(units_used))
                    g = 2 * (state["product"] % 4)
                    state["product"] += 1
                    if c:
                        act.wait_ge(dve_to_act, at(dve_to_act))
                    A(gmid[:, 0:2, :], ps[:, g:g + 2, 0:S], ACT.Sigmoid).then_inc(act_to_dve, 1)
                act.wait_ge(dve_to_act, at(dve_to_act))
                link(A(en, en, ACT.Exp, scale=-1.0))
                A(en, en, ACT.Ln, bias=1.0).then_inc(act_to_dve, 1)
                act.wait_ge(dve_to_act, at(dve_to_act))
                A(qt, eb, ACT.Exp)
                A(ktl, eb, ACT.Exp, scale=-1.0)
                A(kend, gmid, ACT.Exp)
                A(gend, eb.rearrange("p h (c n) -> p h c n", n=GLA_CHUNK)[:, :, :, GLA_CHUNK - 1], ACT.Exp)\
                    .then_inc(act_to_dve, 1)
                act.wait_ge(pe_to_act, at(pe_to_act))
                A(kendT, ps[:, 0:2, :].rearrange("p b (h n) -> p (b h) n", n=P), ACT.Copy).then_inc(act_to_pe, 1)
                act.wait_ge(dve_to_act, at(dve_to_act))
                A(t2, go, ACT.Square).then_inc(act_to_pe, 1)
                inverse_roots(small[:, 0:1024])
                count.skip(units_used, 4)
                state["product"] += 4

            even_mixer()
            latent_norm(0)
            for l in range(DEPTH):
                if l:
                    odd_mixer()
                    latent_norm(3)
                memory_attention()
                latent_norm(3 * l + 1)
                count.skip(units_used, 32)
                state["product"] += 20
                latent_norm(3 * l + 2)

        @block.vector
        def _(dve):
            count = Count(dve)
            at = count.at

            def link(instruction):
                instruction.then_inc(dve_step, 1)
                dve.wait_ge(dve_step, at(dve_step))
            v = nc.vector
            state = {"product": 0, "mark": 0}

            def product(more=1):
                dve.wait_ge(units_used, at(units_used, more))
                g = 2 * (state["product"] % 4)
                state["product"] += 1
                return g

            def taken(instruction, n=1):
                instruction.then_inc(products_taken, n)

            def wide(x, shape, axis=1):
                return x.unsqueeze(axis).broadcast_to(shape)

            def normalize(x, n, eps):
                g = product(0)
                dve.wait_ge(pe_to_dve, at(pe_to_dve))
                link(v.tensor_scalar(stat[:, 0:n], ps[:, g, 0:n], 1.0 / D, None, ALU.mult))
                for kt in range(0, KT, 2):
                    pair = x[:, kt:kt + 2, 0:n]
                    v.tensor_tensor(pair, pair, wide(stat[:, 0:n], [P, 2, n]), ALU.subtract).then_inc(centred, 1)
                dve.wait_ge(pe_to_dve, at(pe_to_dve))
                v.tensor_scalar(stat2[:, 0:n], ps[:, g + 1, 0:n], 1.0 / D, eps, ALU.mult, ALU.add)\
                    .then_inc(variances_ready, 1)
                taken(mark())
                dve.wait_ge(inverses_ready, at(inverses_ready))
                for kt in range(0, KT, 2):
                    pair = x[:, kt:kt + 2, 0:n]
                    v.tensor_tensor(pair, pair, wide(stat2[:, 0:n], [P, 2, n]), ALU.mult).then_inc(scaled, 1)

            def modulate(l, chunk, streams):
                for kt in range(KT):
                    for st in range(streams):
                        last = v.tensor_scalar(u[:, kt, st * S:(st + 1) * S], h[:, kt, st * S:(st + 1) * S],
                                               mod[:, l * 48 + (chunk + 1) * 8 + kt, st:st + 1],
                                               mod[:, l * 48 + chunk * 8 + kt, st:st + 1], ALU.mult, ALU.add)
                last.then_inc(dve_to_pe, 1)

            def mark():
                state["mark"] = (state["mark"] + 1) % 32
                return v.tensor_copy(tick[:, state["mark"]:state["mark"] + 1], ident[:, 0:1])

            def settle():
                link(mark())

            dve.wait_ge(vectors_loaded, 32)
            v.memset(cs, 0.0).then_inc(dve_to_act, 1)
            dve.wait_ge(act_to_dve, at(act_to_dve))
            v.tensor_tensor(cs[:, :, 0:2], cs[:, :, 0:2], V("c").rearrange("p (k s) -> p k s", s=2), ALU.mult)\
                .then_inc(dve_to_pe, 1)

            def modulation(n):
                g = product(4)
                v.tensor_copy(mrow[0], ps[:, g, 0:UC])
                dve.wait_ge(units_used, at(units_used, 4))
                taken(v.tensor_copy(mrow[1], ps[:, g + 1, 0:UC]))
                mark().then_inc(dve_to_pe, 1)
                g = product(0)
                dve.wait_ge(pe_to_dve, at(pe_to_dve))
                to = mod[:, n * 16:(n + 1) * 16, :]
                b_mod = V("b_mod")[:, n * 16:(n + 1) * 16]
                for t in range(2):
                    last = v.tensor_tensor(to.rearrange("p (g t) s -> p t g s", t=2)[:, t, :, :],
                                           ps[:, g, t * UC:(t + 1) * UC].rearrange("p (g s) -> p g s", s=32)[:, :, 0:2],
                                           wide(b_mod.rearrange("p (g t) -> p t g", t=2)[:, t, :], [P, 8, 2], 2), ALU.add)
                taken(last)
                settle()
                for half in range(2):
                    if (2 * n + half) % 6 in (1, 4):
                        m = to[:, half * 8:half * 8 + 8, :]
                        link(v.tensor_scalar(m, m, 1.0, None, ALU.add))

            modulation(0)
            dve.wait_ge(inputs_loaded, 32)
            v.tensor_scalar(nsink, V("sink"), -1.0, None, ALU.mult)
            v.memset(mx[:, 1:2], 0.0).then_inc(y_kept, 1)

            def attend(l, T):
                batches = [(k, b) for k in range(3) for b in range(T // P)]

                def maxima(n):
                    k, b = batches[n]
                    lo = 0 if b < TB else S
                    m = mx[:, n % 2 * 4:n % 2 * 4 + 4]
                    dve.wait_ge(scores_ready, at(scores_ready))
                    link(v.tensor_reduce(m, ps[:, 0:4, lo:512], AX.X, ALU.max))
                    last = v.tensor_scalar(m, m, -(HD ** -0.5), None, ALU.mult)
                    if k == 1:
                        link(last)
                        link(v.tensor_tensor(m, m, nsink[:, 4 * l:4 * l + 4], ALU.min))
                        last = v.tensor_tensor(es[:, n % 2 * 4:n % 2 * 4 + 4], m, nsink[:, 4 * l:4 * l + 4], ALU.subtract)
                    last.then_inc(dve_to_act, 1)

                def keep(n):
                    k, b = batches[n]
                    dve.wait_ge(mixed, at(mixed))
                    o = 0 if k == 0 else 2 * k + 2
                    v.tensor_copy(branch[:, o:o + 2, b * P:(b + 1) * P],
                                            ps[:, 6 + state["mixed"] % 2, 0:2 * P].rearrange("p (t n) -> p t n", n=P)).then_inc(mixed_kept, 1)
                    state["mixed"] += 1

                maxima(0)
                for n, (k, b) in enumerate(batches):
                    lo = 0 if b < TB else S
                    q = n % 2 * 4
                    dve.wait_ge(exps_ready, at(exps_ready))
                    if k == 1:
                        link(v.tensor_tensor(sums[:, q:q + 4], sums[:, q:q + 4], es[:, q:q + 4], ALU.add))
                    link(v.reciprocal(rec[:, 0:4], sums[:, q:q + 4]))
                    pr = prob[n % 2][:, :, lo:512]
                    v.tensor_tensor(pr, pr, wide(rec[:, 0:4], [P, 4, 512 - lo], 2), ALU.mult).then_inc(probs_ready, 1)
                    if n + 1 < len(batches):
                        maxima(n + 1)
                    if n:
                        keep(n - 1)
                keep(len(batches) - 1)

            state["mixed"] = 0

            def layer(l):
                T = 512 if l == 0 else S
                nb, ns = T // P, T // S
                if l:
                    dve.wait_ge(normed, at(normed))
                modulate(l, 0, 2)
                for kind in range(3):
                    if l == 0 and kind == 1:
                        modulation(1)
                    g = product()
                    taken(v.tensor_copy(qk[:, 4 * kind:4 * kind + 2, 0:T], ps[:, g:g + 2, 0:T]))
                    g = product()
                    for t in range(2):
                        for half in range(2):
                            v.tensor_copy(qk[half * HD:(half + 1) * HD, 4 * kind + 2 + t, :],
                                          ps[t * HD:(t + 1) * HD, g, :])
                    last = v.tensor_copy(val[:, :, kind * P:(kind + 1) * P],
                                         ps[:, g + 1, :].rearrange("p (b n) -> p b n", n=P))
                    taken(last)
                    if kind == 0:
                        g = product()
                        mark().then_inc(dve_to_act, 1)
                        taken(v.tensor_copy(four[:, :, 0:T], ps[:, g:g + 2, 0:T]))
                dve.wait_ge(pe_to_dve, at(pe_to_dve))
                for t, n in ((0, T), (2, 512)):
                    v.tensor_scalar(nsq[:, t:t + 2, 0:n], ps[:, t:t + 2, 0:n], 1.0 / HD, EPS1, ALU.mult, ALU.add)
                mark().then_inc(variances_ready, 1)
                dve.wait_ge(inverses_ready, at(inverses_ready))
                for t, n in ((0, T), (2, 512)):
                    last = v.scalar_tensor_tensor(qk[:, t:t + 2, 0:n], qk[:, t:t + 2, 0:n],
                                                  V("qk_gain")[:, 2 * l + t // 2:2 * l + t // 2 + 1],
                                                  nsq[:, t:t + 2, 0:n], ALU.mult, ALU.mult)
                last.then_inc(dve_to_pe, 1)
                dve.wait_ge(pe_to_dve, at(pe_to_dve))
                link(v.tensor_tensor(rtmp, ps[:, 4:8, :].rearrange("p a (b n) -> p (a b) n", n=S),
                                          wide(C("sin"), [P, 8, S]), ALU.mult))
                link(v.tensor_tensor(qk[:, 0:8, 0:S], qk[:, 0:8, 0:S], wide(C("cos"), [P, 8, S]), ALU.mult))
                link(v.tensor_tensor(qk[:, 0:8, 0:S], qk[:, 0:8, 0:S], rtmp, ALU.add))
                for st in range(ns):
                    dve.wait_ge(pe_to_dve, at(pe_to_dve))
                    v.tensor_copy(fmid, ps[:, 0:2, :]).then_inc(dve_to_pe, 1)
                    dve.wait_ge(pe_to_dve, at(pe_to_dve))
                    v.tensor_copy(branch[:, 2:4, st * S:(st + 1) * S], ps[:, 2:4, 0:S])
                dve.wait_ge(bias_loaded, 16 * 16 * (l + 1))
                rows = bias.rearrange("p a (r c) -> p (a r) c", c=64)
                v.scalar_tensor_tensor(rows, rows, HD ** 0.5, wide(C("near"), [P, 32, 64]), ALU.mult, ALU.add)\
                    .then_inc(dve_to_pe, 1)
                attend(l, T)
                mark().then_inc(dve_to_pe, 1)
                for br in range(4):
                    if l == 0:
                        modulation(2 + br)
                    for c in range(4):
                        state["product"] += 1
                        dve.wait_ge(units_used, at(units_used))
                        dve.wait_ge(act_to_dve, at(act_to_dve))
                        mark().then_inc(products_taken, 1)
                    for c in range(4):
                        g = product(1 if c == 0 else 0)
                        e, m = gate[:, 2 * c:2 * c + 2, 0:T], merged[:, 2 * c:2 * c + 2, 0:T]
                        if br == 0:
                            last = v.tensor_tensor(m, e, ps[:, g:g + 2, 0:T], ALU.mult)
                            taken(last)
                        else:
                            t = gated[c % 2][:, :, 0:T]
                            taken(v.tensor_tensor(t, e, ps[:, g:g + 2, 0:T], ALU.mult))
                            settle()
                            last = v.tensor_tensor(m, m, t, ALU.add)
                    if br < 3:
                        settle()
                        mark().then_inc(dve_to_act, 1)
                    else:
                        last.then_inc(dve_to_pe, 1)
                for c in range(4):
                    g = product()
                    for j in range(2):
                        for st in range(ns):
                            last = v.tensor_scalar(u[:, 2 * c + j, st * S:(st + 1) * S],
                                                   ps[:, g + j, st * S:(st + 1) * S],
                                                   mod[:, l * 48 + 16 + 2 * c + j, st:st + 1], None, ALU.mult)
                    taken(last)
                    settle()
                    pair = slice(2 * c, 2 * c + 2)
                    v.scalar_tensor_tensor(u[:, pair, 0:T], h[:, pair, 0:T], ALPHA, u[:, pair, 0:T], ALU.mult, ALU.add)\
                        .then_inc(residual_ready, 1)
                normalize(u, T, EPS1)
                dve.wait_ge(normed, at(normed))
                modulate(l, 3, ns)
                dve.wait_ge(pe_to_dve, at(pe_to_dve))
                lg, lp = logit[:, 0:nb, :], ps[:, 0, 0:nb * E].rearrange("p (b e) -> p b e", e=E)
                link(v.tensor_reduce(mx[:, 0:nb], lp, AX.X, ALU.max))
                v.tensor_tensor(lg, lp, wide(mx[:, 0:nb], [P, nb, E], 2), ALU.subtract).then_inc(dve_to_act, 1)
                dve.wait_ge(act_to_dve, at(act_to_dve))
                link(v.tensor_reduce(sums[:, 0:nb], lg, AX.X, ALU.add))
                link(v.reciprocal(rec[:, 0:nb], sums[:, 0:nb]))
                for st in range(ns):
                    last = v.tensor_tensor(aff[:, :, st, :], logit[:, st * TB:(st + 1) * TB, :],
                                           wide(rec[:, st * TB:(st + 1) * TB], [P, TB, E], 2), ALU.mult)
                last.then_inc(dve_to_pe, 1)
                R = ns * E
                ra, rb, rc = rowa[0:R, :], rowb[0:R, :], rowc[0:R, :]
                dve.wait_ge(pe_to_dve, at(pe_to_dve))
                link(v.tensor_copy(ra, ps[0:R, 1, 0:S]))
                src = ra
                for r, dst in enumerate((rb, rc, rb, rc)):
                    link(v.max(top8[0:R, r, :], src))
                    link(v.match_replace(dst, top8[0:R, r, :], src, -1.0))
                    src = dst
                v.memset(onesrow[0:R, :], 1.0)
                link(v.tensor_scalar(rb, rc, 0.0, None, ALU.is_lt))
                link(v.tensor_tensor_scan(ra, onesrow[0:R, :], rb, 0.0, ALU.mult, ALU.add))
                link(v.tensor_tensor(rc, ra, rb, ALU.mult))
                v.tensor_scalar(rc, rc, -1.0, None, ALU.add).then_inc(dve_to_pe, 1)
                dve.wait_ge(pe_to_dve, at(pe_to_dve))
                link(v.tensor_copy(rank[:, :, 0:ns, :], ps[:, 2, 0:TB * 2 * E]
                                        .rearrange("p (b s e) -> p b s e", b=TB, s=2)[:, :, 0:ns, :]))
                for st in range(ns):
                    for b in range(TB):
                        sel4 = pick[:, st * TB + b, :].rearrange("p (e n) -> p e n", n=CAP)
                        v.tensor_tensor(sel4, wide(rank[:, b, st, :], [P, E, CAP], 2), wide(C("iota"), [P, E, CAP]),
                                        ALU.is_equal)
                settle()
                for st in range(ns):
                    for b in range(TB):
                        sel4 = pick[:, st * TB + b, :].rearrange("p (e n) -> p e n", n=CAP)
                        last = v.tensor_tensor(wpick[:, st * TB + b, :].rearrange("p (e n) -> p e n", n=CAP), sel4,
                                               wide(aff[:, b, st, :], [P, E, CAP], 2), ALU.mult)
                last.then_inc(dve_to_pe, 1)
                for kt in range(KT):
                    for st in range(ns):
                        dve.wait_ge(pe_to_dve, at(pe_to_dve))
                        v.tensor_scalar(xs[:, kt, :, st * CAP:(st + 1) * CAP],
                                        ps[:, (kt * ns + st) % 4, :].rearrange("p (e n) -> p e n", n=CAP),
                                        mod[:, l * 48 + 32 + kt, st:st + 1], mod[:, l * 48 + 24 + kt, st:st + 1],
                                        ALU.mult, ALU.add).then_inc(dve_to_pe, 1)
                slots = CAP * ns
                mark().then_inc(dve_to_act, 1)
                dve.wait_ge(units_used, at(units_used, 0, less=-1))
                last = v.memset(acc[:, :, 0:T], 0.0)
                if l == 0:
                    last.then_inc(added, 2)
                else:
                    link(last)
                beside = P // slots
                pairs = 4 // beside
                with count.loop(E // GROUP, [(units_used, GROUP_UNITS), (act_to_dve, pairs * GROUP), (scattered, KT),
                                             (dve_step, pairs * GROUP)]):
                    for e4 in range(GROUP):
                        for p in range(pairs):
                            dve.wait_ge(act_to_dve, at(act_to_dve))
                            link(v.tensor_tensor(sg[:, p, :], sg[:, p, :], ps[:, p if pairs > 1 else e4 % 2, 0:UC],
                                                 ALU.mult))
                        for p in range(pairs):
                            dve.wait_ge(units_used, at(units_used, beside + (4 if p == 0 else 0)))
                            v.tensor_tensor(hv[:, p, :], sg[:, p, :], ps[:, 2 + (p if pairs > 1 else e4 % 2), 0:UC],
                                            ALU.mult).then_inc(hidden_ready, 1)
                        dve.wait_ge(units_used, at(units_used, 4))
                        for st in range(ns):
                            for j in range(beside):
                                src = ps[j * slots + CAP * st:j * slots + CAP * (st + 1), 5, 0:pairs * UC]
                                last = v.tensor_copy(y4[CAP * e4:CAP * (e4 + 1), st, :]
                                                     .rearrange("p (a j n) -> p a j n", j=beside, n=UC)[:, :, j, :],
                                                     src.rearrange("p (a n) -> p a n", n=UC))
                        last.then_inc(y_kept, 1)
                    for kt in range(KT):
                        dve.wait_ge(scattered, at(scattered))
                        v.tensor_tensor(acc[:, kt, 0:T], acc[:, kt, 0:T], ps[:, 6 + kt % 2, 0:T], ALU.add)\
                            .then_inc(added, 1)
                dve.wait_ge(added, 2 + (l + 1) * KT * E // GROUP)
                for c in range(KT // 2):
                    for kt in (2 * c, 2 * c + 1):
                        for st in range(ns):
                            last = v.tensor_scalar(u[:, kt, st * S:(st + 1) * S], acc[:, kt, st * S:(st + 1) * S],
                                                   mod[:, l * 48 + 40 + kt, st:st + 1], None, ALU.mult)
                    link(last)
                    pair = slice(2 * c, 2 * c + 2)
                    v.scalar_tensor_tensor(u[:, pair, 0:T], h[:, pair, 0:T], ALPHA, u[:, pair, 0:T], ALU.mult, ALU.add)\
                        .then_inc(residual_ready, 1)
                normalize(u, T, EPS1)

            for l in range(DEPTH):
                layer(l)

            def residual(units_each=1):
                for c in range(4):
                    g = product(units_each)
                    taken(v.scalar_tensor_tensor(t1[:, 2 * c:2 * c + 2, :], h[:, 2 * c:2 * c + 2, 0:S], ALPHA,
                                                 ps[:, g:g + 2, 0:S], ALU.mult, ALU.add))

            def memory_attention():
                for c in range(4):
                    g = product()
                    taken(v.tensor_copy(xk[:, 2 * c:2 * c + 2, :], ps[:, g:g + 2, 0:S]))
                for c in range(4):
                    g = product()
                    taken(v.tensor_copy(xv[:, :, c * UC:(c + 1) * UC], ps[:, g:g + 2, 0:S]))
                dve.wait_ge(normed, at(normed))
                for c in range(4):
                    g = product()
                    taken(v.tensor_copy(xq[:, 2 * c:2 * c + 2, :], ps[:, g:g + 2, 0:S]))
                for b in range(TB):
                    dve.wait_ge(pe_to_dve, at(pe_to_dve))
                    link(v.tensor_reduce(mx[:, 0:4], ps[:, 0:2, :].rearrange("p a (b n) -> p (a b) n", n=S),
                                              AX.X, ALU.max))
                    v.tensor_scalar(mx[:, 0:4], mx[:, 0:4], -1.0 / 16, None, ALU.mult).then_inc(dve_to_act, 1)
                    dve.wait_ge(act_to_dve, at(act_to_dve))
                    link(v.reciprocal(rec[:, 0:4], sums[:, 0:4]))
                    v.tensor_tensor(xp, xp, wide(rec[:, 0:4], [P, 4, S], 2), ALU.mult).then_inc(dve_to_pe, 1)
                    dve.wait_ge(pe_to_dve, at(pe_to_dve))
                    last = v.tensor_copy(xo[:, :, b * P:(b + 1) * P],
                                         ps[:, 4:6, :].rearrange("p a (b n) -> p (a b) n", n=P))
                last.then_inc(dve_to_pe, 1)
                residual()
                normalize(t1, S, EPS2)

            def mlp():
                dve.wait_ge(normed, at(normed))
                with count.loop(2, [(units_used, 8), (dve_step, 8)]) as turn:
                    for c in range(8):
                        g = product()
                        r = relu2[:, bass.ds(turn * 16 + 2 * c, 2), :]
                        taken(v.tensor_scalar(r, ps[:, g:g + 2, 0:S], 0.0, None, ALU.max))
                        settle()
                        v.tensor_tensor(r, r, r, ALU.mult).then_inc(squares_kept, 1)
                state["product"] += 8
                residual(4)
                normalize(t1, S, EPS2)

            def even_mixer():
                v.memset(cpad[:, :, 0:CONV_W - 1], 0.0)
                v.memset(xpad[:, :, 0:SSM_W - 1], 0.0)
                dve.wait_ge(pe_to_dve, at(pe_to_dve))
                v.tensor_scalar(dtv, ps[0:16, 7, 0:S], V("dt_bias")[0:16, :], None, ALU.add).then_inc(dve_to_pe, 1)
                settle()
                link(v.tensor_scalar(dts, dtv, -1.0, None, ALU.mult))
                v.tensor_tensor(dts, dtv, dts, ALU.max).then_inc(dve_to_act, 1)
                dve.wait_ge(act_to_dve, at(act_to_dve))
                v.tensor_scalar(acs, dtc, 1.0, None, ALU.add).then_inc(dve_to_act, 1)
                dve.wait_ge(act_to_dve, at(act_to_dve))
                link(v.tensor_scalar(acs, acs, -1.0, None, ALU.add))
                unit16 = part(20244, S, rows=16)
                link(v.tensor_scalar(unit16, acs, 0.0, None, ALU.is_equal))
                link(v.tensor_tensor(acs, acs, unit16, ALU.add))
                link(v.tensor_tensor(dts, dts, unit16, ALU.add))
                link(v.reciprocal(acs, acs))
                link(v.tensor_tensor(dts, dts, acs, ALU.mult))
                link(v.tensor_tensor(dts, dts, dtc, ALU.mult))
                link(v.scalar_tensor_tensor(dtv, dtv, 0.0, dts, ALU.max, ALU.add))
                link(v.tensor_scalar(dtc, dtv, nega, -1.0, ALU.mult, ALU.mult))
                link(v.memset(dts, 1.0))
                link(v.tensor_tensor_scan(acs, dts, dtc, 0.0, ALU.mult, ALU.add))

                conv_b, conv_w = V("conv_b"), V("conv_w")
                steps = [(c, w) for c in range(POOL_PAIRS, KT // 2) for w in range(CONV_W)]

                def convolve(n):
                    for c, w in steps[:n]:
                        for t in (2 * c, 2 * c + 1):
                            src, k = cpad[:, t, w:w + S], conv_w[:, t * CONV_W + w:t * CONV_W + w + 1]
                            if w == 0:
                                ins = v.tensor_scalar(conv[:, t, :], src, k, conv_b[:, t:t + 1], ALU.mult, ALU.add)
                            else:
                                dve.wait_ge(dve_step, at(dve_step, 0, less=1))
                                ins = v.scalar_tensor_tensor(conv[:, t, :], src, k, conv[:, t, :], ALU.mult, ALU.add)
                            ins.then_inc(dve_step, 1)
                            count.skip(dve_step, 1)
                    del steps[:n]

                for c in range(4):
                    g = product(2)
                    product(0)
                    dve.wait_ge(act_to_dve, at(act_to_dve))
                    v.tensor_tensor(cpad[:, 2 * c:2 * c + 2, CONV_W - 1:], sig, ps[:, g:g + 2, 0:S], ALU.mult)\
                        .then_inc(products_taken, 2)
                    settle()
                    mark().then_inc(dve_to_act, 1)
                    if c < POOL_PAIRS:
                        mark().then_inc(pair_gated, 1)
                    else:
                        convolve(12)
                for c in range(6):
                    g = product()
                    taken(v.tensor_copy(xpad[:, 2 * c:2 * c + 2, SSM_W - 1:], ps[:, g:g + 2, 0:S]))
                    convolve(8)
                settle()
                sb_, sw = V("ssm_conv_b"), V("ssm_conv_w")
                for c in range(4):
                    g = product()
                    dve.wait_ge(act_to_dve, at(act_to_dve))
                    taken(v.tensor_tensor(zed[:, 2 * c:2 * c + 2, :], sig, ps[:, g:g + 2, 0:S], ALU.mult))
                    settle()
                    if c < 3:
                        mark().then_inc(dve_to_act, 1)
                    w = c
                    assert SSM_W == 4
                    for t in range(12):
                        src, k = xpad[:, t, w:w + S], sw[:, t * SSM_W + w:t * SSM_W + w + 1]
                        if w == 0:
                            ins = v.tensor_scalar(xbc[:, t, :], src, k, sb_[:, t:t + 1], ALU.mult, ALU.add)
                        else:
                            dve.wait_ge(dve_step, at(dve_step, 0, less=11))
                            ins = v.scalar_tensor_tensor(xbc[:, t, :], src, k, xbc[:, t, :], ALU.mult, ALU.add)
                        ins.then_inc(dve_step, 1)
                        count.skip(dve_step, 1)
                dve.wait_ge(dve_step, at(dve_step, 0))
                mark().then_inc(dve_to_act, 1)
                convolve(len(steps))
                dve.wait_ge(dve_step, at(dve_step, 0))
                dve.wait_ge(pool_step, POOL_PAIRS * 2 * (2 * CONV_W - 1))
                mark().then_inc(residual_ready, KT // 2)
                dve.wait_ge(act_to_dve, at(act_to_dve))
                link(v.tensor_tensor(xbc[:, :, :], xbc[:, :, :], xsig, ALU.mult))
                normalize(conv, S, EPS2)
                dve.wait_ge(act_to_dve, at(act_to_dve))
                v.tensor_tensor(mixin[:, 0:KT, :], mixin[:, 0:KT, :], conv, ALU.mult)
                v.tensor_copy(sel, wide(ident[0:16, 0:16], [16, 16, P], 2))
                dve.wait_ge(pe_to_dve, at(pe_to_dve))
                v.tensor_copy(dtT, ps[:, 5, 0:32])
                link(v.tensor_scalar(acsT, ps[:, 5, 32:64], -1.0, None, ALU.mult))
                mark().then_inc(dve_to_pe, 1)
                dve.wait_ge(pe_to_dve, at(pe_to_dve))
                for b in range(TB):
                    v.tensor_tensor(xdt[:, b, :].rearrange("p (h n) -> p h n", n=HD),
                                    ps[:, 2 * b:2 * b + 2, :].rearrange("p a (h n) -> p (a h) n", n=HD),
                                    wide(dtT[:, b * 16:(b + 1) * 16], [P, 16, HD], 2), ALU.mult)
                dve.wait_ge(pe_to_dve, at(pe_to_dve))
                v.tensor_copy(cb[:, :, :], ps[:, 4:6, 0:384]).then_inc(dve_to_pe, 1)

                def gate_pair(t):
                    dve.wait_ge(head_done, at(head_done, 2))
                    y = mixin[:, KT + t, :]
                    v.scalar_tensor_tensor(y, xbc[:, t, :], V("d_skip")[:, t:t + 1], ps[:, 2 + t % 2, 0:S],
                                           ALU.mult, ALU.add).then_inc(y_tile_kept, 1)
                    settle()
                    return v.tensor_tensor(y, y, zed[:, t, :], ALU.mult)

                settle()
                for n in range(SSM_HEADS):
                    dve.wait_ge(decay_ready, at(decay_ready))
                    if n >= 2:
                        dve.wait_ge(head_done, n - 1)
                    v.tensor_tensor(mask[n % 2], decay[n % 2], cb[:, n // 8, :], ALU.mult).then_inc(dve_to_pe, 1)
                    if n >= 2 and n % 2 == 0:
                        gate_pair(n // 2 - 1)
                gate_pair(KT - 1).then_inc(dve_to_act, 1)
                dve.wait_ge(pe_to_dve, at(pe_to_dve))
                r2 = small[:, 0:512].rearrange("p (g n) -> p g n", g=2)
                v.tensor_scalar(r2, ps[:, 6:8, 0:S], 1.0 / 512, EPS2, ALU.mult, ALU.add).then_inc(variances_ready, 1)
                dve.wait_ge(inverses_ready, at(inverses_ready))
                for t in range(KT):
                    last = v.scalar_tensor_tensor(mixin[:, KT + t, :], mixin[:, KT + t, :],
                                                  V("ssm_norm_g")[:, t:t + 1], r2[:, t // 4, :], ALU.mult, ALU.mult)
                last.then_inc(dve_to_pe, 1)
                residual(2)
                normalize(t1, S, EPS2)

            def odd_mixer():
                dve.wait_ge(normed, at(normed))
                for q in (gq, gk):
                    for c in range(2):
                        g = product()
                        taken(v.tensor_copy(q[:, 2 * c:2 * c + 2, :], ps[:, g:g + 2, 0:S]))
                for c in range(4):
                    g = product()
                    taken(v.tensor_copy(gv[:, :, c * UC:(c + 1) * UC], ps[:, g:g + 2, 0:S]))
                for c in range(4):
                    g = product()
                    dve.wait_ge(act_to_dve, at(act_to_dve))
                    taken(v.tensor_tensor(gout[:, 2 * c:2 * c + 2, :], gmid[:, 0:2, :], ps[:, g:g + 2, 0:S], ALU.mult))
                    settle()
                    if c < 3:
                        mark().then_inc(dve_to_act, 1)
                dve.wait_ge(pe_to_dve, at(pe_to_dve))
                v.tensor_copy(low, ps[0:16, 0, 0:S]).then_inc(dve_to_pe, 1)
                dve.wait_ge(pe_to_dve, at(pe_to_dve))
                link(v.tensor_tensor(logg, ps[:, 2:4, :].rearrange("p a (b n) -> p (a b) n", n=S),
                                          wide(V("b_gate"), [P, 4, S], 2), ALU.add))
                link(v.tensor_scalar(en, logg, -1.0, None, ALU.mult))
                v.tensor_tensor(en, logg, en, ALU.max).then_inc(dve_to_act, 1)
                dve.wait_ge(act_to_dve, at(act_to_dve))
                link(v.scalar_tensor_tensor(logg, logg, 0.0, en, ALU.min, ALU.subtract))
                link(v.tensor_scalar(logg, logg, 1.0 / GLA_TAU, None, ALU.mult))
                for hd in range(4):
                    last = v.tensor_tensor_scan(eb[:, hd, :], C("carry"), logg[:, hd, :], 0.0, ALU.mult, ALU.add)
                link(last)
                for hd in range(4):
                    x = eb[:, hd, :].rearrange("p (c n) -> p c n", n=GLA_CHUNK)
                    last = v.tensor_tensor(gmid[:, hd, :].rearrange("p (c n) -> p c n", n=GLA_CHUNK),
                                           x[:, :, GLA_CHUNK - 1:].broadcast_to([P, 4, GLA_CHUNK]), x, ALU.subtract)
                last.then_inc(dve_to_act, 1)
                dve.wait_ge(act_to_dve, at(act_to_dve))
                v.scalar_tensor_tensor(qt, qt, float(P) ** -0.5, gq, ALU.mult, ALU.mult)
                v.tensor_tensor(ktl, ktl, gk, ALU.mult)
                v.tensor_tensor(kend, kend, gk, ALU.mult).then_inc(dve_to_pe, 1)
                link(v.memset(att, 0.0))
                dve.wait_ge(pe_to_dve, at(pe_to_dve))
                keep = wide(C("chunked").bitcast(U32), [P, 4, P])
                v.copy_predicated(att[:, 0:4, :], keep, ps[:, 4, :].rearrange("p (h n) -> p h n", n=P))
                v.copy_predicated(att[:, 4:8, :], keep, ps[:, 5, :].rearrange("p (h n) -> p h n", n=P))\
                    .then_inc(dve_to_pe, 1)
                for c in range(3):
                    for hd in range(4):
                        n = c * 4 + hd
                        dve.wait_ge(pe_to_dve, at(pe_to_dve))
                        kv, new = ps[:, 6 + n % 2, 0:S], hist[:, hd, c * S:(c + 1) * S]
                        if c == 0:
                            ins = v.tensor_copy(new, kv)
                        else:
                            ins = v.scalar_tensor_tensor(new, hist[:, hd, (c - 1) * S:c * S], gend[:, hd, c:c + 1], kv,
                                                         ALU.mult, ALU.add)
                        ins.then_inc(dve_to_pe, 1)
                        if hd == 3:
                            settle()
                dve.wait_ge(pe_to_dve, at(pe_to_dve))
                v.tensor_copy(go[:, :, :], ps[:, 0:4, :].rearrange("p a (b n) -> p (a b) n", n=S)).then_inc(dve_to_act, 1)
                dve.wait_ge(pe_to_dve, at(pe_to_dve))
                r4 = small[:, 0:1024].rearrange("p (h n) -> p h n", h=4)
                v.tensor_scalar(r4, ps[:, 4:6, :].rearrange("p a (b n) -> p (a b) n", n=S), 1.0 / S, EPS2,
                                ALU.mult, ALU.add).then_inc(variances_ready, 1)
                dve.wait_ge(inverses_ready, at(inverses_ready))
                for t in range(KT):
                    last = v.scalar_tensor_tensor(go[:, t, :], go[:, t, :], V("head_norm_g")[:, t % 2:t % 2 + 1],
                                                  r4[:, t // 2, :], ALU.mult, ALU.mult)
                link(last)
                v.tensor_tensor(go, go, gout, ALU.mult).then_inc(dve_to_pe, 1)
                residual()
                normalize(t1, S, EPS2)

            dve.wait_ge(normed, at(normed))
            even_mixer()
            for l in range(DEPTH):
                if l:
                    odd_mixer()
                memory_attention()
                mlp()


def kernel(**inputs):
    import concourse.bacc as bacc
    from concourse.bass_utils import run_bass_kernel_spmd

    i = {k: np.asarray(v) for k, v in inputs.items()}
    arrays = {
        "tokens": feature_major(np.concatenate([i["x"][0], i["ctx"][0]], 0)),
        "memory": feature_major(i["mem_2"][0]),
        "vectors": vectors(i),
        "constants": constants(),
        "neighbours": neighbour_rows(i["na_rpb"]),
        "units": weight_stream(i),
    }
    arrays = {k: np.ascontiguousarray(v) for k, v in arrays.items()}
    nc = bacc.Bacc("TRN2", target_bir_lowering=False, num_devices=1)
    ap = {k: nc.dram_tensor(k, v.shape, F32, kind="ExternalInput").ap() for k, v in arrays.items()}
    out = nc.dram_tensor("out", (P, KT, S), F32, kind="ExternalOutput").ap()
    build(nc, ap, out)
    got = run_bass_kernel_spmd(nc, [arrays], core_ids=[0]).results[0]["out"]
    return np.ascontiguousarray(np.asarray(got).transpose(2, 1, 0).reshape(1, S, D))
```
